# Optimizing a Trainium2 kernel written in Bass

```python
import math
import jax, jax.numpy as jnp
from jax import lax
import numpy as np

D_MODEL = 1024
BATCH = 1
SEQ = 2048
DEPTH = 1
DEC_BATCH = 8
DEC_SEQ = 4
PAST_LEN = 1024
PAGE_SIZE = 128

HEAD_DIM = 64
HEADS_PER_GROUP = 4
WINDOWS = (128, 512, 2048)
DILATIONS = (1, 4, 16)
N_HEADS = HEADS_PER_GROUP * len(WINDOWS)
ATTN_W = N_HEADS * HEAD_DIM
ATTN_OUT_W = HEADS_PER_GROUP * HEAD_DIM
BLOCK = 128
POOL_WINDOWS = (2, 4, 8, 16)
POOL_GROUPS = len(POOL_WINDOWS)
POOL_GW = 128
POOL_W = POOL_GROUPS * POOL_GW
POOL_STATE = max(POOL_WINDOWS) - 1
N_EXPERT_GROUPS = 4
EXPERTS_PER_GROUP = 8
N_EXPERTS = N_EXPERT_GROUPS * EXPERTS_PER_GROUP
TOP_K = 2
D_EXPERT = 512
MOE_BLOCK = 128
IN_W = 3 * ATTN_W + POOL_W + 2 * D_MODEL
NEG = -1e30
EPS = 1e-6

kernel_name = "hybrid_dilated_pool_hmoe_step"

def rmsnorm(x, g):
    xf = x.astype(jnp.float32)
    y = xf * lax.rsqrt(jnp.mean(xf * xf, axis=-1, keepdims=True) + EPS)
    return (y * g.astype(jnp.float32)).astype(x.dtype)

def project(x, ln1, w_in, q_gain, k_gain):
    B, T, _ = x.shape
    z = rmsnorm(x, ln1) @ w_in
    q, k, v, u, ga, gb = jnp.split(
        z, [ATTN_W, 2 * ATTN_W, 3 * ATTN_W, 3 * ATTN_W + POOL_W, 3 * ATTN_W + POOL_W + D_MODEL], axis=-1)
    q = rmsnorm(q.reshape(B, T, N_HEADS, HEAD_DIM), q_gain)
    k = rmsnorm(k.reshape(B, T, N_HEADS, HEAD_DIM), k_gain)
    v = v.reshape(B, T, N_HEADS, HEAD_DIM)
    return q, k, v, u, ga, gb

def dilated_band_attention(q, k, v, slopes, dil, steps):
    B, T, H, Dh = q.shape
    L = T // dil
    Bs = B * dil

    def to_sub(a):
        return a.reshape(B, L, dil, H, Dh).transpose(0, 2, 1, 3, 4).reshape(Bs, L, H, Dh)

    nb = -(-L // BLOCK)
    Lp = nb * BLOCK
    pad = ((0, 0), (0, Lp - L), (0, 0), (0, 0))
    qs = jnp.pad(to_sub(q), pad).reshape(Bs, nb, BLOCK, H, Dh)
    ks = jnp.pad(to_sub(k), pad).reshape(Bs, nb, BLOCK, H, Dh)
    vs = jnp.pad(to_sub(v), pad).reshape(Bs, nb, BLOCK, H, Dh)
    shift = ((0, 0), (1, 0), (0, 0), (0, 0), (0, 0))
    kband = jnp.concatenate([jnp.pad(ks, shift)[:, :nb], ks], axis=2)
    vband = jnp.concatenate([jnp.pad(vs, shift)[:, :nb], vs], axis=2)

    s = jnp.einsum('bnqhd,bnkhd->bnhqk', qs, kband,
                   preferred_element_type=jnp.float32) * (HEAD_DIM ** -0.5)
    qi = jnp.arange(BLOCK)[:, None]
    kb = jnp.arange(2 * BLOCK)[None, :]
    rel = qi + BLOCK - kb
    keypos = (jnp.arange(nb)[:, None, None] - 1) * BLOCK + kb[None]
    valid = (rel >= 0) & (rel <= steps) & (keypos >= 0)
    bias = -slopes.astype(jnp.float32)[:, None, None] * (dil * rel)[None].astype(jnp.float32)
    s = jnp.where(valid[None, :, None], s + bias[None, None], NEG)
    m = jnp.max(s, axis=-1, keepdims=True)
    p = jnp.exp(s - m)
    den = jnp.sum(p, axis=-1, keepdims=True)
    o = jnp.einsum('bnhqk,bnkhd->bnqhd', p / den, vband.astype(jnp.float32))
    lse = (m + jnp.log(den))[..., 0]

    o = o.reshape(Bs, Lp, H, Dh)[:, :L].reshape(B, dil, L, H, Dh).transpose(0, 2, 1, 3, 4).reshape(B, T, H, Dh)
    lse = lse.transpose(0, 1, 3, 2).reshape(Bs, Lp, H)[:, :L].reshape(B, dil, L, H).transpose(0, 2, 1, 3).reshape(B, T, H)
    return o, lse

def dilated_cached_attention(q, k_new, v_new, k_buf, v_buf, slopes, dil, steps, window):
    Bd, S, H, Dh = q.shape
    Lb = k_buf.shape[1]
    kc = jnp.concatenate([k_buf, k_new.astype(k_buf.dtype)], axis=1)
    vc = jnp.concatenate([v_buf, v_new.astype(v_buf.dtype)], axis=1)
    j = jnp.arange(steps + 1)
    idx = Lb + jnp.arange(S)[:, None] - dil * j[None, :]
    valid = idx >= 0
    idxc = jnp.maximum(idx, 0)
    kg = kc[:, idxc]
    vg = vc[:, idxc]
    s = jnp.einsum('bshd,bsjhd->bhsj', q, kg, preferred_element_type=jnp.float32) * (HEAD_DIM ** -0.5)
    bias = -slopes.astype(jnp.float32)[:, None, None] * (dil * j).astype(jnp.float32)[None, None, :]
    s = jnp.where(valid[None, None], s + bias[None], NEG)
    m = jnp.max(s, axis=-1, keepdims=True)
    p = jnp.exp(s - m)
    den = jnp.sum(p, axis=-1, keepdims=True)
    o = jnp.einsum('bhsj,bsjhd->bshd', p / den, vg.astype(jnp.float32))
    lse = (m + jnp.log(den))[..., 0].transpose(0, 2, 1)
    keep = min(window, Lb + S)
    return o, lse, kc[:, Lb + S - keep:], vc[:, Lb + S - keep:]

def combine_groups(outs, lses, dtype):
    a = jax.nn.softmax(jnp.stack(lses, axis=0), axis=0)
    o = jnp.sum(a[..., None] * jnp.stack(outs, axis=0), axis=0)
    B, T, H, Dh = o.shape
    return o.reshape(B, T, H * Dh).astype(dtype)

def pool_mix(u_ext, pos0, n_new, pool_lin, pool_scale):
    B, Lext, _ = u_ext.shape
    uf = u_ext.astype(jnp.float32).reshape(B, Lext, POOL_GROUPS, POOL_GW)
    cs0 = jnp.pad(jnp.cumsum(uf, axis=1), ((0, 0), (1, 0), (0, 0), (0, 0)))
    rows = jnp.arange(Lext - n_new, Lext)
    pos = pos0 + rows
    means = []
    for g, w in enumerate(POOL_WINDOWS):
        lo = jnp.maximum(rows + 1 - w, 0)
        wsum = cs0[:, rows + 1, g] - cs0[:, lo, g]
        cnt = jnp.minimum(pos + 1, w).astype(jnp.float32)
        means.append(wsum / cnt[None, :, None])
    z = jnp.stack(means, axis=2) - uf[:, Lext - n_new:]
    z = jnp.einsum('btgc,gcd->btgd', z, pool_lin.astype(jnp.float32)).reshape(B, n_new, POOL_W)
    return (z * pool_scale.astype(jnp.float32)).astype(u_ext.dtype)

def merge(x, attn_o, pool_o, ga, gb, w_pa, w_pb, w_o):
    m = jax.nn.sigmoid(ga) * (attn_o @ w_pa) + jax.nn.sigmoid(gb) * (pool_o @ w_pb)
    return x + m @ w_o

def hmoe(h, ln2, w_rg, b_rg, w_re, b_re, w_gate, w_up, w_down):
    B, T, D = h.shape
    N = B * T
    xn = rmsnorm(h, ln2).reshape(N, D)
    gl = (xn @ w_rg).astype(jnp.float32) + b_rg.astype(jnp.float32)
    gsel = jnp.argmax(gl, axis=-1).astype(jnp.int32)
    p_g = jnp.take_along_axis(jax.nn.softmax(gl, axis=-1), gsel[:, None], axis=1)
    el = ((xn @ w_re).astype(jnp.float32) + b_re.astype(jnp.float32)).reshape(N, N_EXPERT_GROUPS, EXPERTS_PER_GROUP)
    el = jnp.take_along_axis(el, gsel[:, None, None], axis=1)[:, 0]
    top_v, top_i = lax.top_k(el, TOP_K)
    wts = p_g * jax.nn.softmax(top_v, axis=-1)
    eid = gsel[:, None] * EXPERTS_PER_GROUP + top_i.astype(jnp.int32)

    A = N * TOP_K
    e = eid.reshape(A)
    tok = jnp.repeat(jnp.arange(N, dtype=jnp.int32), TOP_K)
    w = wts.reshape(A)
    order = jnp.argsort(e)
    e_s, tok_s, w_s = e[order], tok[order], w[order]
    counts = jnp.bincount(e, length=N_EXPERTS)
    padded = (counts + MOE_BLOCK - 1) // MOE_BLOCK * MOE_BLOCK
    starts = jnp.cumsum(counts) - counts
    pad_ends = jnp.cumsum(padded)
    pad_starts = pad_ends - padded
    dest = pad_starts[e_s] + jnp.arange(A, dtype=jnp.int32) - starts[e_s]
    n_blocks = (A + N_EXPERTS * (MOE_BLOCK - 1) + MOE_BLOCK - 1) // MOE_BLOCK
    R = n_blocks * MOE_BLOCK
    row_tok = jnp.full((R,), N, jnp.int32).at[dest].set(tok_s)
    row_w = jnp.zeros((R,), jnp.float32).at[dest].set(w_s)
    blk_e = jnp.minimum(jnp.searchsorted(pad_ends, jnp.arange(n_blocks) * MOE_BLOCK, side='right'), N_EXPERTS - 1)
    x_pad = jnp.concatenate([xn, jnp.zeros((1, D), xn.dtype)], axis=0)
    xb = x_pad[row_tok].reshape(n_blocks, MOE_BLOCK, D)

    def expert_block(args):
        xblk, ex = args
        hid = jax.nn.silu(xblk @ w_gate[ex]) * (xblk @ w_up[ex])
        return hid @ w_down[ex]

    yb = lax.map(expert_block, (xb, blk_e)).reshape(R, D)
    y = jnp.zeros((N + 1, D), jnp.float32).at[row_tok].add(yb.astype(jnp.float32) * row_w[:, None])[:N]
    return (h.astype(jnp.float32) + y.reshape(B, T, D)).astype(h.dtype)

def setup_inputs(seed: int = 0) -> dict:
    key = jax.random.key(seed)
    ks = iter(jax.random.split(key, 32))

    def nrm(shape, scale=1.0):
        return jax.random.normal(next(ks), shape, jnp.float32) * scale

    inp = {}
    inp['x_prompt'] = nrm((BATCH, SEQ, D_MODEL))
    inp['x_sample'] = nrm((DEC_BATCH, DEC_SEQ, D_MODEL))
    for w in WINDOWS:
        lb = min(w, PAST_LEN)
        inp['cache_k_w%d' % w] = nrm((DEC_BATCH, lb, HEADS_PER_GROUP, HEAD_DIM))
        inp['cache_v_w%d' % w] = nrm((DEC_BATCH, lb, HEADS_PER_GROUP, HEAD_DIM))
    inp['state_pool'] = nrm((DEC_BATCH, POOL_STATE, POOL_W))
    inp['ln1'] = 1.0 + nrm((D_MODEL,), 0.02)
    inp['w_in'] = nrm((D_MODEL, IN_W), D_MODEL ** -0.5)
    inp['q_gain'] = 1.0 + nrm((N_HEADS, HEAD_DIM), 0.02)
    inp['k_gain'] = 1.0 + nrm((N_HEADS, HEAD_DIM), 0.02)
    inp['pool_lin'] = nrm((POOL_GROUPS, POOL_GW, POOL_GW), POOL_GW ** -0.5)
    inp['pool_scale'] = 1.0 + nrm((POOL_W,), 0.02)
    inp['w_pa'] = nrm((ATTN_OUT_W, D_MODEL), ATTN_OUT_W ** -0.5)
    inp['w_pb'] = nrm((POOL_W, D_MODEL), POOL_W ** -0.5)
    inp['w_o'] = nrm((D_MODEL, D_MODEL), D_MODEL ** -0.5)
    inp['ln2'] = 1.0 + nrm((D_MODEL,), 0.02)
    inp['w_rg'] = nrm((D_MODEL, N_EXPERT_GROUPS), D_MODEL ** -0.5)
    inp['b_rg'] = nrm((N_EXPERT_GROUPS,), 0.01)
    inp['w_re'] = nrm((D_MODEL, N_EXPERTS), D_MODEL ** -0.5)
    inp['b_re'] = nrm((N_EXPERTS,), 0.01)
    inp['w_gate'] = nrm((N_EXPERTS, D_MODEL, D_EXPERT), D_MODEL ** -0.5)
    inp['w_up'] = nrm((N_EXPERTS, D_MODEL, D_EXPERT), D_MODEL ** -0.5)
    inp['w_down'] = nrm((N_EXPERTS, D_EXPERT, D_MODEL), D_EXPERT ** -0.5)
    return inp

def reference(x_prompt, x_sample, cache_k_w128, cache_v_w128, cache_k_w512, cache_v_w512,
              cache_k_w2048, cache_v_w2048, state_pool, ln1, w_in, q_gain, k_gain, pool_lin, pool_scale,
              w_pa, w_pb, w_o, ln2, w_rg, b_rg, w_re, b_re, w_gate, w_up, w_down):
    slopes = jnp.exp2(-8.0 * jnp.arange(1, N_HEADS + 1, dtype=jnp.float32) / N_HEADS)
    caches = ((cache_k_w128, cache_v_w128), (cache_k_w512, cache_v_w512), (cache_k_w2048, cache_v_w2048))

    for _layer in range(DEPTH):
        T = x_prompt.shape[1]
        q, k, v, u, ga, gb = project(x_prompt, ln1, w_in, q_gain, k_gain)
        outs, lses, pkv = [], [], []
        for g, (w, d) in enumerate(zip(WINDOWS, DILATIONS)):
            hs = slice(g * HEADS_PER_GROUP, (g + 1) * HEADS_PER_GROUP)
            o, l = dilated_band_attention(q[:, :, hs], k[:, :, hs], v[:, :, hs], slopes[hs], d, w // d)
            outs.append(o)
            lses.append(l)
            keep = min(w, T)
            pkv.append((k[:, T - keep:, hs], v[:, T - keep:, hs]))
        attn_o = combine_groups(outs, lses, x_prompt.dtype)
        pool_o = pool_mix(u, 0, T, pool_lin, pool_scale)
        h = merge(x_prompt, attn_o, pool_o, ga, gb, w_pa, w_pb, w_o)
        y_prompt = hmoe(h, ln2, w_rg, b_rg, w_re, b_re, w_gate, w_up, w_down)
        p_pool = u[:, T - POOL_STATE:]

    for _layer in range(DEPTH):
        S = x_sample.shape[1]
        q, k, v, u, ga, gb = project(x_sample, ln1, w_in, q_gain, k_gain)
        outs, lses, skv = [], [], []
        for g, (w, d) in enumerate(zip(WINDOWS, DILATIONS)):
            hs = slice(g * HEADS_PER_GROUP, (g + 1) * HEADS_PER_GROUP)
            o, l, nk, nv = dilated_cached_attention(q[:, :, hs], k[:, :, hs], v[:, :, hs],
                                                    caches[g][0], caches[g][1], slopes[hs], d, w // d, w)
            outs.append(o)
            lses.append(l)
            skv.append((nk, nv))
        attn_o = combine_groups(outs, lses, x_sample.dtype)
        u_ext = jnp.concatenate([state_pool, u.astype(state_pool.dtype)], axis=1)
        pool_o = pool_mix(u_ext, PAST_LEN - state_pool.shape[1], S, pool_lin, pool_scale).astype(x_sample.dtype)
        h = merge(x_sample, attn_o, pool_o, ga, gb, w_pa, w_pb, w_o)
        y_sample = hmoe(h, ln2, w_rg, b_rg, w_re, b_re, w_gate, w_up, w_down)
        s_pool = u_ext[:, u_ext.shape[1] - POOL_STATE:]

    (pk128, pv128), (pk512, pv512), (pk2048, pv2048) = pkv
    (sk128, sv128), (sk512, sv512), (sk2048, sv2048) = skv
    return (y_prompt, y_sample,
            pk128, pv128, pk512, pv512, pk2048, pv2048, p_pool,
            sk128, sv128, sk512, sv512, sk2048, sv2048, s_pool)


_drawn_inputs = setup_inputs


def setup_inputs(seed=0):
    import zlib

    import numpy as np

    out = dict(_drawn_inputs(seed))
    spreads = {}
    factors = {'q_gain': 6.253,
     'k_gain': 2.842,
     'pool_scale': 3.072,
     'b_rg': 17.379,
     'ln2': 3.197,
     'b_re': 8.0}
    for name, (base, spread) in spreads.items():
        noise = np.random.default_rng([zlib.crc32(name.encode()), seed]).standard_normal(out[name].shape)
        drawn = base * np.exp(spread * noise) if base else spread * noise
        out[name] = __import__('jax').numpy.asarray(drawn.astype(out[name].dtype))
    for name, factor in factors.items():
        out[name] = (out[name] * factor).astype(out[name].dtype)
    return out
```

```python
from contextlib import ExitStack

import concourse.bass as bass
from concourse import mybir

F32 = mybir.dt.float32
F32R = mybir.dt.float32r
I32 = mybir.dt.int32
U32 = mybir.dt.uint32
ACT = mybir.ActivationFunctionType
ALU = mybir.AluOpType
AX = mybir.AxisListType

P = 128
D = 1024
KC = D // P
SEQ, DEC_B, DEC_S = 2048, 8, 4
NS = DEC_B * DEC_S
TILES = SEQ // P + 1
ROWS = TILES * P
HD, HG = 64, 4
GW = HG * HD
NG = 3
AW = NG * GW
DIL = (1, 4, 16)
WIN = (128, 512, 2048)
PAST = 1024
LB = tuple(min(w, PAST) for w in WIN)
PW = 512
PG = 4
PSTATE = 15
NE, EG, EPG = 32, 4, 8
FE = 512
FC = FE // P
BLOCKS = (2 * (SEQ + NS) + NE * (P - 1)) // P
EPS = 1e-6
SLOT = 16
SEAT = (0, 2, 1, 3)
ATTW = HG * (HD + 2)


def by_twos(eng, n, body):
    body(0, 0, 0)
    body(1, 1, 0)
    if n > 3:
        with eng.Fori(1, n // 2) as j:
            body(j * 2, 0, j)
            body(j * 2 + 1, 1, j)
    if n % 2:
        body(n - 1, 0, n // 2)


def rows(t):
    return bass.ds(t * P, P)


def wait_apart(eng, sem, count, done):
    if not isinstance(count, int) or count > 0:
        eng.wait_ge(*done)
        eng.wait_ge(sem, count)


class Memory:

    def __init__(self, nc, ctx, stage):
        self.nc, self.ctx, self.stage, self.sems = nc, ctx, stage, []

    def sb(self, name, shape, dt=F32):
        return self.ctx.enter_context(self.nc.sbuf_tensor(f"{self.stage}_{name}", shape, dt))

    def ps(self, name, shape, dt=F32):
        return self.ctx.enter_context(self.nc.psum_tensor(f"{self.stage}_{name}", shape, dt))

    def sem(self, name):
        self.sems.append(self.ctx.enter_context(self.nc.semaphore(f"{self.stage}_{name}")))
        return self.sems[-1]

    def pool_sem(self, name):
        self.sems.append(self.nc.alloc_semaphore(f"{self.stage}_{name}"))
        return self.sems[-1]

    def block(self):
        for s in self.sems:
            self.nc.gpsimd.sem_clear(s)
        self.nc.all_engine_barrier()
        return self.ctx.enter_context(self.nc.Block())


def norm_and_turn(nc, x, ln1, ident_in, xT):
    with ExitStack() as ctx:
        m = Memory(nc, ctx, "norm")
        xin = m.sb("xin", [P, 2, D])
        junk = m.sb("junk", [P, D])
        xn = m.sb("xn", [P, 2, D])
        split = m.sb("split", [P, 2, 2, D], F32R)
        lnrow = m.sb("lnrow", [P, D])
        ident = m.sb("ident", [P, P])
        eps = m.sb("eps", [P, 1])
        ss = m.sb("ss", [P, 2])
        rms = m.sb("rms", [P, 2])
        rstd = m.sb("rstd", [P, 2])
        turned = m.ps("turned", [P, 2, 2, 512])

        consts_in = m.sem("consts_in")
        eps_set = m.sem("eps_set")
        x_in = [m.sem(f"x_in{s}") for s in range(2)]
        squared = m.sem("squared")
        rooted = m.sem("rooted")
        inverted = m.sem("inverted")
        normed = m.sem("normed")
        turns = m.sem("turns")
        hi_done = m.sem("hi_done")
        lo_done = m.sem("lo_done")
        stored = [m.pool_sem(f"stored{s}") for s in range(2)]
        block = m.block()

        @block.sync
        def _(sp):
            sp.dma_start(lnrow[:, :], ln1[None, :].partition_broadcast(P)).then_inc(consts_in, 16)
            sp.dma_start(ident[:, :], ident_in).then_inc(consts_in, 16)

            def load(t, s, k):
                if not (isinstance(t, int) and t < 2):
                    sp.wait_ge(normed, t - 1)
                sp.dma_start(xin[:, s, :], x[rows(t), :]).then_inc(x_in[s], 16)
            by_twos(sp, TILES, load)

        @block.gpsimd
        def _(pool):
            pool.memset(eps[:, :], EPS).then_inc(eps_set, 1)

            def store(t, s, k):
                pool.wait_ge(lo_done, t + 1)
                pool.dma_start(xT[t].rearrange("p a c n -> p a (c n)"), split[:, s, :, :].bitcast(F32)).then_inc(stored[s], 16)
            by_twos(pool, TILES, store)
            pool.wait_ge(stored[0], 16 * (TILES - TILES // 2))
            pool.wait_ge(stored[1], 16 * (TILES // 2))

        @block.scalar
        def _(act):
            act.wait_ge(eps_set, 1)

            def step(t, s, k):
                act.wait_ge(x_in[s], 16 * k + 16)
                act.activation(junk[:, :], xin[:, s, :], ACT.Square, accum_out=ss[:, s:s + 1]).then_inc(squared, 1)
                act.wait_ge(squared, t + 1)
                act.activation(rms[:, s:s + 1], ss[:, s:s + 1], ACT.Sqrt, bias=eps[:, 0:1],
                               scale=1.0 / D).then_inc(rooted, 1)
                act.wait_ge(turns, t + 1)
                if not (isinstance(t, int) and t < 2):
                    act.wait_ge(stored[s], 16 * k)
                act.activation(split[:, s, 0, :].rearrange("p (b n) -> p b n", b=2), turned[:, s, :, :],
                               ACT.Copy).then_inc(hi_done, 1)
            by_twos(act, TILES, step)

        @block.vector
        def _(dve):
            dve.wait_ge(consts_in, 32)

            def step(t, s, k):
                dve.wait_ge(rooted, t + 1)
                dve.reciprocal(rstd[:, s:s + 1], rms[:, s:s + 1]).then_inc(inverted, 1)
                dve.wait_ge(inverted, t + 1)
                if not (isinstance(t, int) and t < 2):
                    dve.wait_ge(turns, t - 1)
                dve.scalar_tensor_tensor(xn[:, s, :], xin[:, s, :], rstd[:, s:s + 1], lnrow[:, :],
                                         ALU.mult, ALU.mult).then_inc(normed, 1)
                dve.wait_ge(hi_done, t + 1)
                dve.tensor_tensor(split[:, s, 1, :].rearrange("p (b n) -> p b n", b=2), turned[:, s, :, :],
                                  split[:, s, 0, :].bitcast(F32).rearrange("p (b n) -> p b n", b=2),
                                  ALU.subtract).then_inc(lo_done, 1)
            by_twos(dve, TILES, step)

        @block.tensor
        def _(pe):
            pe.wait_ge(consts_in, 32)

            def step(t, s, k):
                pe.wait_ge(normed, t + 1)
                if not (isinstance(t, int) and t < 2):
                    pe.wait_ge(lo_done, t - 1)
                for c in range(KC):
                    last = pe.transpose(turned[:, s, c // 4, (c % 4) * P:(c % 4 + 1) * P],
                                        xn[:, s, c * P:(c + 1) * P], ident[:, :])
                last.then_inc(turns, 1)
            by_twos(pe, TILES, step)


def project(nc, xT, w_in, q_gain, k_gain, z):
    groups = [("q", 0, 384), ("k", AW, 384), ("v", 2 * AW, 384), ("u", 3 * AW, 256),
              ("ga", 3 * AW + PW, 512), ("gb", 3 * AW + PW + D, 512)]
    n_slot = (TILES - TILES // 2, TILES // 2)
    heads = AW // HD
    with ExitStack() as ctx:
        m = Memory(nc, ctx, "proj")
        w_raw = m.sb("w_raw", [P, KC, D])
        w_hi = [m.sb(f"w_hi{i}", [P, KC, D], F32R) for i in range(2)]
        w_lo = [m.sb(f"w_lo{i}", [P, KC, D], F32R) for i in range(2)]
        xs = m.sb("xs", [P, 2, 2, KC, P], F32R)
        out = m.sb("out", [P, 2, D])
        sq = m.sb("sq", [P, AW])
        gain = m.sb("gain", [P, 2, AW])
        eps = m.sb("eps", [P, 1])
        ss = m.sb("ss", [P, heads])
        rms = m.sb("rms", [P, heads])
        rstd = m.sb("rstd", [P, heads])
        acc = m.ps("acc", [P, 2, 2, 512])

        consts_in = m.sem("consts_in")
        eps_set = m.sem("eps_set")
        w_loaded = [m.pool_sem(f"w_loaded{c}") for c in range(KC)]
        w_hi_done = m.sem("w_hi_done")
        w_lo_done = m.sem("w_lo_done")
        x_loaded = [m.sem(f"x_loaded{s}") for s in range(2)]
        products = m.sem("products")
        squared = m.sem("squared")
        summed = m.sem("summed")
        rooted = m.sem("rooted")
        inverted = m.sem("inverted")
        scaled = m.sem("scaled")
        left_psum = m.sem("left_psum")
        ready = m.sem("ready")
        stored = [m.pool_sem(f"stored{s}") for s in range(2)]
        block = m.block()

        def width(g):
            return 2 * groups[g][2]

        @block.sync
        def _(sp):
            sp.dma_start(gain[:, 0, :], q_gain.rearrange("h d -> (h d)")[None, :].partition_broadcast(P)).then_inc(consts_in, 16)
            sp.dma_start(gain[:, 1, :], k_gain.rearrange("h d -> (h d)")[None, :].partition_broadcast(P)).then_inc(consts_in, 16)
            for g in range(len(groups)):
                def load(t, s, k, g=g):
                    before = g * TILES + t
                    if not (isinstance(t, int) and t < 2):
                        sp.wait_ge(products, before - 1)
                    elif g and t < 2:
                        sp.wait_ge(products, g * TILES)
                    sp.dma_start(xs[:, s, :, :, :].bitcast(F32), xT[t]).then_inc(x_loaded[s], 16)
                by_twos(sp, TILES, load)

        @block.gpsimd
        def _(pool):
            pool.memset(eps[:, :], EPS).then_inc(eps_set, 1)

            def load_w(g):
                _, col, nb = groups[g]
                for c in range(KC):
                    if g:
                        pool.wait_ge(w_lo_done, KC * (g - 1) + c + 1)
                    pool.dma_start(w_raw[:, c, 0:2 * nb], w_in[c * P:(c + 1) * P, col:col + 2 * nb]).then_inc(w_loaded[c], 16)

            load_w(0)
            for g in range(len(groups)):
                if g + 1 < len(groups):
                    load_w(g + 1)

                def store(t, s, k, g=g):
                    pool.wait_ge(ready, g * TILES + t + 1)
                    pool.dma_start(z[groups[g][0]][rows(t), :], out[:, s, 0:width(g)]).then_inc(stored[s], 16)
                by_twos(pool, TILES, store)
            for s in range(2):
                pool.wait_ge(stored[s], 16 * n_slot[s] * len(groups))

        def slot_free(eng, g, t, s, k):
            if not (isinstance(t, int) and t < 2 and g == 0):
                eng.wait_ge(stored[s], 16 * (g * n_slot[s] + k))

        @block.scalar
        def _(act):
            def split_w(g, c, wait):
                w = width(g)
                act.wait_ge(wait, 16 * (g + 1))
                act.activation(w_hi[g % 2][:, c, 0:w], w_raw[:, c, 0:w], ACT.Copy).then_inc(w_hi_done, 1)

            act.wait_ge(eps_set, 1)
            for c in range(KC):
                split_w(0, c, w_loaded[c])
            for g, (name, _, nb) in enumerate(groups):
                def tile(t, s, k, g=g, name=name, nb=nb):
                    n = g * TILES + t
                    act.wait_ge(products, n + 1)
                    if name in "qk":
                        act.activation(sq[:, :].rearrange("p (b n) -> p b n", b=2), acc[:, s, :, 0:nb],
                                       ACT.Square).then_inc(squared, 1)
                        act.wait_ge(summed, n + 1)
                        act.activation(rms[:, :], ss[:, :], ACT.Sqrt, bias=eps[:, 0:1], scale=1.0 / HD).then_inc(rooted, 1)
                    else:
                        slot_free(act, g, t, s, k)
                        act.activation(out[:, s, 0:2 * nb].rearrange("p (b n) -> p b n", b=2), acc[:, s, :, 0:nb],
                                       ACT.Sigmoid if name in ("ga", "gb") else ACT.Copy).then_inc(ready, 1)
                by_twos(act, TILES, tile)
                if g + 1 < len(groups):
                    for c in range(KC):
                        split_w(g + 1, c, w_loaded[c])

        @block.vector
        def _(dve):
            def split_w(g, c):
                w = width(g)
                dve.wait_ge(w_hi_done, KC * g + c + 1)
                dve.tensor_tensor(w_lo[g % 2][:, c, 0:w], w_raw[:, c, 0:w], w_hi[g % 2][:, c, 0:w].bitcast(F32),
                                  ALU.subtract).then_inc(w_lo_done, 1)

            dve.wait_ge(consts_in, 32)
            for c in range(KC):
                split_w(0, c)
            for g, (name, _, nb) in enumerate(groups):
                def tile(t, s, k, g=g, nb=nb):
                    n = g * TILES + t
                    dve.wait_ge(squared, n + 1)
                    dve.tensor_reduce(ss[:, :], sq[:, :].rearrange("p (h d) -> p h d", d=HD), AX.X, ALU.add).then_inc(summed, 1)
                    dve.wait_ge(rooted, n + 1)
                    dve.reciprocal(rstd[:, :], rms[:, :]).then_inc(inverted, 1)
                    dve.wait_ge(inverted, n + 1)
                    slot_free(dve, g, t, s, k)
                    for b in range(2):
                        r = rstd[:, b * 6:(b + 1) * 6][:, :, None].broadcast_to([P, 6, HD])
                        last = dve.tensor_tensor(out[:, s, b * nb:(b + 1) * nb].rearrange("p (h d) -> p h d", d=HD),
                                                 acc[:, s, b, 0:nb].rearrange("p (h d) -> p h d", d=HD), r, ALU.mult)
                    last.then_inc(scaled, 1)
                    dve.wait_ge(scaled, n + 1)
                    dve.tensor_tensor(out[:, s, 0:AW], out[:, s, 0:AW], gain[:, g, :], ALU.mult).then_inc(ready, 1)
                if name in "qk":
                    by_twos(dve, TILES, tile)
                if g + 1 < len(groups):
                    for c in range(KC):
                        split_w(g + 1, c)

        @block.tensor
        def _(pe):
            for g, (name, _, nb) in enumerate(groups):
                hi, lo = w_hi[g % 2], w_lo[g % 2]
                pe.wait_ge(w_lo_done, KC * (g + 1))

                def tile(t, s, k, g=g, nb=nb, hi=hi, lo=lo):
                    n = g * TILES + t
                    pe.wait_ge(x_loaded[s], 16 * (g * n_slot[s] + k) + 16)
                    if not (isinstance(t, int) and t < 2):
                        pe.wait_ge(ready, n - 1)
                    elif g:
                        pe.wait_ge(ready, g * TILES)
                    for c in range(KC):
                        for i, (xp, w) in enumerate(((0, hi), (0, lo), (1, hi))):
                            for b in range(2):
                                last = pe.matmul(acc[:, s, b, 0:nb], xs[:, s, xp, c, :], w[:, c, b * nb:(b + 1) * nb],
                                                 start=(c == 0 and i == 0), stop=(c == KC - 1 and i == 2))
                    last.then_inc(products, 1)
                by_twos(pe, TILES, tile)


def wait(eng, sem, count):
    if not isinstance(count, int) or count > 0:
        eng.wait_ge(sem, count)


def by_fours(eng, n, body, peel_last=False):
    for s in range(4):
        body(s, s, 0)
    with eng.Fori(1, n // 4 - peel_last) as j:
        for s in range(4):
            body(j * 4 + s, s, j)
    if peel_last:
        for s in range(4):
            body(n - 4 + s, s, n // 4 - 1)


def prompt_attention(nc, z, att, ident_in, bias_in):
    NB = SEQ // P
    steps = NB * NG
    with ExitStack() as ctx:
        m = Memory(nc, ctx, "attn")
        ident = m.sb("ident", [P, P])
        bias = m.sb("bias", [P, NG + 1, HG, 2 * P])
        bias1 = m.sb("bias1", [P, HG, 2 * P])
        q = m.sb("q", [P, 4, GW])
        k = m.sb("k", [P, 4, 2, GW])
        v = m.sb("v", [P, 4, 2, GW])
        qkT = m.sb("qkT", [P, 2, 6, P])
        sc = m.sb("sc", [P, 2, HG, 2 * P])
        pr = m.sb("pr", [P, 2, HG, 2 * P])
        prT = m.sb("prT", [P, 2, HG, 2, P])
        nmax = m.sb("nmax", [P, 4, HG])
        out = m.sb("out", [P, 4, HG, HD + 2])
        ps_turn = m.ps("turn", [P, 2, 512])
        ps_sc = m.ps("sc_ps", [P, HG, 2 * P])
        ps_prT = m.ps("prT_ps", [P, HG, 2, P])
        ps_o = m.ps("o_ps", [P, 2, 512])

        consts_in = m.sem("consts_in")
        qk_in = [m.sem(f"qk_in{s}") for s in range(4)]
        v_in = [m.sem(f"v_in{s}") for s in range(4)]
        qk_turned = m.sem("qk_turned")
        qk_copied = m.sem("qk_copied")
        scored = m.sem("scored")
        biased = m.sem("biased")
        maxed = m.sem("maxed")
        negated = m.sem("negated")
        exped = m.sem("exped")
        p_turned = m.sem("p_turned")
        p_copied_act = m.sem("p_copied_act")
        p_copied_dve = m.sem("p_copied_dve")
        weighted = m.sem("weighted")
        o_copied = m.sem("o_copied")
        stored = [m.pool_sem(f"stored{s}") for s in range(4)]
        block = m.block()

        def nk(g):
            return 1 if g == 2 else 2

        def view(name, g):
            a = z[name][:, g * GW:(g + 1) * GW]
            return a.rearrange("(l r) c -> r l c", r=DIL[g])

        def place(g, i):
            if DIL[g] == NB:
                return i, 0, 0
            if g == 0:
                return 0, i * P, (max(i - 1, 0) * P if isinstance(i, int) else (i - 1) * P)
            if isinstance(i, int):
                return i % DIL[g], i // DIL[g] * P, max(i // DIL[g] - 1, 0) * P
            return i[1], i[0] * P, (i[0] - 1) * P

        def all_blocks(eng, body):
            for g in range(NG):
                def one(t, s, j, g=g):
                    i = t if isinstance(t, int) or g != 1 else (j, s)
                    body(g, g * NB + t, s, g * (NB // 4) + j, i)
                by_fours(eng, NB, one, peel_last=(g == NG - 1))

        @block.sync
        def _(sp):
            sp.dma_start(ident[:, :], ident_in).then_inc(consts_in, 16)
            sp.dma_start(bias[:, :, :, :], bias_in[0:NG + 1].rearrange("g p h k -> p g h k")).then_inc(consts_in, 16)
            sp.dma_start(bias1[:, :, :], bias_in[NG + 1]).then_inc(consts_in, 16)

            def load(g, n, s, j, i):
                r, own, former = place(g, i)
                wait(sp, qk_turned, n - 3)
                wait_apart(sp, weighted, n - 3, (consts_in, 48))
                qv, kv, vv = view("q", g), view("k", g), view("v", g)
                sp.dma_start(q[:, s, :], qv[r, bass.ds(own, P), :]).then_inc(qk_in[s], 16)
                sp.dma_start(k[:, s, 1, :], kv[r, bass.ds(own, P), :]).then_inc(qk_in[s], 16)
                sp.dma_start(v[:, s, 1, :], vv[r, bass.ds(own, P), :]).then_inc(v_in[s], 16)
                sp.dma_start(k[:, s, 0, :], kv[r, bass.ds(former, P), :]).then_inc(qk_in[s], 16)
                sp.dma_start(v[:, s, 0, :], vv[r, bass.ds(former, P), :]).then_inc(v_in[s], 16)
            all_blocks(sp, load)

        @block.gpsimd
        def _(pool):
            def store(g, n, s, j, i):
                r, own, _ = place(g, i)
                wait_apart(pool, o_copied, n + 1, (consts_in, 48))
                dst = att[g].rearrange("(l r) c -> r l c", r=DIL[g])
                pool.dma_start(dst[r, bass.ds(own, P), :], out[:, s, :, :].rearrange("p h e -> p (h e)")).then_inc(stored[s], 16)
            all_blocks(pool, store)
            for s in range(4):
                pool.wait_ge(stored[s], 16 * steps // 4)

        @block.tensor
        def _(pe):
            def turn_qk(g, n, s, j):
                pe.wait_ge(qk_in[s], 48 * (j + 1))
                wait(pe, qk_copied, n)
                parts = [q[:, s, 0:P], q[:, s, P:GW]] + [k[:, s, b, c * P:(c + 1) * P] for b in range(2) for c in range(2)]
                for x, part in enumerate(parts):
                    last = pe.transpose(ps_turn[:, x // 3, (x % 3) * P:(x % 3 + 1) * P], part, ident[:, :])
                last.then_inc(qk_turned, 1)

            def scores(g, n, s):
                pe.wait_ge(qk_copied, n + 1)
                wait(pe, biased, n)
                for h in range(HG):
                    lo = HD * (h % 2)
                    for b in range(2 - nk(g), 2):
                        last = pe.matmul(ps_sc[:, SEAT[h], b * P:(b + 1) * P], qkT[lo:lo + HD, s % 2, h // 2, :],
                                         qkT[lo:lo + HD, s % 2, 2 + 2 * b + h // 2, :], start=True, stop=True)
                last.then_inc(scored, 1)

            def turn_p(g, n, s):
                pe.wait_ge(exped, HG * (n + 1))
                wait(pe, p_copied_act, n)
                wait(pe, p_copied_dve, n)
                for h in range(HG):
                    for b in range(2 - nk(g), 2):
                        last = pe.transpose(ps_prT[:, SEAT[h], b, :], pr[:, s % 2, SEAT[h], b * P:(b + 1) * P], ident[:, :])
                last.then_inc(p_turned, 1)

            def weigh_v(g, n, s, j):
                pe.wait_ge(v_in[s], 32 * (j + 1))
                pe.wait_ge(p_copied_act, n + 1)
                pe.wait_ge(p_copied_dve, n + 1)
                wait(pe, o_copied, n - 1)
                for h in range(HG):
                    for b in range(2 - nk(g), 2):
                        last = pe.matmul(ps_o[:, s % 2, h * HD:(h + 1) * HD], prT[:, s % 2, SEAT[h], b, :],
                                         v[:, s, b, h * HD:(h + 1) * HD], start=(b == 2 - nk(g)), stop=(b == 1))
                last.then_inc(weighted, 1)

            pe.wait_ge(consts_in, 48)
            turn_qk(0, 0, 0, 0)

            def step(g, n, s, j, i):
                first = isinstance(i, int) and i < 2
                gb = g - 1 if first else g
                sb_, jb = (s + 2) % 4, (j if s >= 2 else j - 1)
                if not (isinstance(n, int) and n < 2):
                    turn_p(gb, n - 2, sb_)
                scores(g, n, s)
                sn, jn = (s + 1) % 4, (j if s < 3 else j + 1)
                if not (isinstance(n, int) and n == steps - 1):
                    turn_qk(g, n + 1, sn, jn)
                if not (isinstance(n, int) and n < 2):
                    weigh_v(gb, n - 2, sb_, jb)

            all_blocks(pe, step)
            for n in (steps - 2, steps - 1):
                turn_p(NG - 1, n, n % 4)
                weigh_v(NG - 1, n, n % 4, n // 4)

        @block.vector
        def _(dve):
            def copy_p(g, n, s):
                b = 2 - nk(g)
                dve.wait_ge(p_turned, n + 1)
                wait(dve, weighted, n - 1)
                dve.tensor_copy(prT[:, s % 2, 2:4, b:2, :], ps_prT[:, 2:4, b:2, :]).then_inc(p_copied_dve, 1)

            def copy_o(n, s):
                dve.wait_ge(weighted, n + 1)
                dve.tensor_copy(out[:, s, :, 0:HD], ps_o[:, s % 2, 0:GW].rearrange("p (h d) -> p h d", d=HD)).then_inc(o_copied, 1)

            dve.wait_ge(consts_in, 48)

            def step(g, n, s, j, i):
                gb = g - 1 if isinstance(i, int) and i < 2 else g
                if not (isinstance(n, int) and n < 2):
                    copy_p(gb, n - 2, (s + 2) % 4)
                b = 2 - nk(g)
                table = bias[:, g, :, b * P:2 * P]
                if g == 0 and isinstance(i, int) and i == 0:
                    table = bias[:, NG, :, :]
                if g == 1 and isinstance(i, int) and i < DIL[1]:
                    table = bias1[:, :, :]
                dve.wait_ge(scored, n + 1)
                wait(dve, exped, HG * (n - 1))
                dve.scalar_tensor_tensor(sc[:, s % 2, :, b * P:2 * P], ps_sc[:, :, b * P:2 * P], HD ** -0.5,
                                         table, ALU.mult, ALU.add).then_inc(biased, 1)
                dve.wait_ge(biased, n + 1)
                wait(dve, stored[s], 16 * j)
                dve.tensor_reduce(out[:, s, :, HD].rearrange("p (i o) -> p o i", o=2),
                                  sc[:, s % 2, :, b * P:2 * P].rearrange("p (o i) k -> p o i k", o=2), AX.X, ALU.max).then_inc(maxed, 1)
                dve.wait_ge(maxed, n + 1)
                dve.tensor_scalar(nmax[:, s, :], out[:, s, :, HD], -1.0, None, ALU.mult).then_inc(negated, 1)
                if not (isinstance(n, int) and n < 2):
                    copy_o(n - 2, (s + 2) % 4)
            all_blocks(dve, step)
            for n in (steps - 2, steps - 1):
                copy_p(NG - 1, n, n % 4)
                copy_o(n, n % 4)

        @block.scalar
        def _(act):
            def copy_p(g, n, s):
                b = 2 - nk(g)
                act.wait_ge(p_turned, n + 1)
                wait(act, weighted, n - 1)
                act.activation(prT[:, s % 2, 0:2, b:2, :], ps_prT[:, 0:2, b:2, :], ACT.Copy).then_inc(p_copied_act, 1)

            def copy_qk(n, s):
                act.wait_ge(qk_turned, n + 1)
                wait(act, scored, n - 1)
                act.activation(qkT[:, s % 2, :, :].rearrange("p (a x) n -> p a (x n)", a=2), ps_turn[:, :, 0:3 * P],
                               ACT.Copy).then_inc(qk_copied, 1)

            copy_qk(0, 0)

            def step(g, n, s, j, i):
                gb = g - 1 if isinstance(i, int) and i < 2 else g
                if not (isinstance(n, int) and n < 2):
                    copy_p(gb, n - 2, (s + 2) % 4)
                if not (isinstance(n, int) and n == steps - 1):
                    copy_qk(n + 1, (s + 1) % 4)
                b = 2 - nk(g)
                act.wait_ge(negated, n + 1)
                for h in range(HG):
                    act.activation(pr[:, s % 2, SEAT[h], b * P:2 * P], sc[:, s % 2, SEAT[h], b * P:2 * P], ACT.Exp,
                                   bias=nmax[:, s, h:h + 1], accum_out=out[:, s, h, HD + 1:HD + 2]).then_inc(exped, 1)
            all_blocks(act, step)
            for n in (steps - 2, steps - 1):
                copy_p(NG - 1, n, n % 4)
def sample_attention(nc, z, att, caches_kv, joined, sbias_in):
    with ExitStack() as ctx:
        m = Memory(nc, ctx, "samp")
        q = m.sb("q", [P, 2, HD])
        kv = [m.sb(f"kv{i}", [P, 2, P + 1, HD]) for i in range(2)]
        prod = m.sb("prod", [P, (P + 1) * HD])
        sbias = m.sb("sbias", [P, NG, P + 1])
        sc = m.sb("sc", [P, P + 1])
        ex = m.sb("ex", [P, P + 1])
        nmax = m.sb("nmax", [P, 1])
        out = m.sb("out", [P, NG, HD + 2])
        consts_in = m.sem("consts_in")
        joined_sem = m.sem("joined")
        q_in = [m.sem(f"q_in{i}") for i in range(2)]
        k_in = [m.sem(f"k_in{i}") for i in range(2)]
        v_in = [m.sem(f"v_in{i}") for i in range(2)]
        steps = m.sem("steps")
        negated = m.sem("negated")
        exped = m.sem("exped")
        kv_read = m.sem("kv_read")
        done = m.sem("done")
        stored = m.sem("stored")
        block = m.block()

        def new_rows(name, g):
            return z[name][SEQ:SEQ + NS, g * GW:(g + 1) * GW].rearrange("r (h d) -> h r d", d=HD)

        @block.sync
        def _(sp):
            sp.dma_start(sbias[:, :, :], sbias_in).then_inc(consts_in, 16)
            for i, name in enumerate("kv"):
                sp.dma_start(joined[i][:, 0:P, :], caches_kv[0][i]).then_inc(joined_sem, 16)
                sp.dma_start(joined[i][:, P:P + DEC_S, :], z[name][SEQ:SEQ + NS, 0:GW].rearrange("(b s) c -> b s c", b=DEC_B)).then_inc(joined_sem, 16)
            sp.wait_ge(joined_sem, 64)
            for g in range(NG):
                n = LB[g] // DIL[g]
                if g >= 2:
                    sp.wait_ge(kv_read, g - 1)
                for h in range(HG):
                    sp.dma_start(q[h::HG, g % 2, :], new_rows("q", g)[h]).then_inc(q_in[g % 2], 16)
                for i, name in enumerate("kv"):
                    sem = (k_in, v_in)[i][g % 2]
                    for b in range(DEC_B):
                        src = joined[i][b] if g == 0 else caches_kv[g][i][b]
                        rows_ = n + 1 if g == 0 else n
                        win = bass.AP(src.tensor, src.offset, [[HD, DEC_S * HG], [DIL[g] * GW, rows_], [1, HD]])
                        sp.dma_start(kv[g % 2][b * 16:(b + 1) * 16, i, 0:rows_, :], win).then_inc(sem, 16)
                    if g > 0:
                        for h in range(HG):
                            sp.dma_start(kv[g % 2][h::HG, i, n, :], new_rows(name, g)[h]).then_inc(sem, 16)
            for g in range(NG):
                sp.wait_ge(done, g + 1)
                flat = att[g].rearrange("r (h e) -> (r h) e", e=HD + 2)
                for c in range(HG):
                    lo = SEQ * HG + c * P
                    sp.dma_start(flat[lo:lo + P, :], out[:, g, :]).then_inc(stored, 16)
            sp.wait_ge(stored, 16 * NG * HG)

        @block.vector
        def _(dve):
            dve.wait_ge(consts_in, 16)
            n_in = lambda g: 16 * (DEC_B + (HG if g else 0))
            seen_k = [0, 0]
            n_steps = 0
            for g in range(NG):
                n = LB[g] // DIL[g] + 1
                k, v = kv[g % 2][:, 0, 0:n, :], kv[g % 2][:, 1, 0:n, :]
                seen_k[g % 2] += n_in(g)
                pr = prod[:, 0:n * HD].rearrange("p (k d) -> p k d", d=HD)
                dve.wait_ge(q_in[g % 2], 16 * HG * (g // 2 + 1))
                dve.wait_ge(k_in[g % 2], seen_k[g % 2])
                dve.tensor_tensor(pr, k, q[:, g % 2, :][:, None, :].broadcast_to([P, n, HD]), ALU.mult).then_inc(steps, 1)
                n_steps += 1
                dve.wait_ge(steps, n_steps)
                dve.tensor_reduce(sc[:, 0:n], pr, AX.X, ALU.add).then_inc(steps, 1)
                n_steps += 1
                dve.wait_ge(steps, n_steps)
                dve.scalar_tensor_tensor(sc[:, 0:n], sc[:, 0:n], HD ** -0.5, sbias[:, g, 0:n], ALU.mult, ALU.add).then_inc(steps, 1)
                n_steps += 1
                dve.wait_ge(steps, n_steps)
                dve.tensor_reduce(out[:, g, HD:HD + 1], sc[:, 0:n], AX.X, ALU.max).then_inc(steps, 1)
                n_steps += 1
                dve.wait_ge(steps, n_steps)
                dve.tensor_scalar(nmax[:, :], out[:, g, HD:HD + 1], -1.0, None, ALU.mult).then_inc(negated, 1)
                dve.wait_ge(v_in[g % 2], seen_k[g % 2])
                dve.wait_ge(exped, g + 1)
                dve.tensor_tensor(pr, v, ex[:, 0:n, None].broadcast_to([P, n, HD]), ALU.mult).then_inc(kv_read, 1)
                dve.wait_ge(kv_read, g + 1)
                dve.tensor_reduce(out[:, g, 0:HD], pr.rearrange("p k d -> p d k"), AX.X, ALU.add).then_inc(done, 1)
                dve.wait_ge(done, g + 1)

        @block.scalar
        def _(act):
            for g in range(NG):
                n = LB[g] // DIL[g] + 1
                act.wait_ge(negated, g + 1)
                act.activation(ex[:, 0:n], sc[:, 0:n], ACT.Exp, bias=nmax[:, 0:1],
                               accum_out=out[:, g, HD + 1:HD + 2]).then_inc(exped, 1)


def pooling(nc, z, state, pool_lin, pool_scale, ident_in, inv_count_in, poolT):
    PAD = 16
    W = PAD + SEQ
    EXT = PSTATE + DEC_S
    with ExitStack() as ctx:
        m = Memory(nc, ctx, "mean")
        ident = m.sb("ident", [P, P])
        u = m.sb("u", [P, 2, PW])
        st = m.sb("st", [P, PW])
        uT = m.sb("uT", [P, PG, W])
        ext = m.sb("ext", [P, PG, DEC_B, EXT])
        sums = m.sb("sums", [P, 2, W])
        esums = m.sb("esums", [P, 2, DEC_B, EXT])
        zT = m.sb("zT", [P, PG, ROWS])
        head = m.sb("head", [P, PG, PAD])
        inv = m.sb("inv", [P, PG, PAD])
        lin = m.sb("lin", [P, PG, P])
        scale = m.sb("scale", [P, PG])
        res_hi = m.sb("res_hi", [P, PG, ROWS], F32R)
        res_lo = m.sb("res_lo", [P, 2, 512], F32R)
        ps_turn = m.ps("turn", [P, 2, PG, P])
        ps_lin = m.ps("lin_ps", [P, 2, 512])
        consts_in = m.sem("consts_in")
        state_in = m.sem("state_in")
        cleared = m.sem("cleared")
        u_in = [m.sem(f"u_in{s}") for s in range(2)]
        turned = m.sem("turned")
        copied = m.sem("copied")
        own = m.sem("own")
        mixed = m.sem("mixed")
        mapped = m.sem("mapped")
        hi_done = m.sem("hi_done")
        lo_done = m.sem("lo_done")
        stored = m.sem("stored")
        lo_stored = [m.pool_sem(f"lo_stored{s}") for s in range(2)]
        block = m.block()
        chunks = [(c, min(c + 512, ROWS)) for c in range(0, ROWS, 512)]
        jobs = [(g, a, b) for g in range(PG) for a, b in chunks]

        @block.sync
        def _(sp):
            sp.dma_start(ident[:, :], ident_in).then_inc(consts_in, 16)
            sp.dma_start(inv[:, :, :], inv_count_in).then_inc(consts_in, 16)
            sp.dma_start(lin[:, :, :], pool_lin.rearrange("g c d -> c g d")).then_inc(consts_in, 16)
            sp.dma_start(scale[:, :], pool_scale.rearrange("(g d) -> d g", d=P), allow_slow_non_contiguous=True).then_inc(consts_in, 16)
            sp.dma_start(st[0:DEC_B * PSTATE, :], state.rearrange("b t c -> (b t) c")).then_inc(state_in, 16)

            def load(t, s, k):
                wait(sp, turned, t - 1)
                sp.dma_start(u[:, s, :], z["u"][rows(t), :]).then_inc(u_in[s], 16)
            by_twos(sp, TILES, load)
            for g in range(PG):
                sp.wait_ge(hi_done, len(chunks) * (g + 1))
                sp.dma_start(poolT[:, :, 0, g, :].rearrange("t p n -> p t n"), res_hi[:, g, :].bitcast(F32).rearrange("p (t n) -> p t n", n=P)).then_inc(stored, 16)
            sp.wait_ge(stored, 16 * PG)

        @block.gpsimd
        def _(pool):
            pool.memset(uT[:, :, 0:PAD], 0.0)
            pool.memset(zT[:, :, SEQ:ROWS], 0.0).then_inc(cleared, 1)
            for n, (g, a, b) in enumerate(jobs):
                pool.wait_ge(lo_done, n + 1)
                pool.dma_start(poolT[a // P:b // P, :, 1, g, :].rearrange("t p n -> p t n"),
                               res_lo[:, n % 2, 0:b - a].bitcast(F32).rearrange("p (t n) -> p t n", n=P)).then_inc(lo_stored[n % 2], 16)
            for s in range(2):
                pool.wait_ge(lo_stored[s], 16 * len(jobs) // 2)

        @block.tensor
        def _(pe):
            pe.wait_ge(consts_in, 64)

            def turn(t, s, k):
                pe.wait_ge(u_in[s], 16 * k + 16)
                wait(pe, copied, t - 1)
                for g in range(PG):
                    last = pe.transpose(ps_turn[:, s, g, :], u[:, s, g * P:(g + 1) * P], ident[:, :])
                last.then_inc(turned, 1)
            by_twos(pe, TILES, turn)
            pe.wait_ge(state_in, 16)
            pe.wait_ge(copied, TILES)
            rows_ = DEC_B * PSTATE
            for g in range(PG):
                last = pe.transpose(ps_turn[:, 1, g, 0:rows_], st[0:rows_, g * P:(g + 1) * P], ident[0:rows_, 0:rows_])
            last.then_inc(turned, 1)
            for n, (g, a, b) in enumerate(jobs):
                pe.wait_ge(mixed, g + 1)
                wait(pe, lo_done, n - 1)
                pe.matmul(ps_lin[:, n % 2, 0:b - a], lin[:, g, :], zT[:, g, a:b], start=True, stop=True).then_inc(mapped, 1)

        @block.scalar
        def _(act):
            def copy(t, s, k):
                act.wait_ge(turned, t + 1)
                act.activation(uT[:, :, bass.ds(t * P + PAD, P)], ps_turn[:, s, :, :], ACT.Copy).then_inc(copied, 1)

            copy(0, 0, 0)
            with act.Fori(0, (SEQ // P - 2) // 2) as j:
                copy(j * 2 + 1, 1, j)
                copy(j * 2 + 2, 0, j)
            copy(SEQ // P - 1, 1, 0)
            act.wait_ge(turned, TILES)
            for g in range(PG):
                last = act.activation(ext[:, g, :, PSTATE:EXT], ps_turn[:, 0, g, 0:NS].rearrange("p (b s) -> p b s", b=DEC_B), ACT.Copy)
            last.then_inc(copied, 1)
            act.wait_ge(turned, TILES + 1)
            for g in range(PG):
                last = act.activation(ext[:, g, :, 0:PSTATE], ps_turn[:, 1, g, 0:DEC_B * PSTATE].rearrange("p (b t) -> p b t", b=DEC_B), ACT.Copy)
            last.then_inc(copied, 1)
            act.wait_ge(consts_in, 64)
            for n, (g, a, b) in enumerate(jobs):
                act.wait_ge(mapped, n + 1)
                act.activation(res_hi[:, g, a:b], ps_lin[:, n % 2, 0:b - a], ACT.Copy, scale=scale[:, g:g + 1]).then_inc(hi_done, 1)

        @block.vector
        def _(dve):
            n_own = 0

            def own_step(ins):
                nonlocal n_own
                n_own += 1
                ins.then_inc(own, 1)

            dve.wait_ge(consts_in, 64)
            dve.wait_ge(cleared, 1)
            dve.wait_ge(copied, TILES + 1)
            for g in range(PG):
                if g:
                    dve.wait_ge(own, n_own)
                src, esrc = uT[:, g, :], ext[:, g, :, :]
                for level in range(g + 1):
                    d = 1 << level
                    dst, edst = sums[:, level % 2, :], esums[:, level % 2, :, :]
                    lo = 2 * d - 1
                    own_step(dve.tensor_tensor(dst[:, lo:W], src[:, lo:W], src[:, lo - d:W - d], ALU.add))
                    own_step(dve.tensor_tensor(edst[:, :, lo:EXT], esrc[:, :, lo:EXT], esrc[:, :, lo - d:EXT - d], ALU.add))
                    dve.wait_ge(own, n_own)
                    src, esrc = dst, edst
                w = 2 << g
                own_step(dve.tensor_tensor(head[:, g, :], src[:, PAD:2 * PAD], inv[:, g, :], ALU.mult))
                own_step(dve.scalar_tensor_tensor(zT[:, g, 0:SEQ], src[:, PAD:W], 1.0 / w, uT[:, g, PAD:W], ALU.mult, ALU.subtract))
                own_step(dve.scalar_tensor_tensor(zT[:, g, SEQ:SEQ + NS].rearrange("p (b s) -> p b s", b=DEC_B), esrc[:, :, PSTATE:EXT], 1.0 / w,
                                                  ext[:, g, :, PSTATE:EXT], ALU.mult, ALU.subtract))
                dve.wait_ge(own, n_own)
                dve.tensor_tensor(zT[:, g, 0:PAD], head[:, g, :], uT[:, g, PAD:2 * PAD], ALU.subtract).then_inc(mixed, 1)
            for n, (g, a, b) in enumerate(jobs):
                dve.wait_ge(hi_done, n + 1)
                if n >= 2:
                    dve.wait_ge(lo_stored[n % 2], 16 * (n // 2))
                dve.scalar_tensor_tensor(res_lo[:, n % 2, 0:b - a], ps_lin[:, n % 2, 0:b - a], scale[:, g:g + 1],
                                         res_hi[:, g, a:b].bitcast(F32), ALU.mult, ALU.subtract).then_inc(lo_done, 1)
def merge_and_route(nc, x, z, att, poolT, w_pa, w_pb, w_o, ln2, w_rg, b_rg, w_re, b_re, ident_in, h_out, xn_out, logits_out):
    NL = EG + NE
    with ExitStack() as ctx:
        m = Memory(nc, ctx, "merge")
        KA, KP = GW // P, PW // P
        KW = KA + KP + KC
        w_raw = m.sb("w_raw", [P, 2, D])
        w_hi = m.sb("w_hi", [P, KW, D], F32R)
        w_lo = m.sb("w_lo", [P, KW, D], F32R)
        w_r = m.sb("w_r", [P, KC, NL])
        bias_r = m.sb("bias_r", [P, NL])
        lnrow = m.sb("lnrow", [P, D])
        ident = m.sb("ident", [P, P])
        eps = m.sb("eps", [P, 1])
        a_in = m.sb("a_in", [P, 2, NG, HG, HD + 2])
        p_in = m.sb("p_in", [P, 2, 2, PG, P], F32R)
        gates = m.sb("gates", [P, 2, D])
        xh = m.sb("xh", [P, 2, D])
        mx = m.sb("mx", [P, HG])
        wt = m.sb("wt", [P, NG, HG])
        den = m.sb("den", [P, HG])
        a_mix = m.sb("a_mix", [P, GW])
        aT = m.sb("aT", [P, 2, KA, P], F32R)
        mix = m.sb("mix", [P, D])
        mT = m.sb("mT", [P, 2, KC, P], F32R)
        xn = m.sb("xn", [P, D])
        junk = m.sb("junk", [P, D])
        xnT = m.sb("xnT", [P, KC, P])
        ss = m.sb("ss", [P, 1])
        rms = m.sb("rms", [P, 1])
        rstd = m.sb("rstd", [P, 1])
        logits = m.sb("logits", [P, 2, NL])
        ps_turn = m.ps("turn", [P, 2, 512])
        ps_a = m.ps("a_ps", [P, 2, 512])
        ps_p = m.ps("p_ps", [P, 2, 512])
        ps_o = m.ps("o_ps", [P, 2, 512])
        consts_in = m.sem("consts_in")
        eps_set = m.sem("eps_set")
        w_in_sem = [m.sem(f"w_in{i}") for i in range(2)]
        w_hi_done = m.sem("w_hi_done")
        w_lo_done = m.sem("w_lo_done")
        a_loaded = [m.sem(f"a_loaded{s}") for s in range(2)]
        g_loaded = m.sem("g_loaded")
        x_loaded = [m.sem(f"x_loaded{s}") for s in range(2)]
        p_loaded = [m.sem(f"p_loaded{s}") for s in range(2)]
        mx_done = m.sem("mx_done")
        lowered = m.sem("lowered")
        weights = m.sem("weights")
        own = m.sem("own")
        a_mixed = m.sem("a_mixed")
        a_turned = m.sem("a_turned")
        a_hi = m.sem("a_hi")
        a_split = m.sem("a_split")
        a_product = m.sem("a_product")
        p_product = m.sem("p_product")
        gated = m.sem("gated")
        mixed = m.sem("mixed")
        m_turned = m.sem("m_turned")
        m_hi = m.sem("m_hi")
        m_split = m.sem("m_split")
        o_product = m.sem("o_product")
        h_done = m.sem("h_done")
        squared = m.sem("squared")
        rooted = m.sem("rooted")
        inverted = m.sem("inverted")
        normed = m.sem("normed")
        n_turned = m.sem("n_turned")
        n_copied = m.sem("n_copied")
        l_product = m.sem("l_product")
        l_done = m.sem("l_done")
        h_stored = [m.pool_sem(f"h_stored{s}") for s in range(2)]
        n_stored = m.pool_sem("n_stored")
        l_stored = m.pool_sem("l_stored")
        block = m.block()
        w_rows = [(w_pa, c) for c in range(KA)] + [(w_pb, c) for c in range(KP)] + [(w_o, c) for c in range(KC)]

        @block.sync
        def _(sp):
            for dst, src in ((ident[:, :], ident_in), (lnrow[:, :], ln2[None, :].partition_broadcast(P)),
                             (bias_r[:, 0:EG], b_rg[None, :].partition_broadcast(P)),
                             (bias_r[:, EG:NL], b_re[None, :].partition_broadcast(P)),
                             (w_r[:, :, 0:EG], w_rg.rearrange("(c p) n -> p c n", p=P)),
                             (w_r[:, :, EG:NL], w_re.rearrange("(c p) n -> p c n", p=P))):
                sp.dma_start(dst, src).then_inc(consts_in, 16)
            for i, (w, c) in enumerate(w_rows):
                wait(sp, w_lo_done, i - 1)
                sp.dma_start(w_raw[:, i % 2, :], w[c * P:(c + 1) * P, :]).then_inc(w_in_sem[i % 2], 16)

            def load(t, s, k):
                wait_apart(sp, a_mixed, t - 1, (consts_in, 96))
                sp.dma_start(a_in[:, s].rearrange("p g h e -> p g (h e)"), att[:, rows(t), :].rearrange("g p e -> p g e")).then_inc(a_loaded[s], 16)
                wait_apart(sp, p_product, t - 1, (consts_in, 96))
                sp.dma_start(p_in[:, s].bitcast(F32), poolT[t]).then_inc(p_loaded[s], 16)
                wait_apart(sp, normed, t - 1, (consts_in, 96))
                if not (isinstance(t, int) and t < 2):
                    wait_apart(sp, h_stored[s], 16 * k, (consts_in, 96))
                sp.dma_start(xh[:, s, :], x[rows(t), :]).then_inc(x_loaded[s], 16)
                wait_apart(sp, mixed, t, (consts_in, 96))
                sp.dma_start(gates[:, 0, :], z["ga"][rows(t), :]).then_inc(g_loaded, 16)
                sp.dma_start(gates[:, 1, :], z["gb"][rows(t), :]).then_inc(g_loaded, 16)
            by_twos(sp, TILES, load)

        @block.gpsimd
        def _(pool):
            pool.memset(eps[:, :], EPS).then_inc(eps_set, 1)

            def store(t, s, k):
                wait_apart(pool, h_done, t + 1, (eps_set, 1))
                pool.dma_start(h_out[rows(t), :], xh[:, s, :]).then_inc(h_stored[s], 16)
                wait_apart(pool, normed, t + 1, (eps_set, 1))
                pool.dma_start(xn_out[rows(t), :], xn[:, :]).then_inc(n_stored, 16)
                wait_apart(pool, l_done, t + 1, (eps_set, 1))
                pool.dma_start(logits_out[rows(t), :], logits[:, s, :]).then_inc(l_stored, 16)
            by_twos(pool, TILES, store)
            pool.wait_ge(n_stored, 16 * TILES)
            pool.wait_ge(l_stored, 16 * TILES)
            for s in range(2):
                pool.wait_ge(h_stored[s], 16 * ((TILES + 1 - s) // 2))

        @block.tensor
        def _(pe):
            def product(ps, lhs, c0, n):
                for c in range(n):
                    for i, (part, w) in enumerate(((0, w_hi), (0, w_lo), (1, w_hi))):
                        for b in range(2):
                            last = pe.matmul(ps[:, b, :], lhs(part, c), w[:, c0 + c, b * 512:(b + 1) * 512],
                                             start=(c == 0 and i == 0), stop=(c == n - 1 and i == 2))
                return last

            def turn_a(t):
                pe.wait_ge(a_mixed, t + 1)
                wait(pe, n_copied, t - 1)
                wait(pe, l_done, t - 1)
                for c in range(KA):
                    last = pe.transpose(ps_turn[:, 0, c * P:(c + 1) * P], a_mix[:, c * P:(c + 1) * P], ident[:, :])
                last.then_inc(a_turned, 1)

            def route(t):
                pe.wait_ge(normed, t + 1)
                pe.wait_ge(a_split, t + 1)
                for c in range(KC):
                    last = pe.transpose(ps_turn[:, c // 4, (c % 4) * P:(c % 4 + 1) * P], xn[:, c * P:(c + 1) * P], ident[:, :])
                last.then_inc(n_turned, 1)
                pe.wait_ge(n_copied, t + 1)
                for c in range(KC):
                    last = pe.matmul(ps_turn[:, 0, 0:NL], xnT[:, c, :], w_r[:, c, :], start=(c == 0), stop=(c == KC - 1))
                last.then_inc(l_product, 1)

            pe.wait_ge(consts_in, 96)
            pe.wait_ge(w_lo_done, KW)

            def step(t, s, k):
                turn_a(t)
                pe.wait_ge(p_loaded[s], 16 * k + 16)
                wait(pe, mixed, t)
                product(ps_p, lambda i, c: p_in[:, s, i, c, :], KA, KP).then_inc(p_product, 1)
                pe.wait_ge(a_split, t + 1)
                product(ps_a, lambda i, c: aT[:, i, c, :], 0, KA).then_inc(a_product, 1)
                if not (isinstance(t, int) and t == 0):
                    route(t - 1)
                    pe.wait_ge(l_done, t)
                pe.wait_ge(mixed, t + 1)
                for c in range(KC):
                    last = pe.transpose(ps_turn[:, c // 4, (c % 4) * P:(c % 4 + 1) * P], mix[:, c * P:(c + 1) * P], ident[:, :])
                last.then_inc(m_turned, 1)
                pe.wait_ge(m_split, t + 1)
                wait(pe, h_done, t)
                product(ps_o, lambda i, c: mT[:, i, c, :], KA + KP, KC).then_inc(o_product, 1)
            by_twos(pe, TILES, step)
            route(TILES - 1)

        @block.scalar
        def _(act):
            act.wait_ge(eps_set, 1)
            for i in range(KW):
                act.wait_ge(w_in_sem[i % 2], 16 * (i // 2 + 1))
                act.activation(w_hi[:, i, :], w_raw[:, i % 2, :], ACT.Copy).then_inc(w_hi_done, 1)

            def norm(t, s):
                act.wait_ge(h_done, t + 1)
                act.activation(junk[:, :], xh[:, s, :], ACT.Square, accum_out=ss[:, :]).then_inc(squared, 1)
                act.wait_ge(squared, t + 1)
                act.activation(rms[:, :], ss[:, :], ACT.Sqrt, bias=eps[:, 0:1], scale=1.0 / D).then_inc(rooted, 1)

            def copy_xn(t):
                act.wait_ge(n_turned, t + 1)
                act.activation(xnT[:, :, :].rearrange("p (b c) n -> p b (c n)", b=2), ps_turn[:, :, :], ACT.Copy).then_inc(n_copied, 1)

            def weigh(t):
                act.wait_ge(lowered, t + 1)
                act.activation(wt[:, :, :], wt[:, :, :], ACT.Exp).then_inc(weights, 1)

            weigh(0)

            def step(t, s, k):
                act.wait_ge(a_turned, t + 1)
                act.activation(aT[:, 0, :, :].rearrange("p c n -> p (c n)"), ps_turn[:, 0, 0:GW], ACT.Copy).then_inc(a_hi, 1)
                if not (isinstance(t, int) and t == 0):
                    copy_xn(t - 1)
                act.wait_ge(m_turned, t + 1)
                act.activation(mT[:, 0, :, :].rearrange("p (b c) n -> p b (c n)", b=2), ps_turn[:, :, :], ACT.Copy).then_inc(m_hi, 1)
                if not (isinstance(t, int) and t == TILES - 1):
                    weigh(t + 1)
                norm(t, s)
            by_twos(act, TILES, step)
            copy_xn(TILES - 1)

        @block.vector
        def _(dve):
            dve.wait_ge(consts_in, 96)
            for i in range(KW):
                dve.wait_ge(w_hi_done, i + 1)
                dve.tensor_tensor(w_lo[:, i, :], w_raw[:, i % 2, :], w_hi[:, i, :].bitcast(F32), ALU.subtract).then_inc(w_lo_done, 1)

            def combine(t, s, k):
                a = a_in[:, s]
                dve.wait_ge(a_loaded[s], 16 * k + 16)
                dve.tensor_reduce(mx[:, :], a[:, :, :, HD].rearrange("p g h -> p h g"), AX.X, ALU.max).then_inc(mx_done, 1)
                dve.wait_ge(mx_done, t + 1)
                wait(dve, own, 5 * t)
                dve.tensor_tensor(wt[:, :, :], a[:, :, :, HD], mx[:, None, :].broadcast_to([P, NG, HG]), ALU.subtract).then_inc(lowered, 1)
                dve.wait_ge(weights, t + 1)
                dve.tensor_tensor(a[:, :, :, HD + 1], a[:, :, :, HD + 1], wt[:, :, :], ALU.mult).then_inc(own, 1)
                dve.wait_ge(own, 5 * t + 1)
                dve.tensor_reduce(den[:, :], a[:, :, :, HD + 1].rearrange("p g h -> p h g"), AX.X, ALU.add).then_inc(own, 1)
                dve.wait_ge(own, 5 * t + 2)
                dve.reciprocal(den[:, :], den[:, :]).then_inc(own, 1)
                dve.wait_ge(own, 5 * t + 3)
                dve.tensor_tensor(wt[:, :, :], wt[:, :, :], den[:, None, :].broadcast_to([P, NG, HG]), ALU.mult).then_inc(own, 1)
                dve.wait_ge(own, 5 * t + 4)
                for g in range(NG):
                    last = dve.tensor_tensor(a[:, g, :, 0:HD], a[:, g, :, 0:HD], wt[:, g, :, None].broadcast_to([P, HG, HD]), ALU.mult)
                last.then_inc(own, 1)
                dve.wait_ge(own, 5 * t + 5)
                wait(dve, a_turned, t)
                dve.tensor_reduce(a_mix[:, :].rearrange("p (h d) -> p h d", d=HD), a[:, :, :, 0:HD].rearrange("p g h d -> p h d g"),
                                  AX.X, ALU.add).then_inc(a_mixed, 1)

            def split_a(t):
                dve.wait_ge(a_hi, t + 1)
                dve.tensor_tensor(aT[:, 1, :, :].rearrange("p c n -> p (c n)"), ps_turn[:, 0, 0:GW],
                                  aT[:, 0, :, :].bitcast(F32).rearrange("p c n -> p (c n)"), ALU.subtract).then_inc(a_split, 1)

            def halves(ap):
                return ap.rearrange("p (b n) -> p b n", b=2)

            combine(0, 0, 0)

            def step(t, s, k):
                split_a(t)
                dve.wait_ge(g_loaded, 32 * (t + 1))
                dve.wait_ge(p_product, t + 1)
                dve.tensor_tensor(halves(gates[:, 1, :]), halves(gates[:, 1, :]), ps_p[:, :, :], ALU.mult).then_inc(gated, 1)
                dve.wait_ge(a_product, t + 1)
                dve.tensor_tensor(halves(gates[:, 0, :]), halves(gates[:, 0, :]), ps_a[:, :, :], ALU.mult).then_inc(gated, 1)
                dve.wait_ge(gated, 2 * (t + 1))
                wait(dve, m_turned, t)
                dve.tensor_tensor(mix[:, :], gates[:, 0, :], gates[:, 1, :], ALU.add).then_inc(mixed, 1)
                if not (isinstance(t, int) and t == 0):
                    dve.wait_ge(l_product, t)
                    wait(dve, l_stored, 16 * (t - 1))
                    dve.tensor_tensor(logits[:, 1 - s, :], ps_turn[:, 0, 0:NL], bias_r[:, :], ALU.add).then_inc(l_done, 1)
                dve.wait_ge(m_hi, t + 1)
                dve.tensor_tensor(mT[:, 1, :, :].rearrange("p (b c) n -> p b (c n)", b=2), ps_turn[:, :, :],
                                  mT[:, 0, :, :].bitcast(F32).rearrange("p (b c) n -> p b (c n)", b=2), ALU.subtract).then_inc(m_split, 1)
                if not (isinstance(t, int) and t == TILES - 1):
                    combine(t + 1, 1 - s, k + 1 if s else k)
                dve.wait_ge(o_product, t + 1)
                dve.wait_ge(x_loaded[s], 16 * k + 16)
                dve.tensor_tensor(halves(xh[:, s, :]), halves(xh[:, s, :]), ps_o[:, :, :], ALU.add).then_inc(h_done, 1)
                dve.wait_ge(rooted, t + 1)
                dve.reciprocal(rstd[:, :], rms[:, :]).then_inc(inverted, 1)
                dve.wait_ge(inverted, t + 1)
                wait(dve, n_turned, t)
                if not (isinstance(t, int) and t == 0):
                    dve.wait_ge(n_stored, 16 * t)
                dve.scalar_tensor_tensor(xn[:, :], xh[:, s, :], rstd[:, 0:1], lnrow[:, :], ALU.mult, ALU.mult).then_inc(normed, 1)
            by_twos(dve, TILES, step)
            last = TILES - 1
            dve.wait_ge(l_product, TILES)
            dve.wait_ge(l_stored, 16 * (TILES - 1))
            dve.tensor_tensor(logits[:, last % 2, :], ps_turn[:, 0, 0:NL], bias_r[:, :], ALU.add).then_inc(l_done, 1)


def routing(nc, logits_in, a, slots, dest_out, weight_out, blocks_out):
    PADT, PADE = 16, 16
    with ExitStack() as ctx:
        m = Memory(nc, ctx, "route")
        lg = m.sb("lg", [P, TILES, EG + NE])
        ones = m.sb("ones", [P, P])
        before = m.sb("before", [P, P])
        real = m.sb("real", [P, TILES])
        first_g = m.sb("first_g", [P, EG])
        first_e = m.sb("first_e", [P, NE])
        block_no = m.sb("block_no", [P, BLOCKS, NE])
        token = m.sb("token", [P, TILES, SLOT], I32)
        zero = m.sb("zero", [P, (BLOCKS + 1) * SLOT], I32)
        g4 = [m.sb(f"g4_{i}", [P, TILES, EG]) for i in range(3)]
        t1 = [m.sb(f"t1_{i}", [P, TILES]) for i in range(8)]
        el = m.sb("el", [P, TILES, NE])
        e1 = m.sb("e1", [P, TILES, NE])
        e2 = m.sb("e2", [P, TILES, NE])
        tmp = m.sb("tmp", [P, TILES, NE])
        counts = m.sb("counts", [P, 2, PADT + TILES, NE])
        tile_count = m.sb("tile_count", [P, TILES, NE])
        ends = m.sb("ends", [P, 2, PADE + NE])
        nblk = m.sb("nblk", [P, NE])
        nblk_i = m.sb("nblk_i", [P, NE], I32)
        start = m.sb("start", [P, NE])
        where = m.sb("where", [P, TILES, NE])
        dest_f = m.sb("dest_f", [P, TILES, 2])
        dest = m.sb("dest", [P, 2, TILES], I32)
        weight = m.sb("weight", [P, TILES, 2])
        owner = m.sb("owner", [P, BLOCKS])
        owner_i = m.sb("owner_i", [P, BLOCKS], I32)
        NT = TILES * NE
        HALF = (TILES + 1) // 2
        ps_sum = m.ps("sum_ps", [P, 2, 512])
        ps_rank = m.ps("rank_ps", [P, 2, 512])
        loaded = m.sem("loaded")
        cleared = m.sem("cleared")
        own = m.sem("own")
        lowered = m.sem("lowered")
        exped = m.sem("exped")
        chosen = m.sem("chosen")
        counted = m.sem("counted")
        placed = m.sem("placed")
        zeroed = m.pool_sem("zeroed")
        scattered = m.pool_sem("scattered")
        stored = m.sem("stored")
        block = m.block()

        @block.sync
        def _(sp):
            for dst, src in ((lg[:, :, :], logits_in.rearrange("(t p) n -> p t n", p=P)), (ones[:, :], a["ones"]),
                             (before[:, :], a["before"]), (real[:, :], a["real"]), (first_g[:, :], a["first_group"]),
                             (first_e[:, :], a["first_expert"]), (block_no[:, :, :], a["block_no"]), (token[:, :, :], a["token"])):
                sp.dma_start(dst, src).then_inc(loaded, 16)
            sp.wait_ge(placed, 1)
            sp.dma_start(dest_out.rearrange("k (t p) -> p k t", p=P), dest[:, :, :], allow_slow_non_contiguous=True).then_inc(stored, 16)
            sp.dma_start(weight_out.rearrange("(t p) k -> p t k", p=P), weight[:, :, :], allow_slow_non_contiguous=True).then_inc(stored, 16)
            sp.dma_start(blocks_out, owner_i[0:1, :]).then_inc(stored, 16)
            sp.wait_ge(stored, 48)

        @block.gpsimd
        def _(pool):
            pool.memset(zero[:, :], 0).then_inc(cleared, 1)
            pool.memset(counts[:, :, 0:PADT, :], 0.0)
            pool.memset(ends[:, :, 0:PADE], 0.0).then_inc(cleared, 1)
            pool.wait_ge(cleared, 2)
            pool.dma_start(slots.rearrange("(p b) e -> p (b e)", p=P), zero[:, :]).then_inc(zeroed, 16)
            pool.wait_ge(zeroed, 16)
            pool.wait_ge(placed, 1)
            pool.wait_ge(loaded, 128)
            for t in range(TILES):
                n = P if t < TILES - 1 else NS
                for k in range(2):
                    pool.indirect_dma_start(out=slots, out_offset=bass.IndirectOffsetOnAxis(ap=dest[0:n, k, t:t + 1], axis=0),
                                            in_=token[0:n, t, :], in_offset=None).then_inc(scattered, 16)
            pool.wait_ge(scattered, 16 * 2 * TILES)

        @block.scalar
        def _(act):
            act.wait_ge(lowered, 1)
            act.activation(g4[1][:, :, :], g4[1][:, :, :], ACT.Exp).then_inc(exped, 1)
            act.wait_ge(lowered, 2)
            act.activation(t1[5][:, :], t1[5][:, :], ACT.Exp).then_inc(exped, 1)

        @block.tensor
        def _(pe):
            pe.wait_ge(loaded, 128)
            pe.wait_ge(chosen, 1)
            for i, (a0, b0) in enumerate(((0, HALF), (HALF, TILES))):
                flat = tmp[:, a0:b0, :].rearrange("p t e -> p (t e)")
                w = (b0 - a0) * NE
                pe.matmul(ps_sum[:, i, 0:w], ones[:, :], flat, start=True, stop=True)
                last = pe.matmul(ps_rank[:, i, 0:w], before[:, :], flat, start=True, stop=True)
            last.then_inc(counted, 1)

        @block.vector
        def _(dve):
            n_own = 0

            def then(ins):
                nonlocal n_own
                n_own += 1
                ins.then_inc(own, 1)
                dve.wait_ge(own, n_own)

            def over(ap, n):
                return ap[:, :, None].broadcast_to([P, TILES, n])

            def table(ap, n):
                return ap[:, None, :].broadcast_to([P, TILES, n])

            def pick_first(out, values, best, order, n, scratch):
                then(dve.tensor_tensor(out, values, over(best, n), ALU.is_equal))
                then(dve.tensor_tensor(out, out, table(order, n), ALU.mult))
                then(dve.tensor_reduce(scratch, out, AX.X, ALU.max))
                then(dve.tensor_tensor(out, out, over(scratch, n), ALU.is_equal))

            dve.wait_ge(loaded, 128)
            dve.wait_ge(cleared, 2)
            gl = lg[:, :, 0:EG]
            then(dve.tensor_reduce(t1[0][:, :], gl, AX.X, ALU.max))
            dve.tensor_tensor(g4[1][:, :, :], gl, over(t1[0][:, :], EG), ALU.subtract).then_inc(lowered, 1)
            pick_first(g4[0][:, :, :], gl, t1[0][:, :], first_g[:, :], EG, t1[1][:, :])
            then(dve.tensor_scalar(g4[2][:, :, :], g4[0][:, :, :], 1.0, 1e30, ALU.subtract, ALU.mult))
            for g in range(EG):
                here = slice(g * EPG, (g + 1) * EPG)
                then(dve.tensor_tensor(el[:, :, here], lg[:, :, EG + g * EPG:EG + (g + 1) * EPG], over(g4[0][:, :, g], EPG), ALU.mult))
                then(dve.tensor_tensor(el[:, :, here], el[:, :, here], over(g4[2][:, :, g], EPG), ALU.add))
            then(dve.tensor_reduce(t1[2][:, :], el[:, :, :], AX.X, ALU.max))
            pick_first(e1[:, :, :], el[:, :, :], t1[2][:, :], first_e[:, :], NE, t1[1][:, :])
            then(dve.scalar_tensor_tensor(tmp[:, :, :], e1[:, :, :], -3e38, el[:, :, :], ALU.mult, ALU.add))
            then(dve.tensor_reduce(t1[3][:, :], tmp[:, :, :], AX.X, ALU.max))
            pick_first(e2[:, :, :], tmp[:, :, :], t1[3][:, :], first_e[:, :], NE, t1[1][:, :])
            dve.tensor_tensor(t1[5][:, :], t1[3][:, :], t1[2][:, :], ALU.subtract).then_inc(lowered, 1)
            then(dve.tensor_tensor(e1[:, :, :], e1[:, :, :], over(real[:, :], NE), ALU.mult))
            then(dve.tensor_tensor(e2[:, :, :], e2[:, :, :], over(real[:, :], NE), ALU.mult))
            dve.tensor_tensor(tmp[:, :, :], e1[:, :, :], e2[:, :, :], ALU.add).then_inc(chosen, 1)
            dve.wait_ge(exped, 2)
            then(dve.tensor_reduce(t1[4][:, :], g4[1][:, :, :], AX.X, ALU.add))
            then(dve.scalar_tensor_tensor(t1[6][:, :], t1[5][:, :], 1.0, t1[4][:, :], ALU.add, ALU.mult))
            then(dve.reciprocal(weight[:, :, 0], t1[6][:, :]))
            then(dve.tensor_tensor(weight[:, :, 1], weight[:, :, 0], t1[5][:, :], ALU.mult))
            dve.wait_ge(counted, 1)
            for i, (a0, b0) in enumerate(((0, HALF), (HALF, TILES))):
                w = (b0 - a0) * NE
                then(dve.tensor_copy(tile_count[:, a0:b0, :], ps_sum[:, i, 0:w].rearrange("p (t e) -> p t e", e=NE)))
            then(dve.tensor_copy(counts[:, 0, PADT:, :], tile_count[:, :, :]))
            cur = 0
            for d in (1, 2, 4, 8, 16):
                then(dve.tensor_tensor(counts[:, 1 - cur, PADT:, :], counts[:, cur, PADT:, :], counts[:, cur, PADT - d:PADT + TILES - d, :], ALU.add))
                cur = 1 - cur
            total = counts[:, cur, PADT + TILES - 1, :]
            then(dve.tensor_scalar(nblk[:, :], total, float(P - 1), None, ALU.add))
            then(dve.tensor_copy(nblk_i[:, :], nblk[:, :]))
            then(dve.tensor_scalar(nblk_i[:, :], nblk_i[:, :], 7, None, ALU.logical_shift_right))
            then(dve.tensor_copy(nblk[:, :], nblk_i[:, :]))
            then(dve.tensor_copy(ends[:, 0, PADE:], nblk[:, :]))
            ec = 0
            for d in (1, 2, 4, 8, 16):
                then(dve.tensor_tensor(ends[:, 1 - ec, PADE:], ends[:, ec, PADE:], ends[:, ec, PADE - d:PADE + NE - d], ALU.add))
                ec = 1 - ec
            then(dve.tensor_tensor(start[:, :], ends[:, ec, PADE:], nblk[:, :], ALU.subtract))
            then(dve.tensor_tensor(where[:, :, :], counts[:, cur, PADT:, :], tile_count[:, :, :], ALU.subtract))
            for i, (a0, b0) in enumerate(((0, HALF), (HALF, TILES))):
                w = (b0 - a0) * NE
                then(dve.tensor_tensor(where[:, a0:b0, :], where[:, a0:b0, :], ps_rank[:, i, 0:w].rearrange("p (t e) -> p t e", e=NE), ALU.add))
            then(dve.tensor_scalar(start[:, :], start[:, :], float(P), None, ALU.mult))
            then(dve.tensor_tensor(where[:, :, :], where[:, :, :], table(start[:, :], NE), ALU.add))
            for k, e in enumerate((e1, e2)):
                then(dve.tensor_tensor(tmp[:, :, :], where[:, :, :], e[:, :, :], ALU.mult))
                then(dve.tensor_reduce(dest_f[:, :, k], tmp[:, :, :], AX.X, ALU.add))
                then(dve.tensor_copy(dest[:, k, :], dest_f[:, :, k]))
            last_e = ends[:, ec, PADE:][:, None, :].broadcast_to([P, BLOCKS, NE])
            then(dve.tensor_tensor(block_no[:, :, :], last_e, block_no[:, :, :], ALU.is_le))
            then(dve.tensor_reduce(owner[:, :], block_no[:, :, :], AX.X, ALU.add))
            then(dve.tensor_scalar(owner[:, :], owner[:, :], float(NE - 1), None, ALU.min))
            dve.tensor_copy(owner_i[:, :], owner[:, :]).then_inc(placed, 1)


def experts(nc, xn, slots, blocks_in, w_gate, w_up, w_down, ident_in, y_slots):
    with ExitStack() as ctx:
        m = Memory(nc, ctx, "moe")
        ident = m.sb("ident", [P, P])
        owner = m.sb("owner", [1, BLOCKS], I32)
        wg = m.sb("wg", [P, 2, KC, FE])
        wu = m.sb("wu", [P, 2, KC, FE])
        wd = m.sb("wd", [P, 2, FC, D])
        idx = m.sb("idx", [P, 2, SLOT], I32)
        xg = m.sb("xg", [P, 2, D])
        xgT = m.sb("xgT", [P, 2, KC, P])
        sig = m.sb("sig", [P, FE])
        hid = m.sb("hid", [P, 2, FE])
        hidT = m.sb("hidT", [P, FC, P])
        y = m.sb("y", [P, 2, D])
        ps_turn = m.ps("turn", [P, 2, 512])
        ps_gu = m.ps("gu", [P, 2, 512])
        ps_y = m.ps("y_ps", [P, 2, 512])
        ps_h = m.ps("h_ps", [P, 512])
        consts_in = m.sem("consts_in")
        wg_in = [m.sem(f"wg_in{s}") for s in range(2)]
        wd_in = [m.sem(f"wd_in{s}") for s in range(2)]
        idx_in = [m.pool_sem(f"idx_in{s}") for s in range(2)]
        x_in = [m.pool_sem(f"x_in{s}") for s in range(2)]
        x_turned = m.sem("x_turned")
        x_copied = m.sem("x_copied")
        gu_done = m.sem("gu_done")
        sig_done = m.sem("sig_done")
        gated = m.sem("gated")
        hid_done = m.sem("hid_done")
        h_turned = m.sem("h_turned")
        h_copied = m.sem("h_copied")
        y_done = m.sem("y_done")
        y_copied = m.sem("y_copied")
        stored = [m.sem(f"stored{s}") for s in range(2)]
        block = m.block()

        def loop(eng, body):
            by_twos(eng, BLOCKS, body)

        @block.sync
        def _(sp):
            sp.dma_start(ident[:, :], ident_in).then_inc(consts_in, 16)
            sp.dma_start(owner[:, :], blocks_in).then_inc(consts_in, 16)
            sp.wait_ge(consts_in, 32)

            def load(i, s, k):
                e = sp.value_load(owner[0:1, bass.ds(i, 1)], min_val=0, max_val=NE - 1)
                wait_apart(sp, gu_done, i - 1, (consts_in, 32))
                sp.dma_start(wg[:, s], w_gate[bass.ds(e, 1)].rearrange("o (c p) n -> p (o c) n", p=P)).then_inc(wg_in[s], 16)
                sp.dma_start(wu[:, s], w_up[bass.ds(e, 1)].rearrange("o (c p) n -> p (o c) n", p=P)).then_inc(wg_in[s], 16)
                wait_apart(sp, y_done, i - 1, (consts_in, 32))
                sp.dma_start(wd[:, s], w_down[bass.ds(e, 1)].rearrange("o (c p) n -> p (o c) n", p=P)).then_inc(wd_in[s], 16)
            loop(sp, load)

        @block.gpsimd
        def _(pool):
            pool.dma_start(idx[:, 0, :], slots[rows(0), :]).then_inc(idx_in[0], 16)

            def gather(i, s, k):
                wait(pool, x_turned, i)
                pool.wait_ge(idx_in[s], 16 * k + 16)
                pool.dma_start(idx[:, 1 - s, :], slots[rows(i + 1), :]).then_inc(idx_in[1 - s], 16)
                pool.indirect_dma_start(out=xg[:, s, :], out_offset=None, in_=xn,
                                        in_offset=bass.IndirectOffsetOnAxis(ap=idx[:, s, 0:1], axis=0)).then_inc(x_in[s], 16)

            loop(pool, gather)
            pool.wait_ge(idx_in[0], 16 * (BLOCKS // 2 + 1))

        @block.tensor
        def _(pe):
            pe.wait_ge(consts_in, 32)

            def step(i, s, k):
                pe.wait_ge(x_in[s], 16 * k + 16)
                wait(pe, x_copied, i)
                for c in range(KC):
                    last = pe.transpose(ps_turn[:, c // 4, (c % 4) * P:(c % 4 + 1) * P], xg[:, s, c * P:(c + 1) * P], ident[:, :])
                last.then_inc(x_turned, 1)
                pe.wait_ge(x_copied, i + 1)
                pe.wait_ge(wg_in[s], 32 * k + 32)
                wait(pe, hid_done, i)
                for c in range(KC):
                    for b, w in enumerate((wg, wu)):
                        last = pe.matmul(ps_gu[:, b, :], xgT[:, s, c, :], w[:, s, c, :], start=(c == 0), stop=(c == KC - 1))
                last.then_inc(gu_done, 1)
                pe.wait_ge(hid_done, i + 1)
                wait(pe, h_copied, i)
                for c in range(FC):
                    last = pe.transpose(ps_h[:, c * P:(c + 1) * P], hid[:, s, c * P:(c + 1) * P], ident[:, :])
                last.then_inc(h_turned, 1)
                pe.wait_ge(h_copied, i + 1)
                pe.wait_ge(wd_in[s], 16 * k + 16)
                wait(pe, y_copied, i)
                for c in range(FC):
                    for b in range(2):
                        last = pe.matmul(ps_y[:, b, :], hidT[:, c, :], wd[:, s, c, b * 512:(b + 1) * 512], start=(c == 0), stop=(c == FC - 1))
                last.then_inc(y_done, 1)
            loop(pe, step)

        @block.scalar
        def _(act):
            def step(i, s, k):
                act.wait_ge(x_turned, i + 1)
                wait(act, gu_done, i - 1)
                act.activation(xgT[:, s].rearrange("p (b c) n -> p b (c n)", b=2), ps_turn[:, :, :], ACT.Copy).then_inc(x_copied, 1)
                act.wait_ge(gu_done, i + 1)
                wait(act, gated, i)
                act.activation(sig[:, :], ps_gu[:, 0, :], ACT.Sigmoid).then_inc(sig_done, 1)
                act.wait_ge(h_turned, i + 1)
                act.activation(hidT[:, :, :].rearrange("p c n -> p (c n)"), ps_h[:, :], ACT.Copy).then_inc(h_copied, 1)
                act.wait_ge(y_copied, i + 1)
                act.dma_start(y_slots[rows(i), :], y[:, s, :]).then_inc(stored[s], 16)
            loop(act, step)
            for s in range(2):
                act.wait_ge(stored[s], 16 * BLOCKS // 2)

        @block.vector
        def _(dve):
            def step(i, s, k):
                dve.wait_ge(sig_done, i + 1)
                wait(dve, h_turned, i - 1)
                dve.tensor_tensor(hid[:, s, :], sig[:, :], ps_gu[:, 0, :], ALU.mult).then_inc(gated, 1)
                dve.wait_ge(gated, i + 1)
                dve.tensor_tensor(hid[:, s, :], hid[:, s, :], ps_gu[:, 1, :], ALU.mult).then_inc(hid_done, 1)
                dve.wait_ge(y_done, i + 1)
                if not (isinstance(i, int) and i < 2):
                    dve.wait_ge(stored[s], 16 * k)
                dve.tensor_copy(y[:, s, :].rearrange("p (b n) -> p b n", b=2), ps_y[:, :, :]).then_inc(y_copied, 1)
            loop(dve, step)


def gather_results(nc, h, y_slots, dest_in, weight_in, y_prompt, y_sample):
    with ExitStack() as ctx:
        m = Memory(nc, ctx, "final")
        dest = m.sb("dest", [P, 2, TILES], I32)
        weight = m.sb("weight", [P, TILES, 2])
        ht = m.sb("ht", [P, 2, D])
        ys = m.sb("ys", [P, 2, 2, D])
        out = m.sb("out", [P, 2, D])
        loaded = m.sem("loaded")
        h_in = [m.sem(f"h_in{s}") for s in range(2)]
        y_in = [m.pool_sem(f"y_in{s}") for s in range(2)]
        one = m.sem("one")
        two = m.sem("two")
        stored = [m.sem(f"stored{s}") for s in range(2)]
        block = m.block()

        def n_rows(t):
            return NS if t == TILES - 1 else P

        @block.sync
        def _(sp):
            sp.dma_start(dest[:, :, :], dest_in.rearrange("k (t p) -> p k t", p=P), allow_slow_non_contiguous=True).then_inc(loaded, 16)
            sp.dma_start(weight[:, :, :], weight_in.rearrange("(t p) k -> p t k", p=P), allow_slow_non_contiguous=True).then_inc(loaded, 16)
            for t in range(TILES):
                wait(sp, one, t - 1)
                sp.dma_start(ht[:, t % 2, :], h[t * P:(t + 1) * P, :]).then_inc(h_in[t % 2], 16)

        @block.gpsimd
        def _(pool):
            pool.wait_ge(loaded, 32)
            for t in range(TILES):
                n = n_rows(t)
                wait(pool, two, t - 1)
                for k in range(2):
                    pool.indirect_dma_start(out=ys[0:n, t % 2, k, :], out_offset=None, in_=y_slots,
                                            in_offset=bass.IndirectOffsetOnAxis(ap=dest[0:n, k, t:t + 1], axis=0)).then_inc(y_in[t % 2], 16)

        @block.vector
        def _(dve):
            dve.wait_ge(loaded, 32)
            for t in range(TILES):
                s, n = t % 2, n_rows(t)
                dve.wait_ge(h_in[s], 16 * (t // 2 + 1))
                dve.wait_ge(y_in[s], 32 * (t // 2 + 1))
                wait(dve, stored[s], 16 * (t // 2))
                dve.scalar_tensor_tensor(out[0:n, s, :], ys[0:n, s, 0, :], weight[0:n, t, 0:1], ht[0:n, s, :], ALU.mult, ALU.add).then_inc(one, 1)
                dve.wait_ge(one, t + 1)
                dve.scalar_tensor_tensor(out[0:n, s, :], ys[0:n, s, 1, :], weight[0:n, t, 1:2], out[0:n, s, :], ALU.mult, ALU.add).then_inc(two, 1)

        @block.scalar
        def _(act):
            for t in range(TILES):
                s = t % 2
                act.wait_ge(two, t + 1)
                if t < TILES - 1:
                    act.dma_start(y_prompt[t * P:(t + 1) * P, :], out[:, s, :]).then_inc(stored[s], 16)
                else:
                    act.dma_start(y_sample, out[0:NS, s, :]).then_inc(stored[s], 16)
            for s in range(2):
                act.wait_ge(stored[s], 16 * ((TILES + 1 - s) // 2))


def caches(nc, a, z, outs):
    pairs = []
    for g, w in enumerate(WIN):
        for i, n in enumerate("kv"):
            new = z[n][:, g * GW:(g + 1) * GW]
            pairs.append((outs[2 + 2 * g + i][0].rearrange("t h d -> t (h d)"), new[SEQ - w:SEQ, :]))
            keep = min(w, PAST + DEC_S)
            out = outs[9 + 2 * g + i].rearrange("b t h d -> b t (h d)")
            old = a[f"cache_{n}_w{w}"].rearrange("b t h d -> b t (h d)")
            pairs.append((out[:, 0:keep - DEC_S, :], old[:, LB[g] + DEC_S - keep:LB[g], :]))
            pairs.append((out[:, keep - DEC_S:keep, :], new[SEQ:SEQ + NS, :].rearrange("(b s) c -> b s c", b=DEC_B)))
    pairs.append((outs[8][0], z["u"][SEQ - PSTATE:SEQ, :]))
    pairs.append((outs[15][:, 0:PSTATE - DEC_S, :], a["state_pool"][:, DEC_S:PSTATE, :]))
    pairs.append((outs[15][:, PSTATE - DEC_S:PSTATE, :], z["u"][SEQ:SEQ + NS, :].rearrange("(b s) c -> b s c", b=DEC_B)))
    with ExitStack() as ctx:
        m = Memory(nc, ctx, "caches")
        copied = m.sem("copied")
        block = m.block()

        @block.sync
        def _(sp):
            for dst, src in pairs:
                sp.dma_start(dst, src).then_inc(copied, 16)
            sp.wait_ge(copied, 16 * len(pairs))


def build(nc, a, outs):
    def dram(name, shape, dt=F32):
        return nc.dram_tensor(name, shape, dt).ap()

    xT = dram("xT", [TILES, P, 2, KC, P])
    z = {n: dram("z_" + n, [ROWS, w]) for n, w in (("q", AW), ("k", AW), ("v", AW), ("u", PW), ("ga", D), ("gb", D))}
    att = dram("att", [NG, ROWS, ATTW])
    joined = [dram(f"joined_{n}", [DEC_B, P + DEC_S, GW]) for n in "kv"]
    poolT = dram("poolT", [TILES, P, 2, PG, P])
    h = dram("h", [ROWS, D])
    xn = dram("xn", [ROWS, D])
    logits = dram("logits", [ROWS, EG + NE])
    slots = dram("slots", [(BLOCKS + 1) * P, SLOT], I32)
    dest = dram("dest", [2, ROWS], I32)
    weight = dram("weight", [ROWS, 2])
    owners = dram("owners", [1, BLOCKS], I32)
    y_slots = dram("y_slots", [BLOCKS * P, D])
    caches_kv = [[a[f"cache_{n}_w{w}"].rearrange("b t h d -> b t (h d)") for n in "kv"] for w in WIN]

    norm_and_turn(nc, a["x"], a["ln1"], a["ident"], xT)
    project(nc, xT, a["w_in"], a["q_gain"], a["k_gain"], z)
    prompt_attention(nc, z, att, a["ident"], a["bias"])
    sample_attention(nc, z, att, caches_kv, joined, a["sbias"])
    pooling(nc, z, a["state_pool"], a["pool_lin"], a["pool_scale"], a["ident"], a["inv_count"], poolT)
    merge_and_route(nc, a["x"], z, att, poolT, a["w_pa"], a["w_pb"], a["w_o"], a["ln2"], a["w_rg"], a["b_rg"],
                    a["w_re"], a["b_re"], a["ident"], h, xn, logits)
    routing(nc, logits, a, slots, dest, weight, owners)
    caches(nc, a, z, outs)
    experts(nc, xn, slots, owners, a["w_gate"], a["w_up"], a["w_down"], a["ident"], y_slots)
    gather_results(nc, h, y_slots, dest, weight, outs[0][0], outs[1].rearrange("b t d -> (b t) d"))


def constants(np):
    slope = np.exp2(-8.0 * np.arange(1, NG * HG + 1, dtype=np.float32) / (NG * HG)).astype(np.float32)
    qi, kb = np.arange(P)[:, None], np.arange(2 * P)[None, :]
    rel = qi + P - kb
    valid = (rel >= 0) & (rel <= P)
    bias = np.full((NG + 2, P, HG, 2 * P), -1e30, np.float32)
    for g in range(NG):
        for h in range(HG):
            b = -slope[g * HG + h] * (DIL[g] * rel).astype(np.float32)
            bias[g, :, SEAT[h]] = np.where(valid, b, np.float32(-1e30))
            if g < 2:
                bias[NG + g, :, SEAT[h]] = np.where(valid & (kb >= P), b, np.float32(-1e30))
    sbias = np.zeros((P, NG, P + 1), np.float32)
    for g in range(NG):
        n = LB[g] // DIL[g]
        dist = (DIL[g] * (n - np.arange(n + 1))).astype(np.float32)
        sbias[:, g, :n + 1] = -slope[g * HG + np.arange(P) % HG][:, None] * dist[None, :]
    pos = np.arange(16)
    inv_count = np.stack([1.0 / np.minimum(pos + 1, 2 << g) for g in range(PG)]).astype(np.float32)
    e = np.arange(NE)
    tile_rows = np.arange(TILES)[None, :] * P + np.arange(P)[:, None]
    return {
        "ident": np.eye(P, dtype=np.float32),
        "ones": np.ones((P, P), np.float32),
        "before": (np.arange(P)[:, None] < np.arange(P)[None, :]).astype(np.float32),
        "bias": bias,
        "sbias": sbias,
        "inv_count": np.broadcast_to(inv_count, (P, PG, 16)).copy(),
        "first_group": np.broadcast_to((EG - np.arange(EG)).astype(np.float32), (P, EG)).copy(),
        "first_expert": np.broadcast_to((NE - e).astype(np.float32), (P, NE)).copy(),
        "block_no": np.broadcast_to(np.arange(BLOCKS, dtype=np.float32)[None, :, None], (P, BLOCKS, NE)).copy(),
        "real": (tile_rows < SEQ + NS).astype(np.float32),
        "token": np.broadcast_to(tile_rows[:, :, None], (P, TILES, SLOT)).astype(np.int32).copy(),
    }
def kernel(**inputs):
    import numpy as np
    import concourse.bacc as bacc
    from concourse.bass_utils import run_bass_kernel_spmd

    nc = bacc.Bacc("TRN2", target_bir_lowering=False, num_devices=1)
    arrays = {}
    ins = {}

    def give(name, a):
        a = np.ascontiguousarray(a)
        arrays[name] = a
        ins[name] = nc.dram_tensor(name, a.shape, mybir.dt.from_np(a.dtype), kind="ExternalInput").ap()

    x = np.zeros((ROWS, D), np.float32)
    x[:SEQ] = np.asarray(inputs["x_prompt"]).reshape(SEQ, D)
    x[SEQ:SEQ + NS] = np.asarray(inputs["x_sample"]).reshape(NS, D)
    give("x", x)
    for name, a in inputs.items():
        if not name.startswith("x_"):
            give(name, np.asarray(a))
    for name, a in constants(np).items():
        give(name, a)
    shapes = ([(1, SEQ, D), (DEC_B, DEC_S, D)]
              + [(1, w, HG, HD) for w in WIN for _ in range(2)] + [(1, PSTATE, PW)]
              + [(DEC_B, min(w, PAST + DEC_S), HG, HD) for w in WIN for _ in range(2)] + [(DEC_B, PSTATE, PW)])
    outs = [nc.dram_tensor(f"out_{i}", s, F32, kind="ExternalOutput").ap() for i, s in enumerate(shapes)]
    build(nc, ins, outs)
    r = run_bass_kernel_spmd(nc, [arrays], core_ids=[0])
    return tuple(r.results[0][f"out_{i}"] for i in range(len(shapes)))
```

```python
from contextlib import ExitStack

import concourse.bass as bass
from concourse import mybir

F32 = mybir.dt.float32
F32R = mybir.dt.float32r
I32 = mybir.dt.int32
U32 = mybir.dt.uint32
ACT = mybir.ActivationFunctionType
ALU = mybir.AluOpType
AX = mybir.AxisListType

P = 128
D = 1024
KC = D // P
SEQ, DEC_B, DEC_S = 2048, 8, 4
NS = DEC_B * DEC_S
TILES = SEQ // P + 1
ROWS = TILES * P
HD, HG = 64, 4
GW = HG * HD
NG = 3
AW = NG * GW
DIL = (1, 4, 16)
WIN = (128, 512, 2048)
PAST = 1024
LB = tuple(min(w, PAST) for w in WIN)
PW = 512
PG = 4
PSTATE = 15
NE, EG, EPG = 32, 4, 8
FE = 512
FC = FE // P
OVER = (2 * (SEQ + NS) - 2 * (P + 1)) // P
BLOCKS = 2 * NE + OVER + 2
EPS = 1e-6
SLOT = 16
SEAT = (0, 2, 1, 3)
ATTW = HG * (HD + 2)


def by_twos(eng, n, body):
    body(0, 0, 0)
    body(1, 1, 0)
    if n > 3:
        with eng.Fori(1, n // 2) as j:
            body(j * 2, 0, j)
            body(j * 2 + 1, 1, j)
    if n % 2:
        body(n - 1, 0, n // 2)


def rows(t):
    return bass.ds(t * P, P)


def wait_apart(eng, sem, count, done):
    if not isinstance(count, int) or count > 0:
        eng.wait_ge(*done)
        eng.wait_ge(sem, count)


class Memory:

    def __init__(self, nc, ctx, stage):
        self.nc, self.ctx, self.stage, self.sems = nc, ctx, stage, []

    def sb(self, name, shape, dt=F32):
        return self.ctx.enter_context(self.nc.sbuf_tensor(f"{self.stage}_{name}", shape, dt))

    def ps(self, name, shape, dt=F32):
        return self.ctx.enter_context(self.nc.psum_tensor(f"{self.stage}_{name}", shape, dt))

    def sem(self, name):
        self.sems.append(self.ctx.enter_context(self.nc.semaphore(f"{self.stage}_{name}")))
        return self.sems[-1]

    def pool_sem(self, name):
        self.sems.append(self.nc.alloc_semaphore(f"{self.stage}_{name}"))
        return self.sems[-1]

    def block(self):
        for s in self.sems:
            self.nc.gpsimd.sem_clear(s)
        self.nc.all_engine_barrier()
        return self.ctx.enter_context(self.nc.Block())


def norm_and_turn(nc, x, ln1, ident_in, xT):
    with ExitStack() as ctx:
        m = Memory(nc, ctx, "norm")
        xin = m.sb("xin", [P, 2, D])
        junk = m.sb("junk", [P, D])
        xn = m.sb("xn", [P, 2, D])
        split = m.sb("split", [P, 2, 2, D], F32R)
        lnrow = m.sb("lnrow", [P, D])
        ident = m.sb("ident", [P, P])
        eps = m.sb("eps", [P, 1])
        ss = m.sb("ss", [P, 2])
        rms = m.sb("rms", [P, 2])
        rstd = m.sb("rstd", [P, 2])
        turned = m.ps("turned", [P, 2, 2, 512])

        consts_in = m.sem("consts_in")
        eps_set = m.sem("eps_set")
        x_in = [m.sem(f"x_in{s}") for s in range(2)]
        squared = m.sem("squared")
        rooted = m.sem("rooted")
        inverted = m.sem("inverted")
        normed = m.sem("normed")
        turns = m.sem("turns")
        hi_done = m.sem("hi_done")
        lo_done = m.sem("lo_done")
        stored = [m.pool_sem(f"stored{s}") for s in range(2)]
        block = m.block()

        @block.sync
        def _(sp):
            sp.dma_start(lnrow[:, :], ln1[None, :].partition_broadcast(P)).then_inc(consts_in, 16)
            sp.dma_start(ident[:, :], ident_in).then_inc(consts_in, 16)

            def load(t, s, k):
                if not (isinstance(t, int) and t < 2):
                    sp.wait_ge(normed, t - 1)
                sp.dma_start(xin[:, s, :], x[rows(t), :]).then_inc(x_in[s], 16)
            by_twos(sp, TILES, load)

        @block.gpsimd
        def _(pool):
            pool.memset(eps[:, :], EPS).then_inc(eps_set, 1)

            def store(t, s, k):
                pool.wait_ge(lo_done, t + 1)
                pool.dma_start(xT[t].rearrange("p a c n -> p a (c n)"), split[:, s, :, :].bitcast(F32)).then_inc(stored[s], 16)
            by_twos(pool, TILES, store)
            pool.wait_ge(stored[0], 16 * (TILES - TILES // 2))
            pool.wait_ge(stored[1], 16 * (TILES // 2))

        @block.scalar
        def _(act):
            act.wait_ge(eps_set, 1)

            def step(t, s, k):
                act.wait_ge(x_in[s], 16 * k + 16)
                act.activation(junk[:, :], xin[:, s, :], ACT.Square, accum_out=ss[:, s:s + 1]).then_inc(squared, 1)
                act.wait_ge(squared, t + 1)
                act.activation(rms[:, s:s + 1], ss[:, s:s + 1], ACT.Sqrt, bias=eps[:, 0:1],
                               scale=1.0 / D).then_inc(rooted, 1)
                act.wait_ge(turns, t + 1)
                if not (isinstance(t, int) and t < 2):
                    act.wait_ge(stored[s], 16 * k)
                act.activation(split[:, s, 0, :].rearrange("p (b n) -> p b n", b=2), turned[:, s, :, :],
                               ACT.Copy).then_inc(hi_done, 1)
            by_twos(act, TILES, step)

        @block.vector
        def _(dve):
            dve.wait_ge(consts_in, 32)

            def step(t, s, k):
                dve.wait_ge(rooted, t + 1)
                dve.reciprocal(rstd[:, s:s + 1], rms[:, s:s + 1]).then_inc(inverted, 1)
                dve.wait_ge(inverted, t + 1)
                if not (isinstance(t, int) and t < 2):
                    dve.wait_ge(turns, t - 1)
                dve.scalar_tensor_tensor(xn[:, s, :], xin[:, s, :], rstd[:, s:s + 1], lnrow[:, :],
                                         ALU.mult, ALU.mult).then_inc(normed, 1)
                dve.wait_ge(hi_done, t + 1)
                dve.tensor_tensor(split[:, s, 1, :].rearrange("p (b n) -> p b n", b=2), turned[:, s, :, :],
                                  split[:, s, 0, :].bitcast(F32).rearrange("p (b n) -> p b n", b=2),
                                  ALU.subtract).then_inc(lo_done, 1)
            by_twos(dve, TILES, step)

        @block.tensor
        def _(pe):
            pe.wait_ge(consts_in, 32)

            def step(t, s, k):
                pe.wait_ge(normed, t + 1)
                if not (isinstance(t, int) and t < 2):
                    pe.wait_ge(lo_done, t - 1)
                for c in range(KC):
                    last = pe.transpose(turned[:, s, c // 4, (c % 4) * P:(c % 4 + 1) * P],
                                        xn[:, s, c * P:(c + 1) * P], ident[:, :])
                last.then_inc(turns, 1)
            by_twos(pe, TILES, step)


def project(nc, xT, w_in, q_gain, k_gain, z):
    groups = [("q", 0, 384), ("k", AW, 384), ("v", 2 * AW, 384), ("u", 3 * AW, 256),
              ("ga", 3 * AW + PW, 512), ("gb", 3 * AW + PW + D, 512)]
    n_slot = (TILES - TILES // 2, TILES // 2)
    heads = AW // HD
    with ExitStack() as ctx:
        m = Memory(nc, ctx, "proj")
        w_raw = m.sb("w_raw", [P, KC, D])
        w_hi = [m.sb(f"w_hi{i}", [P, KC, D], F32R) for i in range(2)]
        w_lo = [m.sb(f"w_lo{i}", [P, KC, D], F32R) for i in range(2)]
        xs = m.sb("xs", [P, 2, 2, KC, P], F32R)
        out = m.sb("out", [P, 2, D])
        sq = m.sb("sq", [P, AW])
        gain = m.sb("gain", [P, 2, AW])
        eps = m.sb("eps", [P, 1])
        ss = m.sb("ss", [P, heads])
        rms = m.sb("rms", [P, heads])
        rstd = m.sb("rstd", [P, heads])
        acc = m.ps("acc", [P, 2, 2, 512])

        consts_in = m.sem("consts_in")
        eps_set = m.sem("eps_set")
        w_loaded = [m.pool_sem(f"w_loaded{c}") for c in range(KC)]
        w_hi_done = m.sem("w_hi_done")
        w_lo_done = m.sem("w_lo_done")
        x_loaded = [m.sem(f"x_loaded{s}") for s in range(2)]
        products = m.sem("products")
        squared = m.sem("squared")
        summed = m.sem("summed")
        rooted = m.sem("rooted")
        inverted = m.sem("inverted")
        scaled = m.sem("scaled")
        left_psum = m.sem("left_psum")
        ready = m.sem("ready")
        stored = [m.pool_sem(f"stored{s}") for s in range(2)]
        block = m.block()

        def width(g):
            return 2 * groups[g][2]

        @block.sync
        def _(sp):
            sp.dma_start(gain[:, 0, :], q_gain.rearrange("h d -> (h d)")[None, :].partition_broadcast(P)).then_inc(consts_in, 16)
            sp.dma_start(gain[:, 1, :], k_gain.rearrange("h d -> (h d)")[None, :].partition_broadcast(P)).then_inc(consts_in, 16)
            for g in range(len(groups)):
                def load(t, s, k, g=g):
                    before = g * TILES + t
                    if not (isinstance(t, int) and t < 2):
                        sp.wait_ge(products, before - 1)
                    elif g and t < 2:
                        sp.wait_ge(products, g * TILES)
                    sp.dma_start(xs[:, s, :, :, :].bitcast(F32), xT[t]).then_inc(x_loaded[s], 16)
                by_twos(sp, TILES, load)

        @block.gpsimd
        def _(pool):
            pool.memset(eps[:, :], EPS).then_inc(eps_set, 1)

            def load_w(g):
                _, col, nb = groups[g]
                for c in range(KC):
                    if g:
                        pool.wait_ge(w_lo_done, KC * (g - 1) + c + 1)
                    pool.dma_start(w_raw[:, c, 0:2 * nb], w_in[c * P:(c + 1) * P, col:col + 2 * nb]).then_inc(w_loaded[c], 16)

            load_w(0)
            for g in range(len(groups)):
                if g + 1 < len(groups):
                    load_w(g + 1)

                def store(t, s, k, g=g):
                    pool.wait_ge(ready, g * TILES + t + 1)
                    pool.dma_start(z[groups[g][0]][rows(t), :], out[:, s, 0:width(g)]).then_inc(stored[s], 16)
                by_twos(pool, TILES, store)
            for s in range(2):
                pool.wait_ge(stored[s], 16 * n_slot[s] * len(groups))

        def slot_free(eng, g, t, s, k):
            if not (isinstance(t, int) and t < 2 and g == 0):
                eng.wait_ge(stored[s], 16 * (g * n_slot[s] + k))

        @block.scalar
        def _(act):
            def split_w(g, c, wait):
                w = width(g)
                act.wait_ge(wait, 16 * (g + 1))
                act.activation(w_hi[g % 2][:, c, 0:w], w_raw[:, c, 0:w], ACT.Copy).then_inc(w_hi_done, 1)

            act.wait_ge(eps_set, 1)
            for c in range(KC):
                split_w(0, c, w_loaded[c])
            for g, (name, _, nb) in enumerate(groups):
                def tile(t, s, k, g=g, name=name, nb=nb):
                    n = g * TILES + t
                    act.wait_ge(products, n + 1)
                    if name in "qk":
                        act.activation(sq[:, :].rearrange("p (b n) -> p b n", b=2), acc[:, s, :, 0:nb],
                                       ACT.Square).then_inc(squared, 1)
                        act.wait_ge(summed, n + 1)
                        act.activation(rms[:, :], ss[:, :], ACT.Sqrt, bias=eps[:, 0:1], scale=1.0 / HD).then_inc(rooted, 1)
                    else:
                        slot_free(act, g, t, s, k)
                        act.activation(out[:, s, 0:2 * nb].rearrange("p (b n) -> p b n", b=2), acc[:, s, :, 0:nb],
                                       ACT.Sigmoid if name in ("ga", "gb") else ACT.Copy).then_inc(ready, 1)
                by_twos(act, TILES, tile)
                if g + 1 < len(groups):
                    for c in range(KC):
                        split_w(g + 1, c, w_loaded[c])

        @block.vector
        def _(dve):
            def split_w(g, c):
                w = width(g)
                dve.wait_ge(w_hi_done, KC * g + c + 1)
                dve.tensor_tensor(w_lo[g % 2][:, c, 0:w], w_raw[:, c, 0:w], w_hi[g % 2][:, c, 0:w].bitcast(F32),
                                  ALU.subtract).then_inc(w_lo_done, 1)

            dve.wait_ge(consts_in, 32)
            for c in range(KC):
                split_w(0, c)
            for g, (name, _, nb) in enumerate(groups):
                def tile(t, s, k, g=g, nb=nb):
                    n = g * TILES + t
                    dve.wait_ge(squared, n + 1)
                    dve.tensor_reduce(ss[:, :], sq[:, :].rearrange("p (h d) -> p h d", d=HD), AX.X, ALU.add).then_inc(summed, 1)
                    dve.wait_ge(rooted, n + 1)
                    dve.reciprocal(rstd[:, :], rms[:, :]).then_inc(inverted, 1)
                    dve.wait_ge(inverted, n + 1)
                    slot_free(dve, g, t, s, k)
                    for b in range(2):
                        r = rstd[:, b * 6:(b + 1) * 6][:, :, None].broadcast_to([P, 6, HD])
                        last = dve.tensor_tensor(out[:, s, b * nb:(b + 1) * nb].rearrange("p (h d) -> p h d", d=HD),
                                                 acc[:, s, b, 0:nb].rearrange("p (h d) -> p h d", d=HD), r, ALU.mult)
                    last.then_inc(scaled, 1)
                    dve.wait_ge(scaled, n + 1)
                    dve.tensor_tensor(out[:, s, 0:AW], out[:, s, 0:AW], gain[:, g, :], ALU.mult).then_inc(ready, 1)
                if name in "qk":
                    by_twos(dve, TILES, tile)
                if g + 1 < len(groups):
                    for c in range(KC):
                        split_w(g + 1, c)

        @block.tensor
        def _(pe):
            for g, (name, _, nb) in enumerate(groups):
                hi, lo = w_hi[g % 2], w_lo[g % 2]
                pe.wait_ge(w_lo_done, KC * (g + 1))

                def tile(t, s, k, g=g, nb=nb, hi=hi, lo=lo):
                    n = g * TILES + t
                    pe.wait_ge(x_loaded[s], 16 * (g * n_slot[s] + k) + 16)
                    if not (isinstance(t, int) and t < 2):
                        pe.wait_ge(ready, n - 1)
                    elif g:
                        pe.wait_ge(ready, g * TILES)
                    for c in range(KC):
                        for i, (xp, w) in enumerate(((0, hi), (0, lo), (1, hi))):
                            for b in range(2):
                                last = pe.matmul(acc[:, s, b, 0:nb], xs[:, s, xp, c, :], w[:, c, b * nb:(b + 1) * nb],
                                                 start=(c == 0 and i == 0), stop=(c == KC - 1 and i == 2))
                    last.then_inc(products, 1)
                by_twos(pe, TILES, tile)


def wait(eng, sem, count):
    if not isinstance(count, int) or count > 0:
        eng.wait_ge(sem, count)


def by_fours(eng, n, body, peel_last=False):
    for s in range(4):
        body(s, s, 0)
    with eng.Fori(1, n // 4 - peel_last) as j:
        for s in range(4):
            body(j * 4 + s, s, j)
    if peel_last:
        for s in range(4):
            body(n - 4 + s, s, n // 4 - 1)


def prompt_attention(nc, z, att, ident_in, bias_in):
    NB = SEQ // P
    steps = NB * NG
    with ExitStack() as ctx:
        m = Memory(nc, ctx, "attn")
        ident = m.sb("ident", [P, P])
        bias = m.sb("bias", [P, NG + 1, HG, 2 * P])
        bias1 = m.sb("bias1", [P, HG, 2 * P])
        q = m.sb("q", [P, 4, GW])
        k = m.sb("k", [P, 4, 2, GW])
        v = m.sb("v", [P, 4, 2, GW])
        qkT = m.sb("qkT", [P, 2, 6, P])
        sc = m.sb("sc", [P, 2, HG, 2 * P])
        pr = m.sb("pr", [P, 2, HG, 2 * P])
        prT = m.sb("prT", [P, 2, HG, 2, P])
        nmax = m.sb("nmax", [P, 4, HG])
        out = m.sb("out", [P, 4, HG, HD + 2])
        ps_turn = m.ps("turn", [P, 2, 512])
        ps_sc = m.ps("sc_ps", [P, HG, 2 * P])
        ps_prT = m.ps("prT_ps", [P, HG, 2, P])
        ps_o = m.ps("o_ps", [P, 2, 512])

        consts_in = m.sem("consts_in")
        qk_in = [m.sem(f"qk_in{s}") for s in range(4)]
        v_in = [m.sem(f"v_in{s}") for s in range(4)]
        qk_turned = m.sem("qk_turned")
        qk_copied = m.sem("qk_copied")
        scored = m.sem("scored")
        biased = m.sem("biased")
        maxed = m.sem("maxed")
        negated = m.sem("negated")
        exped = m.sem("exped")
        p_turned = m.sem("p_turned")
        p_copied_act = m.sem("p_copied_act")
        p_copied_dve = m.sem("p_copied_dve")
        weighted = m.sem("weighted")
        o_copied = m.sem("o_copied")
        stored = [m.pool_sem(f"stored{s}") for s in range(4)]
        block = m.block()

        def nk(g):
            return 1 if g == 2 else 2

        def view(name, g):
            a = z[name][:, g * GW:(g + 1) * GW]
            return a.rearrange("(l r) c -> r l c", r=DIL[g])

        def place(g, i):
            if DIL[g] == NB:
                return i, 0, 0
            if g == 0:
                return 0, i * P, (max(i - 1, 0) * P if isinstance(i, int) else (i - 1) * P)
            if isinstance(i, int):
                return i % DIL[g], i // DIL[g] * P, max(i // DIL[g] - 1, 0) * P
            return i[1], i[0] * P, (i[0] - 1) * P

        def all_blocks(eng, body):
            for g in range(NG):
                def one(t, s, j, g=g):
                    i = t if isinstance(t, int) or g != 1 else (j, s)
                    body(g, g * NB + t, s, g * (NB // 4) + j, i)
                by_fours(eng, NB, one, peel_last=(g == NG - 1))

        @block.sync
        def _(sp):
            sp.dma_start(ident[:, :], ident_in).then_inc(consts_in, 16)
            sp.dma_start(bias[:, :, :, :], bias_in[0:NG + 1].rearrange("g p h k -> p g h k")).then_inc(consts_in, 16)
            sp.dma_start(bias1[:, :, :], bias_in[NG + 1]).then_inc(consts_in, 16)

            def load(g, n, s, j, i):
                r, own, former = place(g, i)
                wait(sp, qk_turned, n - 3)
                wait_apart(sp, weighted, n - 3, (consts_in, 48))
                qv, kv, vv = view("q", g), view("k", g), view("v", g)
                sp.dma_start(q[:, s, :], qv[r, bass.ds(own, P), :]).then_inc(qk_in[s], 16)
                sp.dma_start(k[:, s, 1, :], kv[r, bass.ds(own, P), :]).then_inc(qk_in[s], 16)
                sp.dma_start(v[:, s, 1, :], vv[r, bass.ds(own, P), :]).then_inc(v_in[s], 16)
                sp.dma_start(k[:, s, 0, :], kv[r, bass.ds(former, P), :]).then_inc(qk_in[s], 16)
                sp.dma_start(v[:, s, 0, :], vv[r, bass.ds(former, P), :]).then_inc(v_in[s], 16)
            all_blocks(sp, load)

        @block.gpsimd
        def _(pool):
            def store(g, n, s, j, i):
                r, own, _ = place(g, i)
                wait_apart(pool, o_copied, n + 1, (consts_in, 48))
                dst = att[g].rearrange("(l r) c -> r l c", r=DIL[g])
                pool.dma_start(dst[r, bass.ds(own, P), :], out[:, s, :, :].rearrange("p h e -> p (h e)")).then_inc(stored[s], 16)
            all_blocks(pool, store)
            for s in range(4):
                pool.wait_ge(stored[s], 16 * steps // 4)

        @block.tensor
        def _(pe):
            def turn_qk(g, n, s, j):
                pe.wait_ge(qk_in[s], 48 * (j + 1))
                wait(pe, qk_copied, n)
                parts = [q[:, s, 0:P], q[:, s, P:GW]] + [k[:, s, b, c * P:(c + 1) * P] for b in range(2) for c in range(2)]
                for x, part in enumerate(parts):
                    last = pe.transpose(ps_turn[:, x // 3, (x % 3) * P:(x % 3 + 1) * P], part, ident[:, :])
                last.then_inc(qk_turned, 1)

            def scores(g, n, s):
                pe.wait_ge(qk_copied, n + 1)
                wait(pe, biased, n)
                for h in range(HG):
                    lo = HD * (h % 2)
                    for b in range(2 - nk(g), 2):
                        last = pe.matmul(ps_sc[:, SEAT[h], b * P:(b + 1) * P], qkT[lo:lo + HD, s % 2, h // 2, :],
                                         qkT[lo:lo + HD, s % 2, 2 + 2 * b + h // 2, :], start=True, stop=True)
                last.then_inc(scored, 1)

            def turn_p(g, n, s):
                pe.wait_ge(exped, HG * (n + 1))
                wait(pe, p_copied_act, n)
                wait(pe, p_copied_dve, n)
                for h in range(HG):
                    for b in range(2 - nk(g), 2):
                        last = pe.transpose(ps_prT[:, SEAT[h], b, :], pr[:, s % 2, SEAT[h], b * P:(b + 1) * P], ident[:, :])
                last.then_inc(p_turned, 1)

            def weigh_v(g, n, s, j):
                pe.wait_ge(v_in[s], 32 * (j + 1))
                pe.wait_ge(p_copied_act, n + 1)
                pe.wait_ge(p_copied_dve, n + 1)
                wait(pe, o_copied, n - 1)
                for h in range(HG):
                    for b in range(2 - nk(g), 2):
                        last = pe.matmul(ps_o[:, s % 2, h * HD:(h + 1) * HD], prT[:, s % 2, SEAT[h], b, :],
                                         v[:, s, b, h * HD:(h + 1) * HD], start=(b == 2 - nk(g)), stop=(b == 1))
                last.then_inc(weighted, 1)

            pe.wait_ge(consts_in, 48)
            turn_qk(0, 0, 0, 0)

            def step(g, n, s, j, i):
                first = isinstance(i, int) and i < 2
                gb = g - 1 if first else g
                sb_, jb = (s + 2) % 4, (j if s >= 2 else j - 1)
                if not (isinstance(n, int) and n < 2):
                    turn_p(gb, n - 2, sb_)
                scores(g, n, s)
                sn, jn = (s + 1) % 4, (j if s < 3 else j + 1)
                if not (isinstance(n, int) and n == steps - 1):
                    turn_qk(g, n + 1, sn, jn)
                if not (isinstance(n, int) and n < 2):
                    weigh_v(gb, n - 2, sb_, jb)

            all_blocks(pe, step)
            for n in (steps - 2, steps - 1):
                turn_p(NG - 1, n, n % 4)
                weigh_v(NG - 1, n, n % 4, n // 4)

        @block.vector
        def _(dve):
            def copy_p(g, n, s):
                b = 2 - nk(g)
                dve.wait_ge(p_turned, n + 1)
                wait(dve, weighted, n - 1)
                dve.tensor_copy(prT[:, s % 2, 2:4, b:2, :], ps_prT[:, 2:4, b:2, :]).then_inc(p_copied_dve, 1)

            def copy_o(n, s):
                dve.wait_ge(weighted, n + 1)
                dve.tensor_copy(out[:, s, :, 0:HD], ps_o[:, s % 2, 0:GW].rearrange("p (h d) -> p h d", d=HD)).then_inc(o_copied, 1)

            dve.wait_ge(consts_in, 48)

            def step(g, n, s, j, i):
                gb = g - 1 if isinstance(i, int) and i < 2 else g
                if not (isinstance(n, int) and n < 2):
                    copy_p(gb, n - 2, (s + 2) % 4)
                b = 2 - nk(g)
                table = bias[:, g, :, b * P:2 * P]
                if g == 0 and isinstance(i, int) and i == 0:
                    table = bias[:, NG, :, :]
                if g == 1 and isinstance(i, int) and i < DIL[1]:
                    table = bias1[:, :, :]
                dve.wait_ge(scored, n + 1)
                wait(dve, exped, HG * (n - 1))
                dve.scalar_tensor_tensor(sc[:, s % 2, :, b * P:2 * P], ps_sc[:, :, b * P:2 * P], HD ** -0.5,
                                         table, ALU.mult, ALU.add).then_inc(biased, 1)
                dve.wait_ge(biased, n + 1)
                wait(dve, stored[s], 16 * j)
                dve.tensor_reduce(out[:, s, :, HD].rearrange("p (i o) -> p o i", o=2),
                                  sc[:, s % 2, :, b * P:2 * P].rearrange("p (o i) k -> p o i k", o=2), AX.X, ALU.max).then_inc(maxed, 1)
                dve.wait_ge(maxed, n + 1)
                dve.tensor_scalar(nmax[:, s, :], out[:, s, :, HD], -1.0, None, ALU.mult).then_inc(negated, 1)
                if not (isinstance(n, int) and n < 2):
                    copy_o(n - 2, (s + 2) % 4)
            all_blocks(dve, step)
            for n in (steps - 2, steps - 1):
                copy_p(NG - 1, n, n % 4)
                copy_o(n, n % 4)

        @block.scalar
        def _(act):
            def copy_p(g, n, s):
                b = 2 - nk(g)
                act.wait_ge(p_turned, n + 1)
                wait(act, weighted, n - 1)
                act.activation(prT[:, s % 2, 0:2, b:2, :], ps_prT[:, 0:2, b:2, :], ACT.Copy).then_inc(p_copied_act, 1)

            def copy_qk(n, s):
                act.wait_ge(qk_turned, n + 1)
                wait(act, scored, n - 1)
                act.activation(qkT[:, s % 2, :, :].rearrange("p (a x) n -> p a (x n)", a=2), ps_turn[:, :, 0:3 * P],
                               ACT.Copy).then_inc(qk_copied, 1)

            copy_qk(0, 0)

            def step(g, n, s, j, i):
                gb = g - 1 if isinstance(i, int) and i < 2 else g
                if not (isinstance(n, int) and n < 2):
                    copy_p(gb, n - 2, (s + 2) % 4)
                if not (isinstance(n, int) and n == steps - 1):
                    copy_qk(n + 1, (s + 1) % 4)
                b = 2 - nk(g)
                act.wait_ge(negated, n + 1)
                for h in range(HG):
                    act.activation(pr[:, s % 2, SEAT[h], b * P:2 * P], sc[:, s % 2, SEAT[h], b * P:2 * P], ACT.Exp,
                                   bias=nmax[:, s, h:h + 1], accum_out=out[:, s, h, HD + 1:HD + 2]).then_inc(exped, 1)
            all_blocks(act, step)
            for n in (steps - 2, steps - 1):
                copy_p(NG - 1, n, n % 4)
def sample_attention(nc, z, att, caches_kv, joined, sbias_in):
    with ExitStack() as ctx:
        m = Memory(nc, ctx, "samp")
        q = m.sb("q", [P, 2, HD])
        kv = [m.sb(f"kv{i}", [P, 2, P + 1, HD]) for i in range(2)]
        prod = m.sb("prod", [P, (P + 1) * HD])
        sbias = m.sb("sbias", [P, NG, P + 1])
        sc = m.sb("sc", [P, P + 1])
        ex = m.sb("ex", [P, P + 1])
        nmax = m.sb("nmax", [P, 1])
        out = m.sb("out", [P, NG, HD + 2])
        consts_in = m.sem("consts_in")
        joined_sem = m.sem("joined")
        q_in = [m.sem(f"q_in{i}") for i in range(2)]
        k_in = [m.sem(f"k_in{i}") for i in range(2)]
        v_in = [m.sem(f"v_in{i}") for i in range(2)]
        steps = m.sem("steps")
        negated = m.sem("negated")
        exped = m.sem("exped")
        kv_read = m.sem("kv_read")
        done = m.sem("done")
        stored = m.sem("stored")
        block = m.block()

        def new_rows(name, g):
            return z[name][SEQ:SEQ + NS, g * GW:(g + 1) * GW].rearrange("r (h d) -> h r d", d=HD)

        @block.sync
        def _(sp):
            sp.dma_start(sbias[:, :, :], sbias_in).then_inc(consts_in, 16)
            for i, name in enumerate("kv"):
                sp.dma_start(joined[i][:, 0:P, :], caches_kv[0][i]).then_inc(joined_sem, 16)
                sp.dma_start(joined[i][:, P:P + DEC_S, :], z[name][SEQ:SEQ + NS, 0:GW].rearrange("(b s) c -> b s c", b=DEC_B)).then_inc(joined_sem, 16)
            sp.wait_ge(joined_sem, 64)
            for g in range(NG):
                n = LB[g] // DIL[g]
                if g >= 2:
                    sp.wait_ge(kv_read, g - 1)
                for h in range(HG):
                    sp.dma_start(q[h::HG, g % 2, :], new_rows("q", g)[h]).then_inc(q_in[g % 2], 16)
                for i, name in enumerate("kv"):
                    sem = (k_in, v_in)[i][g % 2]
                    for b in range(DEC_B):
                        src = joined[i][b] if g == 0 else caches_kv[g][i][b]
                        rows_ = n + 1 if g == 0 else n
                        win = bass.AP(src.tensor, src.offset, [[HD, DEC_S * HG], [DIL[g] * GW, rows_], [1, HD]])
                        sp.dma_start(kv[g % 2][b * 16:(b + 1) * 16, i, 0:rows_, :], win).then_inc(sem, 16)
                    if g > 0:
                        for h in range(HG):
                            sp.dma_start(kv[g % 2][h::HG, i, n, :], new_rows(name, g)[h]).then_inc(sem, 16)
            for g in range(NG):
                sp.wait_ge(done, g + 1)
                flat = att[g].rearrange("r (h e) -> (r h) e", e=HD + 2)
                for c in range(HG):
                    lo = SEQ * HG + c * P
                    sp.dma_start(flat[lo:lo + P, :], out[:, g, :]).then_inc(stored, 16)
            sp.wait_ge(stored, 16 * NG * HG)

        @block.vector
        def _(dve):
            dve.wait_ge(consts_in, 16)
            n_in = lambda g: 16 * (DEC_B + (HG if g else 0))
            seen_k = [0, 0]
            n_steps = 0
            for g in range(NG):
                n = LB[g] // DIL[g] + 1
                k, v = kv[g % 2][:, 0, 0:n, :], kv[g % 2][:, 1, 0:n, :]
                seen_k[g % 2] += n_in(g)
                pr = prod[:, 0:n * HD].rearrange("p (k d) -> p k d", d=HD)
                dve.wait_ge(q_in[g % 2], 16 * HG * (g // 2 + 1))
                dve.wait_ge(k_in[g % 2], seen_k[g % 2])
                dve.tensor_tensor(pr, k, q[:, g % 2, :][:, None, :].broadcast_to([P, n, HD]), ALU.mult).then_inc(steps, 1)
                n_steps += 1
                dve.wait_ge(steps, n_steps)
                dve.tensor_reduce(sc[:, 0:n], pr, AX.X, ALU.add).then_inc(steps, 1)
                n_steps += 1
                dve.wait_ge(steps, n_steps)
                dve.scalar_tensor_tensor(sc[:, 0:n], sc[:, 0:n], HD ** -0.5, sbias[:, g, 0:n], ALU.mult, ALU.add).then_inc(steps, 1)
                n_steps += 1
                dve.wait_ge(steps, n_steps)
                dve.tensor_reduce(out[:, g, HD:HD + 1], sc[:, 0:n], AX.X, ALU.max).then_inc(steps, 1)
                n_steps += 1
                dve.wait_ge(steps, n_steps)
                dve.tensor_scalar(nmax[:, :], out[:, g, HD:HD + 1], -1.0, None, ALU.mult).then_inc(negated, 1)
                dve.wait_ge(v_in[g % 2], seen_k[g % 2])
                dve.wait_ge(exped, g + 1)
                dve.tensor_tensor(pr, v, ex[:, 0:n, None].broadcast_to([P, n, HD]), ALU.mult).then_inc(kv_read, 1)
                dve.wait_ge(kv_read, g + 1)
                dve.tensor_reduce(out[:, g, 0:HD], pr.rearrange("p k d -> p d k"), AX.X, ALU.add).then_inc(done, 1)
                dve.wait_ge(done, g + 1)

        @block.scalar
        def _(act):
            for g in range(NG):
                n = LB[g] // DIL[g] + 1
                act.wait_ge(negated, g + 1)
                act.activation(ex[:, 0:n], sc[:, 0:n], ACT.Exp, bias=nmax[:, 0:1],
                               accum_out=out[:, g, HD + 1:HD + 2]).then_inc(exped, 1)


def pooling(nc, z, state, pool_lin, pool_scale, ident_in, inv_count_in, poolT):
    PAD = 16
    W = PAD + SEQ
    EXT = PSTATE + DEC_S
    with ExitStack() as ctx:
        m = Memory(nc, ctx, "mean")
        ident = m.sb("ident", [P, P])
        u = m.sb("u", [P, 2, PW])
        st = m.sb("st", [P, PW])
        uT = m.sb("uT", [P, PG, W])
        ext = m.sb("ext", [P, PG, DEC_B, EXT])
        sums = m.sb("sums", [P, 2, W])
        esums = m.sb("esums", [P, 2, DEC_B, EXT])
        zT = m.sb("zT", [P, PG, ROWS])
        head = m.sb("head", [P, PG, PAD])
        inv = m.sb("inv", [P, PG, PAD])
        lin = m.sb("lin", [P, PG, P])
        scale = m.sb("scale", [P, PG])
        res_hi = m.sb("res_hi", [P, PG, ROWS], F32R)
        res_lo = m.sb("res_lo", [P, 2, 512], F32R)
        ps_turn = m.ps("turn", [P, 2, PG, P])
        ps_lin = m.ps("lin_ps", [P, 2, 512])
        consts_in = m.sem("consts_in")
        state_in = m.sem("state_in")
        cleared = m.sem("cleared")
        u_in = [m.sem(f"u_in{s}") for s in range(2)]
        turned = m.sem("turned")
        copied = m.sem("copied")
        own = m.sem("own")
        mixed = m.sem("mixed")
        mapped = m.sem("mapped")
        hi_done = m.sem("hi_done")
        lo_done = m.sem("lo_done")
        stored = m.sem("stored")
        lo_stored = [m.pool_sem(f"lo_stored{s}") for s in range(2)]
        block = m.block()
        chunks = [(c, min(c + 512, ROWS)) for c in range(0, ROWS, 512)]
        jobs = [(g, a, b) for g in range(PG) for a, b in chunks]

        @block.sync
        def _(sp):
            sp.dma_start(ident[:, :], ident_in).then_inc(consts_in, 16)
            sp.dma_start(inv[:, :, :], inv_count_in).then_inc(consts_in, 16)
            sp.dma_start(lin[:, :, :], pool_lin.rearrange("g c d -> c g d")).then_inc(consts_in, 16)
            sp.dma_start(scale[:, :], pool_scale.rearrange("(g d) -> d g", d=P), allow_slow_non_contiguous=True).then_inc(consts_in, 16)
            sp.dma_start(st[0:DEC_B * PSTATE, :], state.rearrange("b t c -> (b t) c")).then_inc(state_in, 16)

            def load(t, s, k):
                wait(sp, turned, t - 1)
                sp.dma_start(u[:, s, :], z["u"][rows(t), :]).then_inc(u_in[s], 16)
            by_twos(sp, TILES, load)
            for g in range(PG):
                sp.wait_ge(hi_done, len(chunks) * (g + 1))
                sp.dma_start(poolT[:, :, 0, g, :].rearrange("t p n -> p t n"), res_hi[:, g, :].bitcast(F32).rearrange("p (t n) -> p t n", n=P)).then_inc(stored, 16)
            sp.wait_ge(stored, 16 * PG)

        @block.gpsimd
        def _(pool):
            pool.memset(uT[:, :, 0:PAD], 0.0)
            pool.memset(zT[:, :, SEQ:ROWS], 0.0).then_inc(cleared, 1)
            for n, (g, a, b) in enumerate(jobs):
                pool.wait_ge(lo_done, n + 1)
                pool.dma_start(poolT[a // P:b // P, :, 1, g, :].rearrange("t p n -> p t n"),
                               res_lo[:, n % 2, 0:b - a].bitcast(F32).rearrange("p (t n) -> p t n", n=P)).then_inc(lo_stored[n % 2], 16)
            for s in range(2):
                pool.wait_ge(lo_stored[s], 16 * len(jobs) // 2)

        @block.tensor
        def _(pe):
            pe.wait_ge(consts_in, 64)

            def turn(t, s, k):
                pe.wait_ge(u_in[s], 16 * k + 16)
                wait(pe, copied, t - 1)
                for g in range(PG):
                    last = pe.transpose(ps_turn[:, s, g, :], u[:, s, g * P:(g + 1) * P], ident[:, :])
                last.then_inc(turned, 1)
            by_twos(pe, TILES, turn)
            pe.wait_ge(state_in, 16)
            pe.wait_ge(copied, TILES)
            rows_ = DEC_B * PSTATE
            for g in range(PG):
                last = pe.transpose(ps_turn[:, 1, g, 0:rows_], st[0:rows_, g * P:(g + 1) * P], ident[0:rows_, 0:rows_])
            last.then_inc(turned, 1)
            for n, (g, a, b) in enumerate(jobs):
                pe.wait_ge(mixed, g + 1)
                wait(pe, lo_done, n - 1)
                pe.matmul(ps_lin[:, n % 2, 0:b - a], lin[:, g, :], zT[:, g, a:b], start=True, stop=True).then_inc(mapped, 1)

        @block.scalar
        def _(act):
            def copy(t, s, k):
                act.wait_ge(turned, t + 1)
                act.activation(uT[:, :, bass.ds(t * P + PAD, P)], ps_turn[:, s, :, :], ACT.Copy).then_inc(copied, 1)

            copy(0, 0, 0)
            with act.Fori(0, (SEQ // P - 2) // 2) as j:
                copy(j * 2 + 1, 1, j)
                copy(j * 2 + 2, 0, j)
            copy(SEQ // P - 1, 1, 0)
            act.wait_ge(turned, TILES)
            for g in range(PG):
                last = act.activation(ext[:, g, :, PSTATE:EXT], ps_turn[:, 0, g, 0:NS].rearrange("p (b s) -> p b s", b=DEC_B), ACT.Copy)
            last.then_inc(copied, 1)
            act.wait_ge(turned, TILES + 1)
            for g in range(PG):
                last = act.activation(ext[:, g, :, 0:PSTATE], ps_turn[:, 1, g, 0:DEC_B * PSTATE].rearrange("p (b t) -> p b t", b=DEC_B), ACT.Copy)
            last.then_inc(copied, 1)
            act.wait_ge(consts_in, 64)
            for n, (g, a, b) in enumerate(jobs):
                act.wait_ge(mapped, n + 1)
                act.activation(res_hi[:, g, a:b], ps_lin[:, n % 2, 0:b - a], ACT.Copy, scale=scale[:, g:g + 1]).then_inc(hi_done, 1)

        @block.vector
        def _(dve):
            n_own = 0

            def own_step(ins):
                nonlocal n_own
                n_own += 1
                ins.then_inc(own, 1)

            dve.wait_ge(consts_in, 64)
            dve.wait_ge(cleared, 1)
            dve.wait_ge(copied, TILES + 1)
            for g in range(PG):
                if g:
                    dve.wait_ge(own, n_own)
                src, esrc = uT[:, g, :], ext[:, g, :, :]
                for level in range(g + 1):
                    d = 1 << level
                    dst, edst = sums[:, level % 2, :], esums[:, level % 2, :, :]
                    lo = 2 * d - 1
                    own_step(dve.tensor_tensor(dst[:, lo:W], src[:, lo:W], src[:, lo - d:W - d], ALU.add))
                    own_step(dve.tensor_tensor(edst[:, :, lo:EXT], esrc[:, :, lo:EXT], esrc[:, :, lo - d:EXT - d], ALU.add))
                    dve.wait_ge(own, n_own)
                    src, esrc = dst, edst
                w = 2 << g
                own_step(dve.tensor_tensor(head[:, g, :], src[:, PAD:2 * PAD], inv[:, g, :], ALU.mult))
                own_step(dve.scalar_tensor_tensor(zT[:, g, 0:SEQ], src[:, PAD:W], 1.0 / w, uT[:, g, PAD:W], ALU.mult, ALU.subtract))
                own_step(dve.scalar_tensor_tensor(zT[:, g, SEQ:SEQ + NS].rearrange("p (b s) -> p b s", b=DEC_B), esrc[:, :, PSTATE:EXT], 1.0 / w,
                                                  ext[:, g, :, PSTATE:EXT], ALU.mult, ALU.subtract))
                dve.wait_ge(own, n_own)
                dve.tensor_tensor(zT[:, g, 0:PAD], head[:, g, :], uT[:, g, PAD:2 * PAD], ALU.subtract).then_inc(mixed, 1)
            for n, (g, a, b) in enumerate(jobs):
                dve.wait_ge(hi_done, n + 1)
                if n >= 2:
                    dve.wait_ge(lo_stored[n % 2], 16 * (n // 2))
                dve.scalar_tensor_tensor(res_lo[:, n % 2, 0:b - a], ps_lin[:, n % 2, 0:b - a], scale[:, g:g + 1],
                                         res_hi[:, g, a:b].bitcast(F32), ALU.mult, ALU.subtract).then_inc(lo_done, 1)
def merge_and_route(nc, x, z, att, poolT, w_pa, w_pb, w_o, ln2, w_rg, b_rg, w_re, b_re, ident_in, h_out, xn_out, logits_out):
    NL = EG + NE
    with ExitStack() as ctx:
        m = Memory(nc, ctx, "merge")
        KA, KP = GW // P, PW // P
        KW = KA + KP + KC
        w_raw = m.sb("w_raw", [P, 2, D])
        w_hi = m.sb("w_hi", [P, KW, D], F32R)
        w_lo = m.sb("w_lo", [P, KW, D], F32R)
        w_r = m.sb("w_r", [P, KC, NL])
        bias_r = m.sb("bias_r", [P, NL])
        lnrow = m.sb("lnrow", [P, D])
        ident = m.sb("ident", [P, P])
        eps = m.sb("eps", [P, 1])
        a_in = m.sb("a_in", [P, 2, NG, HG, HD + 2])
        p_in = m.sb("p_in", [P, 2, 2, PG, P], F32R)
        gates = m.sb("gates", [P, 2, D])
        xh = m.sb("xh", [P, 2, D])
        mx = m.sb("mx", [P, HG])
        wt = m.sb("wt", [P, NG, HG])
        den = m.sb("den", [P, HG])
        a_mix = m.sb("a_mix", [P, GW])
        aT = m.sb("aT", [P, 2, KA, P], F32R)
        mix = m.sb("mix", [P, D])
        mT = m.sb("mT", [P, 2, KC, P], F32R)
        xn = m.sb("xn", [P, D])
        junk = m.sb("junk", [P, D])
        xnT = m.sb("xnT", [P, KC, P])
        ss = m.sb("ss", [P, 1])
        rms = m.sb("rms", [P, 1])
        rstd = m.sb("rstd", [P, 1])
        logits = m.sb("logits", [P, 2, NL])
        ps_turn = m.ps("turn", [P, 2, 512])
        ps_a = m.ps("a_ps", [P, 2, 512])
        ps_p = m.ps("p_ps", [P, 2, 512])
        ps_o = m.ps("o_ps", [P, 2, 512])
        consts_in = m.sem("consts_in")
        eps_set = m.sem("eps_set")
        w_in_sem = [m.sem(f"w_in{i}") for i in range(2)]
        w_hi_done = m.sem("w_hi_done")
        w_lo_done = m.sem("w_lo_done")
        a_loaded = [m.sem(f"a_loaded{s}") for s in range(2)]
        g_loaded = m.sem("g_loaded")
        x_loaded = [m.sem(f"x_loaded{s}") for s in range(2)]
        p_loaded = [m.sem(f"p_loaded{s}") for s in range(2)]
        mx_done = m.sem("mx_done")
        lowered = m.sem("lowered")
        weights = m.sem("weights")
        own = m.sem("own")
        a_mixed = m.sem("a_mixed")
        a_turned = m.sem("a_turned")
        a_hi = m.sem("a_hi")
        a_split = m.sem("a_split")
        a_product = m.sem("a_product")
        p_product = m.sem("p_product")
        gated = m.sem("gated")
        mixed = m.sem("mixed")
        m_turned = m.sem("m_turned")
        m_hi = m.sem("m_hi")
        m_split = m.sem("m_split")
        o_product = m.sem("o_product")
        h_done = m.sem("h_done")
        squared = m.sem("squared")
        rooted = m.sem("rooted")
        inverted = m.sem("inverted")
        normed = m.sem("normed")
        n_turned = m.sem("n_turned")
        n_copied = m.sem("n_copied")
        l_product = m.sem("l_product")
        l_done = m.sem("l_done")
        h_stored = [m.pool_sem(f"h_stored{s}") for s in range(2)]
        n_stored = m.pool_sem("n_stored")
        l_stored = m.pool_sem("l_stored")
        block = m.block()
        w_rows = [(w_pa, c) for c in range(KA)] + [(w_pb, c) for c in range(KP)] + [(w_o, c) for c in range(KC)]

        @block.sync
        def _(sp):
            for dst, src in ((ident[:, :], ident_in), (lnrow[:, :], ln2[None, :].partition_broadcast(P)),
                             (bias_r[:, 0:EG], b_rg[None, :].partition_broadcast(P)),
                             (bias_r[:, EG:NL], b_re[None, :].partition_broadcast(P)),
                             (w_r[:, :, 0:EG], w_rg.rearrange("(c p) n -> p c n", p=P)),
                             (w_r[:, :, EG:NL], w_re.rearrange("(c p) n -> p c n", p=P))):
                sp.dma_start(dst, src).then_inc(consts_in, 16)
            for i, (w, c) in enumerate(w_rows):
                wait(sp, w_lo_done, i - 1)
                sp.dma_start(w_raw[:, i % 2, :], w[c * P:(c + 1) * P, :]).then_inc(w_in_sem[i % 2], 16)

            def load(t, s, k):
                wait_apart(sp, a_mixed, t - 1, (consts_in, 96))
                sp.dma_start(a_in[:, s].rearrange("p g h e -> p g (h e)"), att[:, rows(t), :].rearrange("g p e -> p g e")).then_inc(a_loaded[s], 16)
                wait_apart(sp, p_product, t - 1, (consts_in, 96))
                sp.dma_start(p_in[:, s].bitcast(F32), poolT[t]).then_inc(p_loaded[s], 16)
                wait_apart(sp, normed, t - 1, (consts_in, 96))
                if not (isinstance(t, int) and t < 2):
                    wait_apart(sp, h_stored[s], 16 * k, (consts_in, 96))
                sp.dma_start(xh[:, s, :], x[rows(t), :]).then_inc(x_loaded[s], 16)
                wait_apart(sp, mixed, t, (consts_in, 96))
                sp.dma_start(gates[:, 0, :], z["ga"][rows(t), :]).then_inc(g_loaded, 16)
                sp.dma_start(gates[:, 1, :], z["gb"][rows(t), :]).then_inc(g_loaded, 16)
            by_twos(sp, TILES, load)

        @block.gpsimd
        def _(pool):
            pool.memset(eps[:, :], EPS).then_inc(eps_set, 1)

            def store(t, s, k):
                wait_apart(pool, h_done, t + 1, (eps_set, 1))
                pool.dma_start(h_out[rows(t), :], xh[:, s, :]).then_inc(h_stored[s], 16)
                wait_apart(pool, normed, t + 1, (eps_set, 1))
                pool.dma_start(xn_out[rows(t), :], xn[:, :]).then_inc(n_stored, 16)
                wait_apart(pool, l_done, t + 1, (eps_set, 1))
                pool.dma_start(logits_out[rows(t), :], logits[:, s, :]).then_inc(l_stored, 16)
            by_twos(pool, TILES, store)
            pool.wait_ge(n_stored, 16 * TILES)
            pool.wait_ge(l_stored, 16 * TILES)
            for s in range(2):
                pool.wait_ge(h_stored[s], 16 * ((TILES + 1 - s) // 2))

        @block.tensor
        def _(pe):
            def product(ps, lhs, c0, n):
                for c in range(n):
                    for i, (part, w) in enumerate(((0, w_hi), (0, w_lo), (1, w_hi))):
                        for b in range(2):
                            last = pe.matmul(ps[:, b, :], lhs(part, c), w[:, c0 + c, b * 512:(b + 1) * 512],
                                             start=(c == 0 and i == 0), stop=(c == n - 1 and i == 2))
                return last

            def turn_a(t):
                pe.wait_ge(a_mixed, t + 1)
                wait(pe, n_copied, t - 1)
                wait(pe, l_done, t - 1)
                for c in range(KA):
                    last = pe.transpose(ps_turn[:, 0, c * P:(c + 1) * P], a_mix[:, c * P:(c + 1) * P], ident[:, :])
                last.then_inc(a_turned, 1)

            def route(t):
                pe.wait_ge(normed, t + 1)
                pe.wait_ge(a_split, t + 1)
                for c in range(KC):
                    last = pe.transpose(ps_turn[:, c // 4, (c % 4) * P:(c % 4 + 1) * P], xn[:, c * P:(c + 1) * P], ident[:, :])
                last.then_inc(n_turned, 1)
                pe.wait_ge(n_copied, t + 1)
                for c in range(KC):
                    last = pe.matmul(ps_turn[:, 0, 0:NL], xnT[:, c, :], w_r[:, c, :], start=(c == 0), stop=(c == KC - 1))
                last.then_inc(l_product, 1)

            pe.wait_ge(consts_in, 96)
            pe.wait_ge(w_lo_done, KW)

            def step(t, s, k):
                turn_a(t)
                pe.wait_ge(p_loaded[s], 16 * k + 16)
                wait(pe, mixed, t)
                product(ps_p, lambda i, c: p_in[:, s, i, c, :], KA, KP).then_inc(p_product, 1)
                pe.wait_ge(a_split, t + 1)
                product(ps_a, lambda i, c: aT[:, i, c, :], 0, KA).then_inc(a_product, 1)
                if not (isinstance(t, int) and t == 0):
                    route(t - 1)
                    pe.wait_ge(l_done, t)
                pe.wait_ge(mixed, t + 1)
                for c in range(KC):
                    last = pe.transpose(ps_turn[:, c // 4, (c % 4) * P:(c % 4 + 1) * P], mix[:, c * P:(c + 1) * P], ident[:, :])
                last.then_inc(m_turned, 1)
                pe.wait_ge(m_split, t + 1)
                wait(pe, h_done, t)
                product(ps_o, lambda i, c: mT[:, i, c, :], KA + KP, KC).then_inc(o_product, 1)
            by_twos(pe, TILES, step)
            route(TILES - 1)

        @block.scalar
        def _(act):
            act.wait_ge(eps_set, 1)
            for i in range(KW):
                act.wait_ge(w_in_sem[i % 2], 16 * (i // 2 + 1))
                act.activation(w_hi[:, i, :], w_raw[:, i % 2, :], ACT.Copy).then_inc(w_hi_done, 1)

            def norm(t, s):
                act.wait_ge(h_done, t + 1)
                act.activation(junk[:, :], xh[:, s, :], ACT.Square, accum_out=ss[:, :]).then_inc(squared, 1)
                act.wait_ge(squared, t + 1)
                act.activation(rms[:, :], ss[:, :], ACT.Sqrt, bias=eps[:, 0:1], scale=1.0 / D).then_inc(rooted, 1)

            def copy_xn(t):
                act.wait_ge(n_turned, t + 1)
                act.activation(xnT[:, :, :].rearrange("p (b c) n -> p b (c n)", b=2), ps_turn[:, :, :], ACT.Copy).then_inc(n_copied, 1)

            def weigh(t):
                act.wait_ge(lowered, t + 1)
                act.activation(wt[:, :, :], wt[:, :, :], ACT.Exp).then_inc(weights, 1)

            weigh(0)

            def step(t, s, k):
                act.wait_ge(a_turned, t + 1)
                act.activation(aT[:, 0, :, :].rearrange("p c n -> p (c n)"), ps_turn[:, 0, 0:GW], ACT.Copy).then_inc(a_hi, 1)
                if not (isinstance(t, int) and t == 0):
                    copy_xn(t - 1)
                act.wait_ge(m_turned, t + 1)
                act.activation(mT[:, 0, :, :].rearrange("p (b c) n -> p b (c n)", b=2), ps_turn[:, :, :], ACT.Copy).then_inc(m_hi, 1)
                if not (isinstance(t, int) and t == TILES - 1):
                    weigh(t + 1)
                norm(t, s)
            by_twos(act, TILES, step)
            copy_xn(TILES - 1)

        @block.vector
        def _(dve):
            dve.wait_ge(consts_in, 96)
            for i in range(KW):
                dve.wait_ge(w_hi_done, i + 1)
                dve.tensor_tensor(w_lo[:, i, :], w_raw[:, i % 2, :], w_hi[:, i, :].bitcast(F32), ALU.subtract).then_inc(w_lo_done, 1)

            def combine(t, s, k):
                a = a_in[:, s]
                dve.wait_ge(a_loaded[s], 16 * k + 16)
                dve.tensor_reduce(mx[:, :], a[:, :, :, HD].rearrange("p g h -> p h g"), AX.X, ALU.max).then_inc(mx_done, 1)
                dve.wait_ge(mx_done, t + 1)
                wait(dve, own, 5 * t)
                dve.tensor_tensor(wt[:, :, :], a[:, :, :, HD], mx[:, None, :].broadcast_to([P, NG, HG]), ALU.subtract).then_inc(lowered, 1)
                dve.wait_ge(weights, t + 1)
                dve.tensor_tensor(a[:, :, :, HD + 1], a[:, :, :, HD + 1], wt[:, :, :], ALU.mult).then_inc(own, 1)
                dve.wait_ge(own, 5 * t + 1)
                dve.tensor_reduce(den[:, :], a[:, :, :, HD + 1].rearrange("p g h -> p h g"), AX.X, ALU.add).then_inc(own, 1)
                dve.wait_ge(own, 5 * t + 2)
                dve.reciprocal(den[:, :], den[:, :]).then_inc(own, 1)
                dve.wait_ge(own, 5 * t + 3)
                dve.tensor_tensor(wt[:, :, :], wt[:, :, :], den[:, None, :].broadcast_to([P, NG, HG]), ALU.mult).then_inc(own, 1)
                dve.wait_ge(own, 5 * t + 4)
                for g in range(NG):
                    last = dve.tensor_tensor(a[:, g, :, 0:HD], a[:, g, :, 0:HD], wt[:, g, :, None].broadcast_to([P, HG, HD]), ALU.mult)
                last.then_inc(own, 1)
                dve.wait_ge(own, 5 * t + 5)
                wait(dve, a_turned, t)
                dve.tensor_reduce(a_mix[:, :].rearrange("p (h d) -> p h d", d=HD), a[:, :, :, 0:HD].rearrange("p g h d -> p h d g"),
                                  AX.X, ALU.add).then_inc(a_mixed, 1)

            def split_a(t):
                dve.wait_ge(a_hi, t + 1)
                dve.tensor_tensor(aT[:, 1, :, :].rearrange("p c n -> p (c n)"), ps_turn[:, 0, 0:GW],
                                  aT[:, 0, :, :].bitcast(F32).rearrange("p c n -> p (c n)"), ALU.subtract).then_inc(a_split, 1)

            def halves(ap):
                return ap.rearrange("p (b n) -> p b n", b=2)

            combine(0, 0, 0)

            def step(t, s, k):
                split_a(t)
                dve.wait_ge(g_loaded, 32 * (t + 1))
                dve.wait_ge(p_product, t + 1)
                dve.tensor_tensor(halves(gates[:, 1, :]), halves(gates[:, 1, :]), ps_p[:, :, :], ALU.mult).then_inc(gated, 1)
                dve.wait_ge(a_product, t + 1)
                dve.tensor_tensor(halves(gates[:, 0, :]), halves(gates[:, 0, :]), ps_a[:, :, :], ALU.mult).then_inc(gated, 1)
                dve.wait_ge(gated, 2 * (t + 1))
                wait(dve, m_turned, t)
                dve.tensor_tensor(mix[:, :], gates[:, 0, :], gates[:, 1, :], ALU.add).then_inc(mixed, 1)
                if not (isinstance(t, int) and t == 0):
                    dve.wait_ge(l_product, t)
                    wait(dve, l_stored, 16 * (t - 1))
                    dve.tensor_tensor(logits[:, 1 - s, :], ps_turn[:, 0, 0:NL], bias_r[:, :], ALU.add).then_inc(l_done, 1)
                dve.wait_ge(m_hi, t + 1)
                dve.tensor_tensor(mT[:, 1, :, :].rearrange("p (b c) n -> p b (c n)", b=2), ps_turn[:, :, :],
                                  mT[:, 0, :, :].bitcast(F32).rearrange("p (b c) n -> p b (c n)", b=2), ALU.subtract).then_inc(m_split, 1)
                if not (isinstance(t, int) and t == TILES - 1):
                    combine(t + 1, 1 - s, k + 1 if s else k)
                dve.wait_ge(o_product, t + 1)
                dve.wait_ge(x_loaded[s], 16 * k + 16)
                dve.tensor_tensor(halves(xh[:, s, :]), halves(xh[:, s, :]), ps_o[:, :, :], ALU.add).then_inc(h_done, 1)
                dve.wait_ge(rooted, t + 1)
                dve.reciprocal(rstd[:, :], rms[:, :]).then_inc(inverted, 1)
                dve.wait_ge(inverted, t + 1)
                wait(dve, n_turned, t)
                if not (isinstance(t, int) and t == 0):
                    dve.wait_ge(n_stored, 16 * t)
                dve.scalar_tensor_tensor(xn[:, :], xh[:, s, :], rstd[:, 0:1], lnrow[:, :], ALU.mult, ALU.mult).then_inc(normed, 1)
            by_twos(dve, TILES, step)
            last = TILES - 1
            dve.wait_ge(l_product, TILES)
            dve.wait_ge(l_stored, 16 * (TILES - 1))
            dve.tensor_tensor(logits[:, last % 2, :], ps_turn[:, 0, 0:NL], bias_r[:, :], ALU.add).then_inc(l_done, 1)


def routing(nc, logits_in, a, slots, weight_out, counts_out, over_out):
    PADT, PADE = 16, 16
    with ExitStack() as ctx:
        m = Memory(nc, ctx, "route")
        lg = m.sb("lg", [P, TILES, EG + NE])
        ones = m.sb("ones", [P, P])
        before = m.sb("before", [P, P])
        real = m.sb("real", [P, TILES])
        first_g = m.sb("first_g", [P, EG])
        first_e = m.sb("first_e", [P, NE])
        block_no = m.sb("block_no", [P, OVER, NE])
        entry = m.sb("entry", [P, 2, TILES, SLOT], I32)
        zero = m.sb("zero", [P, BLOCKS * SLOT], I32)
        g4 = [m.sb(f"g4_{i}", [P, TILES, EG]) for i in range(3)]
        t1 = [m.sb(f"t1_{i}", [P, TILES]) for i in range(8)]
        el = m.sb("el", [P, TILES, NE])
        e1 = m.sb("e1", [P, TILES, NE])
        e2 = m.sb("e2", [P, TILES, NE])
        tmp = m.sb("tmp", [P, TILES, NE])
        counts = m.sb("counts", [P, 2, PADT + TILES, NE])
        tile_count = m.sb("tile_count", [P, TILES, NE])
        ends = m.sb("ends", [P, 2, PADE + NE])
        nblk = m.sb("nblk", [P, NE])
        nblk_i = m.sb("nblk_i", [P, NE], I32)
        start = m.sb("start", [P, NE])
        where = m.sb("where", [P, TILES, NE])
        dest_f = m.sb("dest_f", [P, TILES, 2])
        dest = m.sb("dest", [P, 2, TILES], I32)
        weight = m.sb("weight", [P, TILES, 2])
        owner = m.sb("owner", [P, OVER + 1])
        owner_i = m.sb("owner_i", [P, OVER + 1], I32)
        total_i = m.sb("total_i", [P, 2, NE], I32)
        second = m.sb("second", [P, 2, PADE + NE])
        beyond = m.sb("beyond", [P, TILES, NE])
        base = m.sb("base", [P, NE])
        NT = TILES * NE
        HALF = (TILES + 1) // 2
        ps_sum = m.ps("sum_ps", [P, 2, 512])
        ps_rank = m.ps("rank_ps", [P, 2, 512])
        loaded = m.sem("loaded")
        cleared = m.sem("cleared")
        own = m.sem("own")
        lowered = m.sem("lowered")
        exped = m.sem("exped")
        chosen = m.sem("chosen")
        counted = m.sem("counted")
        placed = m.sem("placed")
        zeroed = m.pool_sem("zeroed")
        scattered = m.pool_sem("scattered")
        stored = m.sem("stored")
        block = m.block()

        @block.sync
        def _(sp):
            for dst, src in ((lg[:, :, :], logits_in.rearrange("(t p) n -> p t n", p=P)), (ones[:, :], a["ones"]),
                             (before[:, :], a["before"]), (real[:, :], a["real"]), (first_g[:, :], a["first_group"]),
                             (first_e[:, :], a["first_expert"]), (block_no[:, :, :], a["block_no"]), (base[:, :], a["base"]), (entry[:, :, :, :], a["entry"])):
                sp.dma_start(dst, src).then_inc(loaded, 16)
            sp.wait_ge(placed, 1)
            sp.dma_start(weight_out.rearrange("(t p) k -> p t k", p=P), weight[:, :, :], allow_slow_non_contiguous=True).then_inc(stored, 16)
            sp.dma_start(over_out, owner_i[0:1, :]).then_inc(stored, 16)
            sp.dma_start(counts_out, total_i[0:1, :, :].rearrange("p a e -> p (a e)")).then_inc(stored, 16)
            sp.wait_ge(stored, 48)

        @block.gpsimd
        def _(pool):
            pool.memset(zero[:, :], 0).then_inc(cleared, 1)
            pool.memset(counts[:, :, 0:PADT, :], 0.0)
            pool.memset(second[:, :, 0:PADE], 0.0)
            pool.memset(ends[:, :, 0:PADE], 0.0).then_inc(cleared, 1)
            pool.wait_ge(cleared, 2)
            pool.dma_start(slots.rearrange("(p b) e -> p (b e)", p=P), zero[:, :]).then_inc(zeroed, 16)
            pool.wait_ge(zeroed, 16)
            pool.wait_ge(placed, 1)
            pool.wait_ge(loaded, 144)
            for t in range(TILES):
                n = P if t < TILES - 1 else NS
                for k in range(2):
                    pool.indirect_dma_start(out=slots, out_offset=bass.IndirectOffsetOnAxis(ap=dest[0:n, k, t:t + 1], axis=0),
                                            in_=entry[0:n, k, t, :], in_offset=None).then_inc(scattered, 16)
            pool.wait_ge(scattered, 16 * 2 * TILES)

        @block.scalar
        def _(act):
            act.wait_ge(lowered, 1)
            act.activation(g4[1][:, :, :], g4[1][:, :, :], ACT.Exp).then_inc(exped, 1)
            act.wait_ge(lowered, 2)
            act.activation(t1[5][:, :], t1[5][:, :], ACT.Exp).then_inc(exped, 1)

        @block.tensor
        def _(pe):
            pe.wait_ge(loaded, 144)
            pe.wait_ge(chosen, 1)
            for i, (a0, b0) in enumerate(((0, HALF), (HALF, TILES))):
                flat = tmp[:, a0:b0, :].rearrange("p t e -> p (t e)")
                w = (b0 - a0) * NE
                pe.matmul(ps_sum[:, i, 0:w], ones[:, :], flat, start=True, stop=True)
                last = pe.matmul(ps_rank[:, i, 0:w], before[:, :], flat, start=True, stop=True)
            last.then_inc(counted, 1)

        @block.vector
        def _(dve):
            n_own = 0

            def then(ins):
                nonlocal n_own
                n_own += 1
                ins.then_inc(own, 1)
                dve.wait_ge(own, n_own)

            def over(ap, n):
                return ap[:, :, None].broadcast_to([P, TILES, n])

            def table(ap, n):
                return ap[:, None, :].broadcast_to([P, TILES, n])

            def pick_first(out, values, best, order, n, scratch):
                then(dve.tensor_tensor(out, values, over(best, n), ALU.is_equal))
                then(dve.tensor_tensor(out, out, table(order, n), ALU.mult))
                then(dve.tensor_reduce(scratch, out, AX.X, ALU.max))
                then(dve.tensor_tensor(out, out, over(scratch, n), ALU.is_equal))

            dve.wait_ge(loaded, 144)
            dve.wait_ge(cleared, 2)
            gl = lg[:, :, 0:EG]
            then(dve.tensor_reduce(t1[0][:, :], gl, AX.X, ALU.max))
            dve.tensor_tensor(g4[1][:, :, :], gl, over(t1[0][:, :], EG), ALU.subtract).then_inc(lowered, 1)
            pick_first(g4[0][:, :, :], gl, t1[0][:, :], first_g[:, :], EG, t1[1][:, :])
            then(dve.tensor_scalar(g4[2][:, :, :], g4[0][:, :, :], 1.0, 1e30, ALU.subtract, ALU.mult))
            for g in range(EG):
                here = slice(g * EPG, (g + 1) * EPG)
                then(dve.tensor_tensor(el[:, :, here], lg[:, :, EG + g * EPG:EG + (g + 1) * EPG], over(g4[0][:, :, g], EPG), ALU.mult))
                then(dve.tensor_tensor(el[:, :, here], el[:, :, here], over(g4[2][:, :, g], EPG), ALU.add))
            then(dve.tensor_reduce(t1[2][:, :], el[:, :, :], AX.X, ALU.max))
            pick_first(e1[:, :, :], el[:, :, :], t1[2][:, :], first_e[:, :], NE, t1[1][:, :])
            then(dve.scalar_tensor_tensor(tmp[:, :, :], e1[:, :, :], -3e38, el[:, :, :], ALU.mult, ALU.add))
            then(dve.tensor_reduce(t1[3][:, :], tmp[:, :, :], AX.X, ALU.max))
            pick_first(e2[:, :, :], tmp[:, :, :], t1[3][:, :], first_e[:, :], NE, t1[1][:, :])
            dve.tensor_tensor(t1[5][:, :], t1[3][:, :], t1[2][:, :], ALU.subtract).then_inc(lowered, 1)
            then(dve.tensor_tensor(e1[:, :, :], e1[:, :, :], over(real[:, :], NE), ALU.mult))
            then(dve.tensor_tensor(e2[:, :, :], e2[:, :, :], over(real[:, :], NE), ALU.mult))
            dve.tensor_tensor(tmp[:, :, :], e1[:, :, :], e2[:, :, :], ALU.add).then_inc(chosen, 1)
            dve.wait_ge(exped, 2)
            then(dve.tensor_reduce(t1[4][:, :], g4[1][:, :, :], AX.X, ALU.add))
            then(dve.scalar_tensor_tensor(t1[6][:, :], t1[5][:, :], 1.0, t1[4][:, :], ALU.add, ALU.mult))
            then(dve.reciprocal(weight[:, :, 0], t1[6][:, :]))
            then(dve.tensor_tensor(weight[:, :, 1], weight[:, :, 0], t1[5][:, :], ALU.mult))
            dve.wait_ge(counted, 1)
            for i, (a0, b0) in enumerate(((0, HALF), (HALF, TILES))):
                w = (b0 - a0) * NE
                then(dve.tensor_copy(tile_count[:, a0:b0, :], ps_sum[:, i, 0:w].rearrange("p (t e) -> p t e", e=NE)))
            then(dve.tensor_copy(counts[:, 0, PADT:, :], tile_count[:, :, :]))
            cur = 0
            for d in (1, 2, 4, 8, 16):
                then(dve.tensor_tensor(counts[:, 1 - cur, PADT:, :], counts[:, cur, PADT:, :], counts[:, cur, PADT - d:PADT + TILES - d, :], ALU.add))
                cur = 1 - cur
            total = counts[:, cur, PADT + TILES - 1, :]
            then(dve.tensor_copy(total_i[:, 0, :], total))
            then(dve.tensor_scalar(second[:, 0, PADE:], total, float(P), None, ALU.is_gt))
            sc = 0
            for d in (1, 2, 4, 8, 16):
                then(dve.tensor_tensor(second[:, 1 - sc, PADE:], second[:, sc, PADE:], second[:, sc, PADE - d:PADE + NE - d], ALU.add))
                sc = 1 - sc
            then(dve.tensor_copy(total_i[:, 1, :], second[:, sc, PADE:]))
            then(dve.tensor_scalar(nblk[:, :], total, float(P - 1), None, ALU.add))
            then(dve.tensor_copy(nblk_i[:, :], nblk[:, :]))
            then(dve.tensor_scalar(nblk_i[:, :], nblk_i[:, :], 7, None, ALU.logical_shift_right))
            then(dve.tensor_copy(nblk[:, :], nblk_i[:, :]))
            then(dve.tensor_scalar(nblk[:, :], nblk[:, :], 2.0, 0.0, ALU.subtract, ALU.max))
            then(dve.tensor_copy(ends[:, 0, PADE:], nblk[:, :]))
            ec = 0
            for d in (1, 2, 4, 8, 16):
                then(dve.tensor_tensor(ends[:, 1 - ec, PADE:], ends[:, ec, PADE:], ends[:, ec, PADE - d:PADE + NE - d], ALU.add))
                ec = 1 - ec
            then(dve.tensor_tensor(start[:, :], ends[:, ec, PADE:], nblk[:, :], ALU.subtract))
            then(dve.tensor_tensor(where[:, :, :], counts[:, cur, PADT:, :], tile_count[:, :, :], ALU.subtract))
            for i, (a0, b0) in enumerate(((0, HALF), (HALF, TILES))):
                w = (b0 - a0) * NE
                then(dve.tensor_tensor(where[:, a0:b0, :], where[:, a0:b0, :], ps_rank[:, i, 0:w].rearrange("p (t e) -> p t e", e=NE), ALU.add))
            then(dve.tensor_scalar(beyond[:, :, :], where[:, :, :], float(2 * P), None, ALU.is_ge))
            then(dve.tensor_tensor(where[:, :, :], where[:, :, :], table(base[:, :], NE), ALU.add))
            then(dve.tensor_scalar(start[:, :], start[:, :], float(P), float((NE - 1) * 2 * P), ALU.mult, ALU.add))
            then(dve.tensor_tensor(start[:, :], start[:, :], base[:, :], ALU.subtract))
            then(dve.tensor_tensor(beyond[:, :, :], beyond[:, :, :], table(start[:, :], NE), ALU.mult))
            then(dve.tensor_tensor(where[:, :, :], where[:, :, :], beyond[:, :, :], ALU.add))
            for k, e in enumerate((e1, e2)):
                then(dve.tensor_tensor(tmp[:, :, :], where[:, :, :], e[:, :, :], ALU.mult))
                then(dve.tensor_reduce(dest_f[:, :, k], tmp[:, :, :], AX.X, ALU.add))
                then(dve.tensor_copy(dest[:, k, :], dest_f[:, :, k]))
            last_e = ends[:, ec, PADE:][:, None, :].broadcast_to([P, OVER, NE])
            then(dve.tensor_tensor(block_no[:, :, :], last_e, block_no[:, :, :], ALU.is_le))
            then(dve.tensor_reduce(owner[:, 1:], block_no[:, :, :], AX.X, ALU.add))
            then(dve.tensor_scalar(owner[:, 1:], owner[:, 1:], float(NE - 1), None, ALU.min))
            then(dve.tensor_copy(owner[:, 0:1], ends[:, ec, PADE + NE - 1:PADE + NE]))
            dve.tensor_copy(owner_i[:, :], owner[:, :]).then_inc(placed, 1)


def experts(nc, xn, slots, counts_in, w_gate, w_up, w_down, ident_in, y_tok):
    U = 12
    with ExitStack() as ctx:
        m = Memory(nc, ctx, "moe")
        ident = m.sb("ident", [P, P])
        counts = m.sb("counts", [1, 2 * NE], I32)
        raw_gu = m.sb("raw_gu", [P, KC, 2, FE])
        raw_d = m.sb("raw_d", [P, FC, D])
        gu_hi = m.sb("gu_hi", [P, KC, 2, 2, FE // 2], F32R)
        gu_lo = m.sb("gu_lo", [P, KC, 2, 2, FE // 2], F32R)
        d_hi = m.sb("d_hi", [P, FC, D], F32R)
        d_lo = m.sb("d_lo", [P, FC, D], F32R)
        lists = m.sb("lists", [P, 2 * NE, SLOT], I32)
        rows_in = m.sb("rows_in", [P, 2, 2], I32)
        rows_out = m.sb("rows_out", [P, 2, 2], I32)
        ps_turn = m.ps("turn", [P, 2, 512])
        ps_gu = m.ps("gu", [P, 2, 2, FE // 2])
        ps_y = m.ps("y_ps", [P, 2, 512])
        ps_h = m.ps("h_ps", [P, 2, 512])
        consts_in = m.sem("consts_in")
        raw_in = [m.sem(f"raw_in{i}") for i in range(4)]
        w_hi = m.sem("w_hi")
        w_lo = m.sem("w_lo")
        passed = m.sem("passed")
        lists_in = m.sem("lists_in")
        picked = m.sem("picked")

        class Kind:

            def __init__(self, f, number):
                self.number = number
                self.xg = m.sb(f"xg_{f}", [P, D])
                self.xT = m.sb(f"xT_{f}", [P, 2, KC, P], F32R)
                self.sig = m.sb(f"sig_{f}", [P, 2, FE // 2])
                self.hid = m.sb(f"hid_{f}", [P, 2, FE // 2])
                self.hT = m.sb(f"hT_{f}", [P, 2, FC, P], F32R)
                self.y = m.sb(f"y_{f}", [P, D])
                self.x_in = m.pool_sem(f"x_in_{f}")
                self.x_turned = m.sem(f"x_turned_{f}")
                self.x_hi = m.sem(f"x_hi_{f}")
                self.x_lo = m.sem(f"x_lo_{f}")
                self.used = m.sem(f"used_{f}")
                self.sigged = m.sem(f"sigged_{f}")
                self.gated = m.sem(f"gated_{f}")
                self.hidden = m.sem(f"hidden_{f}")
                self.h_turned = m.sem(f"h_turned_{f}")
                self.h_hi = m.sem(f"h_hi_{f}")
                self.h_lo = m.sem(f"h_lo_{f}")
                self.y_copied = m.sem(f"y_copied_{f}")
                self.stored = m.pool_sem(f"stored_{f}")

        X, M = Kind("x", 1), Kind("m", 0)
        X.y_free = m.sem("y_free_x")
        block = m.block()

        def loop(eng, body):
            body(0, 0, 0)
            body(1, 1, 0)
            with eng.Fori(1, NE // 2 - 1) as j:
                body(j * 2, 0, j)
                body(j * 2 + 1, 1, j)
            body(NE - 2, 0, NE // 2 - 1)
            body(NE - 1, 1, NE // 2 - 1)

        def x_blocks(eng, e):
            return eng.value_load(counts[0:1, bass.ds(e + NE, 1)], min_val=1, max_val=NE)

        def is_last(e):
            return isinstance(e, int) and e == NE - 1

        def if_x(eng, e, do, otherwise):
            count = eng.value_load(counts[0:1, bass.ds(e, 1)], min_val=0, max_val=SEQ + NS)
            with eng.If(count > P):
                do()
            with eng.Else():
                otherwise()

        def x_then_m(eng, run_x, skip_x, run_m):
            def one(e, s, k):
                if_x(eng, e, lambda: run_x(e), lambda: skip_x(e))
                run_m(e)
            loop(eng, one)

        @block.sync
        def _(sp):
            sp.dma_start(ident[:, :], ident_in).then_inc(consts_in, 16)
            sp.dma_start(counts[:, :], counts_in).then_inc(consts_in, 16)
            sp.dma_start(lists[:, :, :], slots[0:2 * NE * P, :].rearrange("(b p) w -> p b w", p=P)).then_inc(lists_in, 16)

            def load(e, s, k):
                for i in range(2):
                    wait(sp, w_lo, U * e - U + 6 + 2 * i)
                    for b, w in enumerate((w_gate, w_up)):
                        src = w[bass.ds(e, 1), i * 512:(i + 1) * 512, :].rearrange("o (c p) n -> p (o c) n", p=P)
                        sp.dma_start(raw_gu[:, 4 * i:4 * i + 4, b, :], src).then_inc(raw_in[i], 16)
                for i in range(2):
                    wait(sp, w_lo, U * e - U + 10 + 2 * i)
                    src = w_down[bass.ds(e, 1), i * 256:(i + 1) * 256, :].rearrange("o (c p) n -> p (o c) n", p=P)
                    sp.dma_start(raw_d[:, 2 * i:2 * i + 2, :], src).then_inc(raw_in[2 + i], 16)
            loop(sp, load)

        @block.gpsimd
        def _(pool):
            def has_x(e):
                return pool.value_load(counts[0:1, bass.ds(e, 1)], min_val=0, max_val=SEQ + NS) > P

            def pick(to, e, s, word, n):
                first = e * 2
                pool.tensor_copy(to[:, s, :], lists[:, bass.ds(first, 2), word]).then_inc(picked, 1)
                pool.wait_ge(picked, n)

            def gather(B, s):
                pool.sem_inc(passed, 1)
                pool.indirect_dma_start(out=B.xg[:, :], out_offset=None, in_=xn,
                                        in_offset=bass.IndirectOffsetOnAxis(ap=rows_in[:, s, B.number:B.number + 1], axis=0)).then_inc(B.x_in, 16)

            def scatter(B, e, s):
                pool.wait_ge(B.y_copied, e + 1)
                pool.sem_inc(passed, 1)
                pool.indirect_dma_start(out=y_tok, out_offset=bass.IndirectOffsetOnAxis(ap=rows_out[:, s, B.number:B.number + 1], axis=0),
                                        in_=B.y[:, :], in_offset=None).then_inc(B.stored, 16)

            def step(e, s, k):
                this_has_x = has_x(e)
                if not is_last(e):
                    next_has_x = has_x(e + 1)
                    pool.wait_ge(M.x_turned, e + 1)
                    wait(pool, X.x_turned, e)
                    pick(rows_in, e + 1, 1 - s, 0, e * 2 + 2)
                    gather(M, 1 - s)
                    pool.wait_ge(X.x_turned, e + 1)
                    pool.sem_inc(passed, 1)
                    with pool.If(next_has_x):
                        gather(X, 1 - s)
                wait(pool, M.stored, 16 * e)
                pick(rows_out, e, s, 1, e * 2 + 3 - is_last(e))
                pool.sem_inc(passed, 1)
                with pool.If(this_has_x):
                    scatter(X, e, s)
                    pool.wait_ge(X.stored, 16 * x_blocks(pool, e))
                pool.sem_inc(X.y_free, 1)
                scatter(M, e, s)

            pool.wait_ge(consts_in, 32)
            pool.wait_ge(lists_in, 16)
            pick(rows_in, 0, 0, 0, 1)
            gather(M, 0)
            with pool.If(has_x(0)):
                gather(X, 0)
            loop(pool, step)
            pool.wait_ge(M.stored, 16 * NE)

        def unit(i):
            if i < 8:
                half, c = i // 4, 2 * (i % 4)
                cs, cols = slice(c, c + 2), slice(half * FE // 2, (half + 1) * FE // 2)
                return gu_hi[:, cs, half, :, :], gu_lo[:, cs, half, :, :], raw_gu[:, cs, :, cols], (c // 4, 32)
            c = i - 8
            return d_hi[:, c, :], d_lo[:, c, :], raw_d[:, c, :], (2 + c // 2, 16)

        @block.tensor
        def _(pe):
            def turn_x(B, e, other, others):
                pe.wait_ge(B.x_in, 16 * (x_blocks(pe, e) if B is X else e + 1))
                wait(pe, other.x_lo, others)
                for c in range(KC):
                    last = pe.transpose(ps_turn[:, c // 4, (c % 4) * P:(c % 4 + 1) * P], B.xg[:, c * P:(c + 1) * P], ident[:, :])
                last.then_inc(B.x_turned, 1)

            def gate_up(B, e, i):
                half = i // 4
                wait(pe, w_lo, U * e + i + 1)
                for c in (2 * (i % 4), 2 * (i % 4) + 1):
                    for n, (part, w) in enumerate(((0, gu_hi), (0, gu_lo), (1, gu_hi))):
                        last = pe.matmul(ps_gu[:, half, :, :].rearrange("p a n -> p (a n)"), B.xT[:, part, c, :],
                                         w[:, c, half, :, :].rearrange("p a n -> p (a n)"),
                                         start=(c == 0 and n == 0), stop=(c == KC - 1 and n == 2))
                last.then_inc(B.used, 1)

            def turn_h(B, e, half, other, others):
                pe.wait_ge(B.hidden, 2 * e + half + 1)
                wait(pe, other.h_lo, 2 * others - 1 + half)
                for c in range(2):
                    last = pe.transpose(ps_h[:, half, c * P:(c + 1) * P], B.hid[:, half, c * P:(c + 1) * P], ident[:, :])
                last.then_inc(B.h_turned, 1)

            def down(B, e, i, other, others):
                c = i - 8
                wait(pe, w_lo, U * e + i + 1)
                if c == 0:
                    wait(pe, other.y_copied, others)
                if c % 2 == 0:
                    pe.wait_ge(B.h_lo, 2 * e + c // 2 + 1)
                for n, (part, w) in enumerate(((0, d_hi), (0, d_lo), (1, d_hi))):
                    for b in range(2):
                        last = pe.matmul(ps_y[:, b, :], B.hT[:, part, c, :], w[:, c, b * 512:(b + 1) * 512],
                                         start=(c == 0 and n == 0), stop=(c == FC - 1 and n == 2))
                last.then_inc(B.used, 1)

            def run(B, e, other, others, turn_next):
                pe.wait_ge(B.x_lo, e + 1)
                wait(pe, other.hidden, 2 * others - 1)
                for i in range(4):
                    gate_up(B, e, i)
                wait(pe, other.hidden, 2 * others)
                gate_up(B, e, 4)
                gate_up(B, e, 5)
                turn_h(B, e, 0, other, others)
                gate_up(B, e, 6)
                gate_up(B, e, 7)
                if turn_next:
                    turn_x(M, e + 1, X, e + 1)
                down(B, e, 8, other, others)
                turn_h(B, e, 1, other, others)
                down(B, e, 9, other, others)
                if turn_next:
                    if_x(pe, e + 1, lambda: turn_x(X, e + 1, M, e + 2), lambda: pe.sem_inc(X.x_turned, 1))
                down(B, e, 10, other, others)
                down(B, e, 11, other, others)

            def run_x(e):
                run(X, e, M, e, False)

            def skip_x(e):
                pe.sem_inc(X.used, U)
                pe.sem_inc(X.h_turned, 2)

            def run_m(e):
                run(M, e, X, e + 1, not is_last(e))

            pe.wait_ge(consts_in, 32)
            turn_x(M, 0, X, 0)
            if_x(pe, 0, lambda: turn_x(X, 0, M, 1), lambda: pe.sem_inc(X.x_turned, 1))
            x_then_m(pe, run_x, skip_x, run_m)

        @block.scalar
        def _(act):
            def split_hi(e, i):
                hi, _, raw, (part, n) = unit(i)
                act.wait_ge(raw_in[part], n * (e + 1))
                wait(act, M.used, U * (e - 1) + i + 1)
                act.activation(hi, raw, ACT.Copy).then_inc(w_hi, 1)

            def x_hi(B, e):
                act.wait_ge(B.x_turned, e + 1)
                wait(act, B.used, U * (e - 1) + 8)
                act.activation(B.xT[:, 0].rearrange("p (b c) n -> p b (c n)", b=2), ps_turn[:, :, :], ACT.Copy).then_inc(B.x_hi, 1)

            def sigmoid(B, e, half):
                act.wait_ge(B.used, U * e + 4 * half + 4)
                wait(act, B.hidden, 2 * e - 1 + half)
                act.activation(B.sig[:, half, :], ps_gu[:, half, 0, :], ACT.Sigmoid).then_inc(B.sigged, 1)

            def h_hi(B, e, half):
                act.wait_ge(B.h_turned, 2 * e + half + 1)
                wait(act, B.used, U * e)
                act.activation(B.hT[:, 0, 2 * half:2 * half + 2, :].rearrange("p c n -> p (c n)"), ps_h[:, half, 0:2 * P],
                               ACT.Copy).then_inc(B.h_hi, 1)

            def store_y(B, e):
                act.wait_ge(B.used, U * e + U)
                if B is X:
                    wait(act, X.y_free, e)
                else:
                    wait(act, M.stored, 16 * e)
                act.activation(B.y[:, :].rearrange("p (b n) -> p b n", b=2), ps_y[:, :, :], ACT.Copy).then_inc(B.y_copied, 1)

            def last_units(e):
                split_hi(e, 10)
                split_hi(e, 11)

            def run_x(e):
                last_units(e)
                sigmoid(X, e, 0)
                h_hi(X, e, 0)
                sigmoid(X, e, 1)
                h_hi(X, e, 1)
                store_y(X, e)

            def skip_x(e):
                act.sem_inc(X.sigged, 2)
                act.sem_inc(X.h_hi, 2)
                act.sem_inc(X.y_copied, 1)
                last_units(e)

            def run_m(e):
                def split(*units):
                    if not is_last(e):
                        for i in units:
                            split_hi(e + 1, i)
                split(0, 1, 2)
                sigmoid(M, e, 0)
                split(3, 4)
                h_hi(M, e, 0)
                split(5)
                sigmoid(M, e, 1)
                if not is_last(e):
                    x_hi(M, e + 1)
                h_hi(M, e, 1)
                split(6, 7)
                if not is_last(e):
                    if_x(act, e + 1, lambda: x_hi(X, e + 1), lambda: act.sem_inc(X.x_hi, 1))
                split(8, 9)
                store_y(M, e)

            act.wait_ge(consts_in, 32)
            for i in range(10):
                split_hi(0, i)
                if i == 4:
                    x_hi(M, 0)
                    if_x(act, 0, lambda: x_hi(X, 0), lambda: act.sem_inc(X.x_hi, 1))
            x_then_m(act, run_x, skip_x, run_m)

        @block.vector
        def _(dve):
            def split_lo(e, i):
                hi, lo, raw, _ = unit(i)
                dve.wait_ge(w_hi, U * e + i + 1)
                dve.tensor_tensor(lo, raw, hi.bitcast(F32), ALU.subtract).then_inc(w_lo, 1)

            def x_lo(B, e):
                dve.wait_ge(B.x_hi, e + 1)
                dve.tensor_tensor(B.xT[:, 1].rearrange("p (b c) n -> p b (c n)", b=2), ps_turn[:, :, :],
                                  B.xT[:, 0].bitcast(F32).rearrange("p (b c) n -> p b (c n)", b=2), ALU.subtract).then_inc(B.x_lo, 1)

            def hidden(B, e, half):
                dve.wait_ge(B.sigged, 2 * e + half + 1)
                wait(dve, B.h_turned, 2 * e - 1 + half)
                dve.tensor_tensor(B.hid[:, half, :], B.sig[:, half, :], ps_gu[:, half, 0, :], ALU.mult).then_inc(B.gated, 1)
                dve.wait_ge(B.gated, 2 * e + half + 1)
                dve.tensor_tensor(B.hid[:, half, :], B.hid[:, half, :], ps_gu[:, half, 1, :], ALU.mult).then_inc(B.hidden, 1)

            def h_lo(B, e, half):
                dve.wait_ge(B.h_hi, 2 * e + half + 1)
                part = slice(2 * half, 2 * half + 2)
                dve.tensor_tensor(B.hT[:, 1, part, :].rearrange("p c n -> p (c n)"), ps_h[:, half, 0:2 * P],
                                  B.hT[:, 0, part, :].bitcast(F32).rearrange("p c n -> p (c n)"), ALU.subtract).then_inc(B.h_lo, 1)

            def last_units(e):
                split_lo(e, 10)
                split_lo(e, 11)

            def run_x(e):
                last_units(e)
                hidden(X, e, 0)
                h_lo(X, e, 0)
                hidden(X, e, 1)
                h_lo(X, e, 1)

            def skip_x(e):
                dve.sem_inc(X.gated, 2)
                dve.sem_inc(X.hidden, 2)
                dve.sem_inc(X.h_lo, 2)
                last_units(e)

            def run_m(e):
                def split(*units):
                    if not is_last(e):
                        for i in units:
                            split_lo(e + 1, i)
                split(0, 1, 2)
                hidden(M, e, 0)
                split(3, 4)
                h_lo(M, e, 0)
                split(5)
                hidden(M, e, 1)
                if not is_last(e):
                    x_lo(M, e + 1)
                h_lo(M, e, 1)
                split(6, 7)
                if not is_last(e):
                    if_x(dve, e + 1, lambda: x_lo(X, e + 1), lambda: dve.sem_inc(X.x_lo, 1))
                split(8, 9)

            dve.wait_ge(consts_in, 32)
            for i in range(10):
                split_lo(0, i)
                if i == 4:
                    x_lo(M, 0)
                    if_x(dve, 0, lambda: x_lo(X, 0), lambda: dve.sem_inc(X.x_lo, 1))
            x_then_m(dve, run_x, skip_x, run_m)


def expert_overflow(nc, xn, slots, over_in, w_gate, w_up, w_down, ident_in, y_tok):
    with ExitStack() as ctx:
        m = Memory(nc, ctx, "over")
        ident = m.sb("ident", [P, P])
        over = m.sb("over", [1, OVER + 1], I32)
        wg = m.sb("wg", [P, KC, FE])
        wu = m.sb("wu", [P, KC, FE])
        wd = m.sb("wd", [P, FC, D])
        idx = m.sb("idx", [P, 2, SLOT], I32)
        xg = m.sb("xg", [P, D])
        xgT = m.sb("xgT", [P, KC, P])
        hid = m.sb("hid", [P, 2, FE])
        hidT = m.sb("hidT", [P, FC, P])
        y = m.sb("y", [P, D])
        ps_turn = m.ps("turn", [P, 2, 512])
        ps_gu = m.ps("gu", [P, 2, 512])
        ps_y = m.ps("y_ps", [P, 2, 512])
        consts_in = m.sem("consts_in")
        fresh = m.sem("fresh")
        w_in_sem = m.sem("w_in")
        idx_in = [m.pool_sem(f"idx_in{i}") for i in range(2)]
        x_in = m.pool_sem("x_in")
        passed = m.sem("passed")
        x_turned = m.sem("x_turned")
        x_copied = m.sem("x_copied")
        gu_done = m.sem("gu_done")
        sigged = m.sem("sigged")
        gated = m.sem("gated")
        hidden = m.sem("hidden")
        h_turned = m.sem("h_turned")
        h_copied = m.sem("h_copied")
        y_done = m.sem("y_done")
        y_copied = m.sem("y_copied")
        stored = m.pool_sem("stored")
        block = m.block()

        def each(eng, body):
            eng.wait_ge(consts_in, 32)
            n = eng.value_load(over[0:1, 0:1], min_val=0, max_val=OVER)
            with eng.If(n > 0):
                with eng.Fori(0, OVER) as j:
                    body(j)
            with eng.Else():
                eng.wait_ge(consts_in, 32)

        @block.sync
        def _(sp):
            sp.dma_start(ident[:, :], ident_in).then_inc(consts_in, 16)
            sp.dma_start(over[:, :], over_in).then_inc(consts_in, 16)

            def load(j):
                e = sp.value_load(over[0:1, bass.ds(j + 1, 1)], min_val=0, max_val=NE - 1)
                wait_apart(sp, fresh, j + 1, (consts_in, 32))
                for dst, w in ((wg, w_gate), (wu, w_up), (wd, w_down)):
                    sp.dma_start(dst[:, :, :], w[bass.ds(e, 1)].rearrange("o (c p) n -> p (o c) n", p=P)).then_inc(w_in_sem, 16)
            each(sp, load)

        @block.gpsimd
        def _(pool):
            first = NE * 2 * P
            pool.dma_start(idx[:, 0, :], slots[first:first + P, :]).then_inc(idx_in[0], 16)
            pool.wait_ge(consts_in, 32)
            n = pool.value_load(over[0:1, 0:1], min_val=0, max_val=OVER)
            with pool.If(n > 0):
                with pool.Fori(0, OVER // 2) as k:
                    for half in range(2):
                        j = k * 2 + half
                        wait_apart(pool, idx_in[half], 16 * k + 16, (consts_in, 32))
                        pool.dma_start(idx[:, 1 - half, :], slots[bass.ds(j * P + (first + P), P), :]).then_inc(idx_in[1 - half], 16)
                        pool.indirect_dma_start(out=xg[:, :], out_offset=None, in_=xn,
                                                in_offset=bass.IndirectOffsetOnAxis(ap=idx[:, half, 0:1], axis=0)).then_inc(x_in, 16)
                        pool.wait_ge(y_copied, j + 1)
                        pool.sem_inc(passed, 1)
                        pool.indirect_dma_start(out=y_tok, out_offset=bass.IndirectOffsetOnAxis(ap=idx[:, half, 1:2], axis=0),
                                                in_=y[:, :], in_offset=None).then_inc(stored, 16)
                        pool.wait_ge(stored, 16 * j + 16)
                pool.wait_ge(idx_in[0], 16 * (OVER // 2) + 16)
            with pool.Else():
                pool.wait_ge(idx_in[0], 16)

        @block.tensor
        def _(pe):
            def step(j):
                pe.wait_ge(x_in, 16 * j + 16)
                for c in range(KC):
                    last = pe.transpose(ps_turn[:, c // 4, (c % 4) * P:(c % 4 + 1) * P], xg[:, c * P:(c + 1) * P], ident[:, :])
                last.then_inc(x_turned, 1)
                pe.wait_ge(x_copied, j + 1)
                pe.wait_ge(w_in_sem, 48 * j + 48)
                for c in range(KC):
                    for b, w in enumerate((wg, wu)):
                        last = pe.matmul(ps_gu[:, b, :], xgT[:, c, :], w[:, c, :], start=(c == 0), stop=(c == KC - 1))
                last.then_inc(gu_done, 1)
                pe.wait_ge(hidden, j + 1)
                for c in range(FC):
                    last = pe.transpose(ps_turn[:, 0, c * P:(c + 1) * P], hid[:, 1, c * P:(c + 1) * P], ident[:, :])
                last.then_inc(h_turned, 1)
                pe.wait_ge(h_copied, j + 1)
                for c in range(FC):
                    for b in range(2):
                        last = pe.matmul(ps_y[:, b, :], hidT[:, c, :], wd[:, c, b * 512:(b + 1) * 512], start=(c == 0), stop=(c == FC - 1))
                last.then_inc(y_done, 1)
            each(pe, step)

        @block.scalar
        def _(act):
            act.sem_inc(fresh, 1)

            def step(j):
                act.wait_ge(x_turned, j + 1)
                act.activation(xgT[:, :, :].rearrange("p (b c) n -> p b (c n)", b=2), ps_turn[:, :, :], ACT.Copy).then_inc(x_copied, 1)
                act.wait_ge(gu_done, j + 1)
                act.activation(hid[:, 0, :], ps_gu[:, 0, :], ACT.Sigmoid).then_inc(sigged, 1)
                act.wait_ge(h_turned, j + 1)
                act.activation(hidT[:, :, :].rearrange("p c n -> p (c n)"), ps_turn[:, 0, :], ACT.Copy).then_inc(h_copied, 1)
                act.wait_ge(y_done, j + 1)
                act.activation(y[:, :].rearrange("p (b n) -> p b n", b=2), ps_y[:, :, :], ACT.Copy).then_inc(y_copied, 1)
                act.wait_ge(stored, 16 * j + 16)
                act.sem_inc(fresh, 1)
            each(act, step)

        @block.vector
        def _(dve):
            def step(j):
                dve.wait_ge(sigged, j + 1)
                dve.tensor_tensor(hid[:, 1, :], hid[:, 0, :], ps_gu[:, 0, :], ALU.mult).then_inc(gated, 1)
                dve.wait_ge(gated, j + 1)
                dve.tensor_tensor(hid[:, 1, :], hid[:, 1, :], ps_gu[:, 1, :], ALU.mult).then_inc(hidden, 1)
            each(dve, step)


def add_results(nc, h, y_tok, weight_in, y_prompt, y_sample):
    with ExitStack() as ctx:
        m = Memory(nc, ctx, "final")
        SLOTS = 3
        weight = m.sb("weight", [P, TILES, 2])
        ht = m.sb("ht", [P, SLOTS, D])
        ys = m.sb("ys", [P, SLOTS, 2, D])
        out = m.sb("out", [P, SLOTS, D])
        loaded = m.sem("loaded")
        tile_in = [m.sem(f"tile_in{s}") for s in range(SLOTS)]
        one = m.sem("one")
        two = m.sem("two")
        stored = [m.sem(f"stored{s}") for s in range(SLOTS)]
        block = m.block()

        def n_rows(t):
            return NS if t == TILES - 1 else P

        @block.sync
        def _(sp):
            sp.dma_start(weight[:, :, :], weight_in.rearrange("(t p) k -> p t k", p=P), allow_slow_non_contiguous=True).then_inc(loaded, 16)
            for t in range(TILES):
                s, n = t % SLOTS, n_rows(t)
                wait(sp, two, t + 1 - SLOTS)
                sp.dma_start(ht[0:n, s, :], h[t * P:t * P + n, :]).then_inc(tile_in[s], 16)
                for k in range(2):
                    first = 1 + k * ROWS + t * P
                    sp.dma_start(ys[0:n, s, k, :], y_tok[first:first + n, :]).then_inc(tile_in[s], 16)

        @block.vector
        def _(dve):
            dve.wait_ge(loaded, 16)
            for t in range(TILES):
                s, n = t % SLOTS, n_rows(t)
                dve.wait_ge(tile_in[s], 48 * (t // SLOTS + 1))
                wait(dve, stored[s], 16 * (t // SLOTS))
                dve.scalar_tensor_tensor(out[0:n, s, :], ys[0:n, s, 0, :], weight[0:n, t, 0:1], ht[0:n, s, :], ALU.mult, ALU.add).then_inc(one, 1)
                dve.wait_ge(one, t + 1)
                dve.scalar_tensor_tensor(out[0:n, s, :], ys[0:n, s, 1, :], weight[0:n, t, 1:2], out[0:n, s, :], ALU.mult, ALU.add).then_inc(two, 1)

        @block.scalar
        def _(act):
            for t in range(TILES):
                s = t % SLOTS
                act.wait_ge(two, t + 1)
                if t < TILES - 1:
                    act.dma_start(y_prompt[t * P:(t + 1) * P, :], out[:, s, :]).then_inc(stored[s], 16)
                else:
                    act.dma_start(y_sample, out[0:NS, s, :]).then_inc(stored[s], 16)
            for s in range(SLOTS):
                act.wait_ge(stored[s], 16 * ((TILES + SLOTS - 1 - s) // SLOTS))


def caches(nc, a, z, outs):
    pairs = []
    for g, w in enumerate(WIN):
        for i, n in enumerate("kv"):
            new = z[n][:, g * GW:(g + 1) * GW]
            pairs.append((outs[2 + 2 * g + i][0].rearrange("t h d -> t (h d)"), new[SEQ - w:SEQ, :]))
            keep = min(w, PAST + DEC_S)
            out = outs[9 + 2 * g + i].rearrange("b t h d -> b t (h d)")
            old = a[f"cache_{n}_w{w}"].rearrange("b t h d -> b t (h d)")
            pairs.append((out[:, 0:keep - DEC_S, :], old[:, LB[g] + DEC_S - keep:LB[g], :]))
            pairs.append((out[:, keep - DEC_S:keep, :], new[SEQ:SEQ + NS, :].rearrange("(b s) c -> b s c", b=DEC_B)))
    pairs.append((outs[8][0], z["u"][SEQ - PSTATE:SEQ, :]))
    pairs.append((outs[15][:, 0:PSTATE - DEC_S, :], a["state_pool"][:, DEC_S:PSTATE, :]))
    pairs.append((outs[15][:, PSTATE - DEC_S:PSTATE, :], z["u"][SEQ:SEQ + NS, :].rearrange("(b s) c -> b s c", b=DEC_B)))
    with ExitStack() as ctx:
        m = Memory(nc, ctx, "caches")
        copied = m.sem("copied")
        block = m.block()

        @block.sync
        def _(sp):
            for dst, src in pairs:
                sp.dma_start(dst, src).then_inc(copied, 16)
            sp.wait_ge(copied, 16 * len(pairs))


def build(nc, a, outs):
    def dram(name, shape, dt=F32):
        return nc.dram_tensor(name, shape, dt).ap()

    xT = dram("xT", [TILES, P, 2, KC, P])
    z = {n: dram("z_" + n, [ROWS, w]) for n, w in (("q", AW), ("k", AW), ("v", AW), ("u", PW), ("ga", D), ("gb", D))}
    att = dram("att", [NG, ROWS, ATTW])
    joined = [dram(f"joined_{n}", [DEC_B, P + DEC_S, GW]) for n in "kv"]
    poolT = dram("poolT", [TILES, P, 2, PG, P])
    h = dram("h", [ROWS, D])
    xn = dram("xn", [ROWS, D])
    logits = dram("logits", [ROWS, EG + NE])
    slots = dram("slots", [BLOCKS * P, SLOT], I32)
    weight = dram("weight", [ROWS, 2])
    counts = dram("counts", [1, 2 * NE], I32)
    over = dram("over", [1, OVER + 1], I32)
    y_tok = dram("y_tok", [1 + 2 * ROWS, D])
    caches_kv = [[a[f"cache_{n}_w{w}"].rearrange("b t h d -> b t (h d)") for n in "kv"] for w in WIN]

    norm_and_turn(nc, a["x"], a["ln1"], a["ident"], xT)
    project(nc, xT, a["w_in"], a["q_gain"], a["k_gain"], z)
    prompt_attention(nc, z, att, a["ident"], a["bias"])
    sample_attention(nc, z, att, caches_kv, joined, a["sbias"])
    pooling(nc, z, a["state_pool"], a["pool_lin"], a["pool_scale"], a["ident"], a["inv_count"], poolT)
    merge_and_route(nc, a["x"], z, att, poolT, a["w_pa"], a["w_pb"], a["w_o"], a["ln2"], a["w_rg"], a["b_rg"],
                    a["w_re"], a["b_re"], a["ident"], h, xn, logits)
    routing(nc, logits, a, slots, weight, counts, over)
    caches(nc, a, z, outs)
    experts(nc, xn, slots, counts, a["w_gate"], a["w_up"], a["w_down"], a["ident"], y_tok)
    expert_overflow(nc, xn, slots, over, a["w_gate"], a["w_up"], a["w_down"], a["ident"], y_tok)
    add_results(nc, h, y_tok, weight, outs[0][0], outs[1].rearrange("b t d -> (b t) d"))


def constants(np):
    slope = np.exp2(-8.0 * np.arange(1, NG * HG + 1, dtype=np.float32) / (NG * HG)).astype(np.float32)
    qi, kb = np.arange(P)[:, None], np.arange(2 * P)[None, :]
    rel = qi + P - kb
    valid = (rel >= 0) & (rel <= P)
    bias = np.full((NG + 2, P, HG, 2 * P), -1e30, np.float32)
    for g in range(NG):
        for h in range(HG):
            b = -slope[g * HG + h] * (DIL[g] * rel).astype(np.float32)
            bias[g, :, SEAT[h]] = np.where(valid, b, np.float32(-1e30))
            if g < 2:
                bias[NG + g, :, SEAT[h]] = np.where(valid & (kb >= P), b, np.float32(-1e30))
    sbias = np.zeros((P, NG, P + 1), np.float32)
    for g in range(NG):
        n = LB[g] // DIL[g]
        dist = (DIL[g] * (n - np.arange(n + 1))).astype(np.float32)
        sbias[:, g, :n + 1] = -slope[g * HG + np.arange(P) % HG][:, None] * dist[None, :]
    pos = np.arange(16)
    inv_count = np.stack([1.0 / np.minimum(pos + 1, 2 << g) for g in range(PG)]).astype(np.float32)
    e = np.arange(NE)
    tile_rows = np.arange(TILES)[None, :] * P + np.arange(P)[:, None]
    entry = np.zeros((P, 2, TILES, SLOT), np.int32)
    entry[:, :, :, 0] = tile_rows[:, None, :]
    entry[:, :, :, 1] = 1 + ROWS * np.arange(2)[None, :, None] + tile_rows[:, None, :]
    return {
        "ident": np.eye(P, dtype=np.float32),
        "ones": np.ones((P, P), np.float32),
        "before": (np.arange(P)[:, None] < np.arange(P)[None, :]).astype(np.float32),
        "bias": bias,
        "sbias": sbias,
        "inv_count": np.broadcast_to(inv_count, (P, PG, 16)).copy(),
        "first_group": np.broadcast_to((EG - np.arange(EG)).astype(np.float32), (P, EG)).copy(),
        "first_expert": np.broadcast_to((NE - e).astype(np.float32), (P, NE)).copy(),
        "block_no": np.broadcast_to(np.arange(OVER, dtype=np.float32)[None, :, None], (P, OVER, NE)).copy(),
        "base": np.broadcast_to((2 * P * e).astype(np.float32), (P, NE)).copy(),
        "real": (tile_rows < SEQ + NS).astype(np.float32),
        "entry": entry,
    }
def kernel(**inputs):
    import numpy as np
    import concourse.bacc as bacc
    from concourse.bass_utils import run_bass_kernel_spmd

    nc = bacc.Bacc("TRN2", target_bir_lowering=False, num_devices=1)
    arrays = {}
    ins = {}

    def give(name, a):
        a = np.ascontiguousarray(a)
        arrays[name] = a
        ins[name] = nc.dram_tensor(name, a.shape, mybir.dt.from_np(a.dtype), kind="ExternalInput").ap()

    x = np.zeros((ROWS, D), np.float32)
    x[:SEQ] = np.asarray(inputs["x_prompt"]).reshape(SEQ, D)
    x[SEQ:SEQ + NS] = np.asarray(inputs["x_sample"]).reshape(NS, D)
    give("x", x)
    for name, a in inputs.items():
        if not name.startswith("x_"):
            give(name, np.asarray(a))
    for name, a in constants(np).items():
        give(name, a)
    shapes = ([(1, SEQ, D), (DEC_B, DEC_S, D)]
              + [(1, w, HG, HD) for w in WIN for _ in range(2)] + [(1, PSTATE, PW)]
              + [(DEC_B, min(w, PAST + DEC_S), HG, HD) for w in WIN for _ in range(2)] + [(DEC_B, PSTATE, PW)])
    outs = [nc.dram_tensor(f"out_{i}", s, F32, kind="ExternalOutput").ap() for i, s in enumerate(shapes)]
    build(nc, ins, outs)
    r = run_bass_kernel_spmd(nc, [arrays], core_ids=[0])
    return tuple(r.results[0][f"out_{i}"] for i in range(len(shapes)))
```

```python
from contextlib import ExitStack

import concourse.bass as bass
from concourse import mybir

F32 = mybir.dt.float32
F32R = mybir.dt.float32r
I32 = mybir.dt.int32
U32 = mybir.dt.uint32
ACT = mybir.ActivationFunctionType
ALU = mybir.AluOpType
AX = mybir.AxisListType

P = 128
D = 1024
KC = D // P
SEQ, DEC_B, DEC_S = 2048, 8, 4
NS = DEC_B * DEC_S
TILES = SEQ // P + 1
ROWS = TILES * P
HD, HG = 64, 4
GW = HG * HD
NG = 3
AW = NG * GW
DIL = (1, 4, 16)
WIN = (128, 512, 2048)
PAST = 1024
LB = tuple(min(w, PAST) for w in WIN)
PW = 512
PG = 4
PSTATE = 15
NE, EG, EPG = 32, 4, 8
FE = 512
FC = FE // P
OVER = (2 * (SEQ + NS) - 2 * (P + 1)) // P
BLOCKS = 2 * NE + OVER + 2
EPS = 1e-6
SLOT = 16
SEAT = (0, 2, 1, 3)
ATTW = HG * (HD + 2)


def by_twos(eng, n, body, peeled=1):
    for t in range(2 * peeled):
        body(t, t % 2, t // 2)
    if n // 2 > peeled:
        with eng.Fori(peeled, n // 2) as j:
            body(j * 2, 0, j)
            body(j * 2 + 1, 1, j)
    if n % 2:
        body(n - 1, 0, n // 2)


def rows(t):
    return bass.ds(t * P, P)


def wait_apart(eng, sem, count, done):
    if not isinstance(count, int) or count > 0:
        eng.wait_ge(*done)
        eng.wait_ge(sem, count)


class Memory:

    def __init__(self, nc, ctx, stage):
        self.nc, self.ctx, self.stage, self.sems = nc, ctx, stage, []

    def sb(self, name, shape, dt=F32):
        return self.ctx.enter_context(self.nc.sbuf_tensor(f"{self.stage}_{name}", shape, dt))

    def ps(self, name, shape, dt=F32):
        return self.ctx.enter_context(self.nc.psum_tensor(f"{self.stage}_{name}", shape, dt))

    def sem(self, name):
        self.sems.append(self.ctx.enter_context(self.nc.semaphore(f"{self.stage}_{name}")))
        return self.sems[-1]

    def pool_sem(self, name):
        self.sems.append(self.nc.alloc_semaphore(f"{self.stage}_{name}"))
        return self.sems[-1]

    def block(self):
        for s in self.sems:
            self.nc.gpsimd.sem_clear(s)
        self.nc.all_engine_barrier()
        return self.ctx.enter_context(self.nc.Block())


def norm_and_turn(nc, x, ln1, ident_in, xT):
    with ExitStack() as ctx:
        m = Memory(nc, ctx, "norm")
        xin = m.sb("xin", [P, 2, D])
        junk = m.sb("junk", [P, D])
        xn = m.sb("xn", [P, 2, D])
        split = m.sb("split", [P, 2, 2, D], F32R)
        lnrow = m.sb("lnrow", [P, D])
        ident = m.sb("ident", [P, P])
        eps = m.sb("eps", [P, 1])
        ss = m.sb("ss", [P, 2])
        rms = m.sb("rms", [P, 2])
        rstd = m.sb("rstd", [P, 2])
        turned = m.ps("turned", [P, 2, 2, 512])

        consts_in = m.sem("consts_in")
        eps_set = m.sem("eps_set")
        x_in = [m.sem(f"x_in{s}") for s in range(2)]
        squared = m.sem("squared")
        rooted = m.sem("rooted")
        inverted = m.sem("inverted")
        normed = m.sem("normed")
        turns = m.sem("turns")
        hi_done = m.sem("hi_done")
        lo_done = m.sem("lo_done")
        stored = [m.pool_sem(f"stored{s}") for s in range(2)]
        block = m.block()

        @block.sync
        def _(sp):
            sp.dma_start(lnrow[:, :], ln1[None, :].partition_broadcast(P)).then_inc(consts_in, 16)
            sp.dma_start(ident[:, :], ident_in).then_inc(consts_in, 16)

            def load(t, s, k):
                if not (isinstance(t, int) and t < 2):
                    sp.wait_ge(normed, t - 1)
                sp.dma_start(xin[:, s, :], x[rows(t), :]).then_inc(x_in[s], 16)
            by_twos(sp, TILES, load)

        @block.gpsimd
        def _(pool):
            pool.memset(eps[:, :], EPS).then_inc(eps_set, 1)

            def store(t, s, k):
                pool.wait_ge(lo_done, t + 1)
                pool.dma_start(xT[t].rearrange("p a c n -> p a (c n)"), split[:, s, :, :].bitcast(F32)).then_inc(stored[s], 16)
            by_twos(pool, TILES, store)
            pool.wait_ge(stored[0], 16 * (TILES - TILES // 2))
            pool.wait_ge(stored[1], 16 * (TILES // 2))

        @block.scalar
        def _(act):
            act.wait_ge(eps_set, 1)

            def root(t, s, k):
                act.wait_ge(x_in[s], 16 * k + 16)
                if not (isinstance(t, int) and t < 2):
                    act.wait_ge(normed, t - 1)
                act.activation(junk[:, :], xin[:, s, :], ACT.Square, accum_out=ss[:, s:s + 1]).then_inc(squared, 1)
                act.wait_ge(squared, t + 1)
                act.activation(rms[:, s:s + 1], ss[:, s:s + 1], ACT.Sqrt, bias=eps[:, 0:1],
                               scale=1.0 / D).then_inc(rooted, 1)

            def step(t, s, k):
                if not (isinstance(t, int) and t == TILES - 1):
                    root(t + 1, 1 - s, k + s)
                act.wait_ge(turns, t + 1)
                if not (isinstance(t, int) and t < 2):
                    act.wait_ge(stored[s], 16 * k)
                act.activation(split[:, s, 0, :].rearrange("p (b n) -> p b n", b=2), turned[:, s, :, :],
                               ACT.Copy).then_inc(hi_done, 1)
            root(0, 0, 0)
            by_twos(act, TILES, step)

        @block.vector
        def _(dve):
            dve.wait_ge(consts_in, 32)

            def norm(t, s):
                dve.wait_ge(rooted, t + 1)
                dve.reciprocal(rstd[:, s:s + 1], rms[:, s:s + 1]).then_inc(inverted, 1)
                dve.wait_ge(inverted, t + 1)
                if not (isinstance(t, int) and t < 2):
                    dve.wait_ge(turns, t - 1)
                dve.scalar_tensor_tensor(xn[:, s, :], xin[:, s, :], rstd[:, s:s + 1], lnrow[:, :],
                                         ALU.mult, ALU.mult).then_inc(normed, 1)

            def step(t, s, k):
                if not (isinstance(t, int) and t == TILES - 1):
                    norm(t + 1, 1 - s)
                dve.wait_ge(hi_done, t + 1)
                dve.tensor_tensor(split[:, s, 1, :].rearrange("p (b n) -> p b n", b=2), turned[:, s, :, :],
                                  split[:, s, 0, :].bitcast(F32).rearrange("p (b n) -> p b n", b=2),
                                  ALU.subtract).then_inc(lo_done, 1)
            norm(0, 0)
            by_twos(dve, TILES, step)

        @block.tensor
        def _(pe):
            pe.wait_ge(consts_in, 32)

            def step(t, s, k):
                pe.wait_ge(normed, t + 1)
                if not (isinstance(t, int) and t < 2):
                    pe.wait_ge(lo_done, t - 1)
                for c in range(KC):
                    last = pe.transpose(turned[:, s, c // 4, (c % 4) * P:(c % 4 + 1) * P],
                                        xn[:, s, c * P:(c + 1) * P], ident[:, :])
                last.then_inc(turns, 1)
            by_twos(pe, TILES, step)


def project(nc, xT, w_in, q_gain, k_gain, z, kept):
    groups = [("q", 0, 384), ("k", AW, 384), ("v", 2 * AW, 384), ("u", 3 * AW, 256),
              ("ga", 3 * AW + PW, 512), ("gb", 3 * AW + PW + D, 512)]
    heads = AW // HD
    with ExitStack() as ctx:
        m = Memory(nc, ctx, "proj")
        w_raw = m.sb("w_raw", [P, KC, D])
        w_hi = [m.sb(f"w_hi{i}", [P, KC, D], F32R) for i in range(2)]
        w_lo = [m.sb(f"w_lo{i}", [P, KC, D], F32R) for i in range(2)]
        xs = m.sb("xs", [P, 2, 2, KC, P], F32R)
        out = m.sb("out", [P, 2, D])
        sq = m.sb("sq", [P, AW])
        gain = m.sb("gain", [P, 2, AW])
        eps = m.sb("eps", [P, 1])
        ss = m.sb("ss", [P, heads])
        rms = m.sb("rms", [P, heads])
        rstd = m.sb("rstd", [P, heads])
        acc = m.ps("acc", [P, 2, 2, 512])

        consts_in = m.sem("consts_in")
        eps_set = m.sem("eps_set")
        w_first = [m.pool_sem(f"w_first{c}") for c in range(KC)]
        w_loaded = m.pool_sem("w_loaded")
        w_hi_done = m.sem("w_hi_done")
        w_lo_done = m.sem("w_lo_done")
        x_loaded = [m.sem(f"x_loaded{s}") for s in range(2)]
        copied = m.sem("copied")
        products = m.sem("products")
        squared = m.sem("squared")
        summed = m.sem("summed")
        rooted = m.sem("rooted")
        inverted = m.sem("inverted")
        scaled = m.sem("scaled")
        left_psum = m.sem("left_psum")
        normed = m.sem("normed")
        copied_out = m.sem("copied_out")
        stored = [m.pool_sem(f"stored{s}") for s in range(2)]
        block = m.block()

        def width(g):
            return 2 * groups[g][2]

        def seat(g, s, k):
            return (g * TILES + s) % 2, k + (g * TILES + s) // 2

        def wait_output(eng, g, t):
            if g < 2:
                wait(eng, normed, t + (g * TILES + 1))
            else:
                wait(eng, copied_out, t + ((g - 2) * TILES + 1))

        @block.sync
        def _(sp):
            sp.dma_start(gain[:, 0, :], q_gain.rearrange("h d -> (h d)")[None, :].partition_broadcast(P)).then_inc(consts_in, 16)
            sp.dma_start(gain[:, 1, :], k_gain.rearrange("h d -> (h d)")[None, :].partition_broadcast(P)).then_inc(consts_in, 16)
            for g in range(len(groups)):
                def load(t, s, k, g=g):
                    q, _ = seat(g, s, k)
                    wait(sp, products, t + (g * TILES - 1))
                    sp.dma_start(xs[:, q, :, :, :].bitcast(F32), xT[t]).then_inc(x_loaded[q], 16)
                    if not (isinstance(t, int) and t == TILES - 1):
                        dst, src = kept[g]
                        sp.dma_start(dst[bass.ds(k, 1), s], src[bass.ds(k, 1), s]).then_inc(copied, 16)
                by_twos(sp, TILES, load)
            sp.wait_ge(copied, 16 * (TILES - 1) * len(groups))

        @block.gpsimd
        def _(pool):
            pool.memset(eps[:, :], EPS).then_inc(eps_set, 1)

            def load_w(g):
                _, col, nb = groups[g]
                for c in range(KC):
                    if g:
                        pool.wait_ge(w_lo_done, KC * (g - 1) + c + 1)
                    pool.dma_start(w_raw[:, c, 0:2 * nb], w_in[c * P:(c + 1) * P, col:col + 2 * nb]).then_inc(w_loaded if g else w_first[c], 16)

            load_w(0)
            for g in range(len(groups)):
                if g + 1 < len(groups):
                    load_w(g + 1)

                def store(t, s, k, g=g):
                    q, _ = seat(g, s, k)
                    wait_output(pool, g, t)
                    pool.dma_start(z[groups[g][0]][rows(t), :], out[:, q, 0:width(g)]).then_inc(stored[q], 16)
                by_twos(pool, TILES, store)
            for s in range(2):
                pool.wait_ge(stored[s], 16 * ((TILES * len(groups) + 1 - s) // 2))

        def slot_free(eng, q, before):
            wait(eng, stored[q], 16 * before)

        @block.scalar
        def _(act):
            def split_w(g, c):
                w, cs = width(g), bass.ds(c, 1)
                act.activation(w_hi[g % 2][:, cs, 0:w], w_raw[:, cs, 0:w], ACT.Copy).then_inc(w_hi_done, 1)

            act.wait_ge(eps_set, 1)
            for c in range(KC):
                act.wait_ge(w_first[c], 16)
                split_w(0, c)
            for g, (name, _, nb) in enumerate(groups):
                def tile(t, s, k, g=g, name=name, nb=nb):
                    n = g * TILES + t
                    q, before = seat(g, s, k)
                    act.wait_ge(products, n + 1)
                    if name in "qk":
                        act.activation(sq[:, :].rearrange("p (b n) -> p b n", b=2), acc[:, q, :, 0:nb],
                                       ACT.Square).then_inc(squared, 1)
                        act.wait_ge(summed, n + 1)
                        act.activation(rms[:, :], ss[:, :], ACT.Sqrt, bias=eps[:, 0:1], scale=1.0 / HD).then_inc(rooted, 1)
                    else:
                        slot_free(act, q, before)
                        act.activation(out[:, q, 0:2 * nb].rearrange("p (b n) -> p b n", b=2), acc[:, q, :, 0:nb],
                                       ACT.Sigmoid if name in ("ga", "gb") else ACT.Copy).then_inc(copied_out, 1)
                    if s == 1 and g + 1 < len(groups):
                        act.wait_ge(w_loaded, 16 * KC * (g + 1))
                        split_w(g + 1, k)
                by_twos(act, TILES, tile)

        @block.vector
        def _(dve):
            def split_w(g, c):
                w, cs = width(g), bass.ds(c, 1)
                dve.wait_ge(w_hi_done, c + (KC * g + 1))
                dve.tensor_tensor(w_lo[g % 2][:, cs, 0:w], w_raw[:, cs, 0:w], w_hi[g % 2][:, cs, 0:w].bitcast(F32),
                                  ALU.subtract).then_inc(w_lo_done, 1)

            dve.wait_ge(consts_in, 32)
            for c in range(KC):
                split_w(0, c)
            for g, (name, _, nb) in enumerate(groups):
                def tile(t, s, k, g=g, nb=nb):
                    n = g * TILES + t
                    q, before = seat(g, s, k)
                    dve.wait_ge(squared, n + 1)
                    dve.tensor_reduce(ss[:, :], sq[:, :].rearrange("p (h d) -> p h d", d=HD), AX.X, ALU.add).then_inc(summed, 1)
                    dve.wait_ge(rooted, n + 1)
                    dve.reciprocal(rstd[:, :], rms[:, :]).then_inc(inverted, 1)
                    dve.wait_ge(inverted, n + 1)
                    slot_free(dve, q, before)
                    for b in range(2):
                        r = rstd[:, b * 6:(b + 1) * 6][:, :, None].broadcast_to([P, 6, HD])
                        last = dve.tensor_tensor(out[:, q, b * nb:(b + 1) * nb].rearrange("p (h d) -> p h d", d=HD),
                                                 acc[:, q, b, 0:nb].rearrange("p (h d) -> p h d", d=HD), r, ALU.mult)
                    last.then_inc(scaled, 1)
                    dve.wait_ge(scaled, n + 1)
                    dve.tensor_tensor(out[:, q, 0:AW], out[:, q, 0:AW], gain[:, g, :], ALU.mult).then_inc(normed, 1)
                    if s == 1:
                        split_w(g + 1, k)
                if name in "qk":
                    by_twos(dve, TILES, tile)
                elif g + 1 < len(groups):
                    for c in range(KC):
                        split_w(g + 1, c)

        @block.tensor
        def _(pe):
            for g, (name, _, nb) in enumerate(groups):
                hi, lo = w_hi[g % 2], w_lo[g % 2]
                pe.wait_ge(w_lo_done, KC * (g + 1))

                def tile(t, s, k, g=g, nb=nb, hi=hi, lo=lo):
                    n = g * TILES + t
                    q, before = seat(g, s, k)
                    pe.wait_ge(x_loaded[q], 16 * before + 16)
                    if not (isinstance(t, int) and t < 2):
                        wait_output(pe, g, t - 2)
                    elif g:
                        wait_output(pe, g - 1, TILES + t - 2)
                    for c in range(KC):
                        for i, (xp, w) in enumerate(((0, hi), (0, lo), (1, hi))):
                            for b in range(2):
                                last = pe.matmul(acc[:, q, b, 0:nb], xs[:, q, xp, c, :], w[:, c, b * nb:(b + 1) * nb],
                                                 start=(c == 0 and i == 0), stop=(c == KC - 1 and i == 2))
                    last.then_inc(products, 1)
                by_twos(pe, TILES, tile)


def wait(eng, sem, count):
    if not isinstance(count, int) or count > 0:
        eng.wait_ge(sem, count)


def by_fours(eng, n, body, peel_last=False):
    for s in range(4):
        body(s, s, 0)
    with eng.Fori(1, n // 4 - peel_last) as j:
        for s in range(4):
            body(j * 4 + s, s, j)
    if peel_last:
        for s in range(4):
            body(n - 4 + s, s, n // 4 - 1)


def prompt_attention(nc, z, att, ident_in, bias_in):
    NB = SEQ // P
    steps = NB * NG
    with ExitStack() as ctx:
        m = Memory(nc, ctx, "attn")
        ident = m.sb("ident", [P, P])
        bias = m.sb("bias", [P, NG + 1, HG, 2 * P])
        bias1 = m.sb("bias1", [P, HG, 2 * P])
        q = m.sb("q", [P, 4, GW])
        k = m.sb("k", [P, 4, 2, GW])
        v = m.sb("v", [P, 4, 2, GW])
        qkT = m.sb("qkT", [P, 2, 6, P])
        sc = m.sb("sc", [P, 2, HG, 2 * P])
        pr = m.sb("pr", [P, 2, HG, 2 * P])
        prT = m.sb("prT", [P, 2, HG, 2, P])
        nmax = m.sb("nmax", [P, 4, HG])
        out = m.sb("out", [P, 4, HG, HD + 2])
        ps_turn = m.ps("turn", [P, 2, 512])
        ps_sc = m.ps("sc_ps", [P, HG, 2 * P])
        ps_prT = m.ps("prT_ps", [P, HG, 2, P])
        ps_o = m.ps("o_ps", [P, 2, 512])

        consts_in = m.sem("consts_in")
        qk_in = [m.sem(f"qk_in{s}") for s in range(4)]
        v_in = [m.sem(f"v_in{s}") for s in range(4)]
        qk_turned = m.sem("qk_turned")
        qk_copied = m.sem("qk_copied")
        scored = m.sem("scored")
        biased = m.sem("biased")
        maxed = m.sem("maxed")
        negated = m.sem("negated")
        exped = m.sem("exped")
        p_turned = m.sem("p_turned")
        p_copied_act = m.sem("p_copied_act")
        p_copied_dve = m.sem("p_copied_dve")
        weighted = m.sem("weighted")
        o_copied = m.sem("o_copied")
        stored = [m.pool_sem(f"stored{s}") for s in range(4)]
        block = m.block()

        def nk(g):
            return 1 if g == 2 else 2

        def view(name, g):
            a = z[name][:, g * GW:(g + 1) * GW]
            return a.rearrange("(l r) c -> r l c", r=DIL[g])

        def place(g, i):
            if DIL[g] == NB:
                return i, 0, 0
            if g == 0:
                return 0, i * P, (max(i - 1, 0) * P if isinstance(i, int) else (i - 1) * P)
            if isinstance(i, int):
                return i % DIL[g], i // DIL[g] * P, max(i // DIL[g] - 1, 0) * P
            return i[1], i[0] * P, (i[0] - 1) * P

        def all_blocks(eng, body):
            for g in range(NG):
                def one(t, s, j, g=g):
                    i = t if isinstance(t, int) or g != 1 else (j, s)
                    body(g, g * NB + t, s, g * (NB // 4) + j, i)
                by_fours(eng, NB, one, peel_last=(g == NG - 1))

        @block.sync
        def _(sp):
            sp.dma_start(ident[:, :], ident_in).then_inc(consts_in, 16)
            sp.dma_start(bias[:, :, :, :], bias_in[0:NG + 1].rearrange("g p h k -> p g h k")).then_inc(consts_in, 16)
            sp.dma_start(bias1[:, :, :], bias_in[NG + 1]).then_inc(consts_in, 16)

            def load(g, n, s, j, i):
                r, own, former = place(g, i)
                qv, kv, vv = view("q", g), view("k", g), view("v", g)
                wait_apart(sp, qk_turned, n - 3, (consts_in, 48))
                sp.dma_start(q[:, s, :], qv[r, bass.ds(own, P), :]).then_inc(qk_in[s], 16)
                sp.dma_start(k[:, s, 1, :], kv[r, bass.ds(own, P), :]).then_inc(qk_in[s], 16)
                sp.dma_start(k[:, s, 0, :], kv[r, bass.ds(former, P), :]).then_inc(qk_in[s], 16)
                wait_apart(sp, weighted, n - 3, (consts_in, 48))
                sp.dma_start(v[:, s, 1, :], vv[r, bass.ds(own, P), :]).then_inc(v_in[s], 16)
                sp.dma_start(v[:, s, 0, :], vv[r, bass.ds(former, P), :]).then_inc(v_in[s], 16)
            all_blocks(sp, load)

        @block.gpsimd
        def _(pool):
            def store(g, n, s, j, i):
                r, own, _ = place(g, i)
                wait_apart(pool, o_copied, n + 1, (consts_in, 48))
                dst = att[g].rearrange("(l r) c -> r l c", r=DIL[g])
                pool.dma_start(dst[r, bass.ds(own, P), :], out[:, s, :, :].rearrange("p h e -> p (h e)")).then_inc(stored[s], 16)
            all_blocks(pool, store)
            for s in range(4):
                pool.wait_ge(stored[s], 16 * steps // 4)

        @block.tensor
        def _(pe):
            def turn_qk(g, n, s, j):
                pe.wait_ge(qk_in[s], 48 * (j + 1))
                wait(pe, qk_copied, n)
                parts = [q[:, s, 0:P], q[:, s, P:GW]] + [k[:, s, b, c * P:(c + 1) * P] for b in range(2) for c in range(2)]
                for x, part in enumerate(parts):
                    last = pe.transpose(ps_turn[:, x // 3, (x % 3) * P:(x % 3 + 1) * P], part, ident[:, :])
                last.then_inc(qk_turned, 1)

            def scores(g, n, s):
                pe.wait_ge(qk_copied, n + 1)
                wait(pe, biased, n)
                b = 2 - nk(g)
                for h in range(HG):
                    lo = HD * (h % 2)
                    last = pe.matmul(ps_sc[:, SEAT[h], b * P:2 * P].rearrange("p (b n) -> p b n", n=P), qkT[lo:lo + HD, s % 2, h // 2, :],
                                     qkT[lo:lo + HD, s % 2, 2 + 2 * b + h // 2:6:2, :], start=True, stop=True)
                last.then_inc(scored, 1)

            def turn_p(g, n, s):
                pe.wait_ge(exped, HG * (n + 1))
                wait(pe, p_copied_act, n)
                wait(pe, p_copied_dve, n)
                for h in range(HG):
                    for b in range(2 - nk(g), 2):
                        last = pe.transpose(ps_prT[:, SEAT[h], b, :], pr[:, s % 2, SEAT[h], b * P:(b + 1) * P], ident[:, :])
                last.then_inc(p_turned, 1)

            def weigh_v(g, n, s, j):
                pe.wait_ge(v_in[s], 32 * (j + 1))
                pe.wait_ge(p_copied_act, n + 1)
                pe.wait_ge(p_copied_dve, n + 1)
                wait(pe, o_copied, n - 1)
                for h in range(HG):
                    for b in range(2 - nk(g), 2):
                        last = pe.matmul(ps_o[:, s % 2, h * HD:(h + 1) * HD], prT[:, s % 2, SEAT[h], b, :],
                                         v[:, s, b, h * HD:(h + 1) * HD], start=(b == 2 - nk(g)), stop=(b == 1))
                last.then_inc(weighted, 1)

            pe.wait_ge(consts_in, 48)
            turn_qk(0, 0, 0, 0)

            def step(g, n, s, j, i):
                first = isinstance(i, int) and i < 2
                gb = g - 1 if first else g
                sb_, jb = (s + 2) % 4, (j if s >= 2 else j - 1)
                if not (isinstance(n, int) and n < 2):
                    turn_p(gb, n - 2, sb_)
                scores(g, n, s)
                sn, jn = (s + 1) % 4, (j if s < 3 else j + 1)
                if not (isinstance(n, int) and n == steps - 1):
                    turn_qk(g, n + 1, sn, jn)
                if not (isinstance(n, int) and n < 2):
                    weigh_v(gb, n - 2, sb_, jb)

            all_blocks(pe, step)
            for n in (steps - 2, steps - 1):
                turn_p(NG - 1, n, n % 4)
                weigh_v(NG - 1, n, n % 4, n // 4)

        @block.vector
        def _(dve):
            def copy_p(g, n, s):
                b = 2 - nk(g)
                dve.wait_ge(p_turned, n + 1)
                wait(dve, weighted, n - 1)
                dve.tensor_copy(prT[:, s % 2, 2:4, b:2, :], ps_prT[:, 2:4, b:2, :]).then_inc(p_copied_dve, 1)

            def copy_o(n, s):
                dve.wait_ge(weighted, n + 1)
                dve.tensor_copy(out[:, s, :, 0:HD], ps_o[:, s % 2, 0:GW].rearrange("p (h d) -> p h d", d=HD)).then_inc(o_copied, 1)

            dve.wait_ge(consts_in, 48)

            def step(g, n, s, j, i):
                gb = g - 1 if isinstance(i, int) and i < 2 else g
                if not (isinstance(n, int) and n < 2):
                    copy_p(gb, n - 2, (s + 2) % 4)
                b = 2 - nk(g)
                table = bias[:, g, :, b * P:2 * P]
                if g == 0 and isinstance(i, int) and i == 0:
                    table = bias[:, NG, :, :]
                if g == 1 and isinstance(i, int) and i < DIL[1]:
                    table = bias1[:, :, :]
                dve.wait_ge(scored, n + 1)
                wait(dve, exped, HG * (n - 1))
                dve.scalar_tensor_tensor(sc[:, s % 2, :, b * P:2 * P], ps_sc[:, :, b * P:2 * P], HD ** -0.5,
                                         table, ALU.mult, ALU.add).then_inc(biased, 1)
                dve.wait_ge(biased, n + 1)
                wait(dve, stored[s], 16 * j)
                dve.tensor_reduce(out[:, s, :, HD].rearrange("p (i o) -> p o i", o=2),
                                  sc[:, s % 2, :, b * P:2 * P].rearrange("p (o i) k -> p o i k", o=2), AX.X, ALU.max).then_inc(maxed, 1)
                dve.wait_ge(maxed, n + 1)
                dve.tensor_scalar(nmax[:, s, :], out[:, s, :, HD], -1.0, None, ALU.mult).then_inc(negated, 1)
                if not (isinstance(n, int) and n < 2):
                    copy_o(n - 2, (s + 2) % 4)
            all_blocks(dve, step)
            for n in (steps - 2, steps - 1):
                copy_p(NG - 1, n, n % 4)
                copy_o(n, n % 4)

        @block.scalar
        def _(act):
            def copy_p(g, n, s):
                b = 2 - nk(g)
                act.wait_ge(p_turned, n + 1)
                wait(act, weighted, n - 1)
                act.activation(prT[:, s % 2, 0:2, b:2, :], ps_prT[:, 0:2, b:2, :], ACT.Copy).then_inc(p_copied_act, 1)

            def copy_qk(n, s):
                act.wait_ge(qk_turned, n + 1)
                wait(act, scored, n - 1)
                act.activation(qkT[:, s % 2, :, :].rearrange("p (a x) n -> p a (x n)", a=2), ps_turn[:, :, 0:3 * P],
                               ACT.Copy).then_inc(qk_copied, 1)

            copy_qk(0, 0)

            def step(g, n, s, j, i):
                gb = g - 1 if isinstance(i, int) and i < 2 else g
                if not (isinstance(n, int) and n < 2):
                    copy_p(gb, n - 2, (s + 2) % 4)
                if not (isinstance(n, int) and n == steps - 1):
                    copy_qk(n + 1, (s + 1) % 4)
                b = 2 - nk(g)
                act.wait_ge(negated, n + 1)
                for h in range(HG):
                    act.activation(pr[:, s % 2, SEAT[h], b * P:2 * P], sc[:, s % 2, SEAT[h], b * P:2 * P], ACT.Exp,
                                   bias=nmax[:, s, h:h + 1], accum_out=out[:, s, h, HD + 1:HD + 2]).then_inc(exped, 1)
            all_blocks(act, step)
            for n in (steps - 2, steps - 1):
                copy_p(NG - 1, n, n % 4)

def sample_and_pooling(nc, z, att, caches_kv, joined, sbias_in, state, pool_lin, pool_scale, ident_in, inv_count_in, poolT):
    ORDER = (1, 0, 2)
    PAD = 16
    W = PAD + SEQ
    EXT = PSTATE + DEC_S
    with ExitStack() as ctx:
        m = Memory(nc, ctx, "mean")
        q = m.sb("q", [P, NG, HD])
        keys = m.sb("keys", [P, P + 1, HD])
        values = m.sb("values", [P, P + 1, HD])
        prod = m.sb("prod", [P, (P + 1) * HD])
        sbias = m.sb("sbias", [P, NG, P + 1])
        sc = m.sb("sc", [P, P + 1])
        ex = m.sb("ex", [P, P + 1])
        nmax = m.sb("nmax", [P, 1])
        att_out = m.sb("att_out", [P, NG, HD + 2])
        sbias_sem = m.sem("sbias_in")
        joined_sem = m.sem("joined")
        q_in = m.sem("q_in")
        k_in = m.sem("k_in")
        v_in = m.sem("v_in")
        k_read = m.sem("k_read")
        steps = m.sem("steps")
        negated = m.sem("negated")
        exped = m.sem("exped")
        v_read = m.sem("v_read")
        attended = m.sem("attended")
        att_stored = m.sem("att_stored")
        ident = m.sb("ident", [P, P])
        u = m.sb("u", [P, 4, PW])
        st = prod[:, 0:PW]
        uT = m.sb("uT", [P, PG, W])
        ext = m.sb("ext", [P, PG, DEC_B, EXT])
        sums = m.sb("sums", [P, 2, W])
        esums = m.sb("esums", [P, 2, DEC_B, EXT])
        zT = m.sb("zT", [P, PG, ROWS])
        head = m.sb("head", [P, PG, PAD])
        inv = m.sb("inv", [P, PG, PAD])
        lin = m.sb("lin", [P, PG, P])
        scale = m.sb("scale", [P, PG])
        res_hi = m.sb("res_hi", [P, 2, 512], F32R)
        res_lo = m.sb("res_lo", [P, 2, 512], F32R)
        ps_turn = m.ps("turn", [P, 2, PG, P])
        ps_lin = m.ps("lin_ps", [P, 2, 512])
        consts_in = m.sem("consts_in")
        state_in = m.sem("state_in")
        cleared = m.sem("cleared")
        u_in = [m.sem(f"u_in{s}") for s in range(4)]
        turned = m.sem("turned")
        copied = m.sem("copied")
        own = m.sem("own")
        mixed = m.sem("mixed")
        mapped = m.sem("mapped")
        hi_done = m.sem("hi_done")
        lo_done = m.sem("lo_done")
        hi_stored = [m.sem(f"hi_stored{s}") for s in range(2)]
        lo_stored = [m.pool_sem(f"lo_stored{s}") for s in range(2)]
        block = m.block()
        chunks = [(c, min(c + 512, ROWS)) for c in range(0, ROWS, 512)]
        jobs = [(g, a, b) for g in range(PG) for a, b in chunks]

        def new_rows(name, g):
            return z[name][SEQ:SEQ + NS, g * GW:(g + 1) * GW].rearrange("r (h d) -> h r d", d=HD)

        def n_dmas(g):
            return DEC_B + (HG if g else 0)

        seen = {g: 16 * sum(n_dmas(x) for x in ORDER[:o + 1]) for o, g in enumerate(ORDER)}

        @block.sync
        def _(sp):
            sp.dma_start(ident[:, :], ident_in).then_inc(consts_in, 16)
            sp.dma_start(inv[:, :, :], inv_count_in).then_inc(consts_in, 16)
            sp.dma_start(lin[:, :, :], pool_lin.rearrange("g c d -> c g d")).then_inc(consts_in, 16)
            sp.dma_start(scale[:, :], pool_scale.rearrange("(g d) -> d g", d=P), allow_slow_non_contiguous=True).then_inc(consts_in, 16)
            sp.dma_start(st[0:DEC_B * PSTATE, :], state.rearrange("b t c -> (b t) c")).then_inc(state_in, 16)
            sp.dma_start(sbias[:, :, :], sbias_in).then_inc(sbias_sem, 16)

            def load(t, s, j):
                wait(sp, turned, t - 3)
                sp.dma_start(u[:, s, :], z["u"][rows(t), :]).then_inc(u_in[s], 16)
            by_fours(sp, TILES - 1, load)
            load(TILES - 1, 0, 0)
            for i, name in enumerate("kv"):
                sp.dma_start(joined[i][:, 0:P, :], caches_kv[0][i]).then_inc(joined_sem, 16)
                sp.dma_start(joined[i][:, P:P + DEC_S, :], z[name][SEQ:SEQ + NS, 0:GW].rearrange("(b s) c -> b s c", b=DEC_B)).then_inc(joined_sem, 16)
            for g in range(NG):
                for h in range(HG):
                    sp.dma_start(q[h::HG, g, :], new_rows("q", g)[h]).then_inc(q_in, 16)
            for o, g in enumerate(ORDER):
                n = LB[g] // DIL[g]
                if g == 0:
                    sp.wait_ge(joined_sem, 64)
                for i, (name, to, sem, used) in enumerate((("k", keys, k_in, k_read), ("v", values, v_in, v_read))):
                    wait(sp, used, o)
                    for b in range(DEC_B):
                        src = joined[i][b] if g == 0 else caches_kv[g][i][b]
                        rows_ = n + 1 if g == 0 else n
                        win = bass.AP(src.tensor, src.offset, [[HD, DEC_S * HG], [DIL[g] * GW, rows_], [1, HD]])
                        sp.dma_start(to[b * 16:(b + 1) * 16, 0:rows_, :], win).then_inc(sem, 16)
                    if g > 0:
                        for h in range(HG):
                            sp.dma_start(to[h::HG, n, :], new_rows(name, g)[h]).then_inc(sem, 16)
            for o, g in enumerate(ORDER):
                sp.wait_ge(attended, o + 1)
                flat = att[g].rearrange("r (h e) -> (r h) e", e=HD + 2)
                for c in range(HG):
                    lo = SEQ * HG + c * P
                    sp.dma_start(flat[lo:lo + P, :], att_out[:, g, :]).then_inc(att_stored, 16)
            sp.wait_ge(att_stored, 16 * NG * HG)

        @block.gpsimd
        def _(pool):
            pool.memset(uT[:, :, 0:PAD], 0.0)
            pool.memset(zT[:, :, SEQ:ROWS], 0.0).then_inc(cleared, 1)
            for n, (g, a, b) in enumerate(jobs):
                pool.wait_ge(lo_done, n + 1)
                pool.dma_start(poolT[a // P:b // P, :, 1, g, :].rearrange("t p n -> p t n"),
                               res_lo[:, n % 2, 0:b - a].bitcast(F32).rearrange("p (t n) -> p t n", n=P)).then_inc(lo_stored[n % 2], 16)
            for s in range(2):
                pool.wait_ge(lo_stored[s], 16 * len(jobs) // 2)

        @block.tensor
        def _(pe):
            pe.wait_ge(consts_in, 64)

            def turn(t, s, j):
                pe.wait_ge(u_in[s], 16 * j + 16)
                wait(pe, copied, t - 1)
                for g in range(PG):
                    last = pe.transpose(ps_turn[:, s % 2, g, :], u[:, s, g * P:(g + 1) * P], ident[:, :])
                last.then_inc(turned, 1)
            by_fours(pe, TILES - 1, turn)
            turn(TILES - 1, 0, (TILES - 1) // 4)
            pe.wait_ge(state_in, 16)
            pe.wait_ge(copied, TILES)
            rows_ = DEC_B * PSTATE
            for g in range(PG):
                last = pe.transpose(ps_turn[:, 1, g, 0:rows_], st[0:rows_, g * P:(g + 1) * P], ident[0:rows_, 0:rows_])
            last.then_inc(turned, 1)
            for n, (g, a, b) in enumerate(jobs):
                pe.wait_ge(mixed, g + 1)
                wait(pe, lo_done, n - 1)
                pe.matmul(ps_lin[:, n % 2, 0:b - a], lin[:, g, :], zT[:, g, a:b], start=True, stop=True).then_inc(mapped, 1)

        @block.scalar
        def _(act):
            def exponentials(o):
                n = LB[ORDER[o]] // DIL[ORDER[o]] + 1
                act.wait_ge(negated, o + 1)
                act.activation(ex[:, 0:n], sc[:, 0:n], ACT.Exp, bias=nmax[:, 0:1],
                               accum_out=att_out[:, ORDER[o], HD + 1:HD + 2]).then_inc(exped, 1)

            def copy(t, s, k):
                act.wait_ge(turned, t + 1)
                act.activation(uT[:, :, bass.ds(t * P + PAD, P)], ps_turn[:, s, :, :], ACT.Copy).then_inc(copied, 1)

            copy(0, 0, 0)
            with act.Fori(0, (SEQ // P - 2) // 2) as j:
                copy(j * 2 + 1, 1, j)
                copy(j * 2 + 2, 0, j)
            copy(SEQ // P - 1, 1, 0)
            act.wait_ge(turned, TILES)
            for g in range(PG):
                last = act.activation(ext[:, g, :, PSTATE:EXT], ps_turn[:, 0, g, 0:NS].rearrange("p (b s) -> p b s", b=DEC_B), ACT.Copy)
            last.then_inc(copied, 1)
            act.wait_ge(turned, TILES + 1)
            for g in range(PG):
                last = act.activation(ext[:, g, :, 0:PSTATE], ps_turn[:, 1, g, 0:DEC_B * PSTATE].rearrange("p (b t) -> p b t", b=DEC_B), ACT.Copy)
            last.then_inc(copied, 1)
            act.wait_ge(consts_in, 64)
            n_jobs = 0

            def next_hi():
                nonlocal n_jobs
                for n in range(n_jobs, min(n_jobs + 2, len(jobs))):
                    g, a, b = jobs[n]
                    act.wait_ge(mapped, n + 1)
                    if n >= 2:
                        act.wait_ge(hi_stored[n % 2], 16 * (n // 2))
                        act.wait_ge(lo_done, n - 1)
                    act.activation(res_hi[:, n % 2, 0:b - a], ps_lin[:, n % 2, 0:b - a], ACT.Copy, scale=scale[:, g:g + 1]).then_inc(hi_done, 1)
                    act.wait_ge(hi_done, n + 1)
                    act.dma_start(poolT[a // P:b // P, :, 0, g, :].rearrange("t p n -> p t n"),
                                  res_hi[:, n % 2, 0:b - a].bitcast(F32).rearrange("p (t n) -> p t n", n=P)).then_inc(hi_stored[n % 2], 16)
                n_jobs = min(n_jobs + 2, len(jobs))

            next_hi()
            for o in range(NG):
                next_hi()
                exponentials(o)
                next_hi()
                next_hi()
                next_hi()
            for s in range(2):
                act.wait_ge(hi_stored[s], 16 * len(jobs) // 2)

        @block.vector
        def _(dve):
            n_jobs = 0

            def next_lo():
                nonlocal n_jobs
                for n in range(n_jobs, min(n_jobs + 2, len(jobs))):
                    g, a, b = jobs[n]
                    dve.wait_ge(hi_done, n + 1)
                    if n >= 2:
                        dve.wait_ge(lo_stored[n % 2], 16 * (n // 2))
                    dve.scalar_tensor_tensor(res_lo[:, n % 2, 0:b - a], ps_lin[:, n % 2, 0:b - a], scale[:, g:g + 1],
                                             res_hi[:, n % 2, 0:b - a].bitcast(F32), ALU.mult, ALU.subtract).then_inc(lo_done, 1)
                n_jobs = min(n_jobs + 2, len(jobs))

            def products(o):
                g = ORDER[o]
                n = LB[g] // DIL[g] + 1
                return g, n, prod[:, 0:n * HD].rearrange("p (k d) -> p k d", d=HD)

            def scores(o):
                g, n, pr = products(o)
                dve.wait_ge(k_in, seen[g])
                dve.tensor_tensor(pr, keys[:, 0:n, :], q[:, g, :][:, None, :].broadcast_to([P, n, HD]), ALU.mult).then_inc(k_read, 1)
                next_lo()
                dve.wait_ge(k_read, o + 1)
                dve.tensor_reduce(sc[:, 0:n], pr, AX.X, ALU.add).then_inc(steps, 1)
                dve.wait_ge(steps, 3 * o + 1)
                dve.scalar_tensor_tensor(sc[:, 0:n], sc[:, 0:n], HD ** -0.5, sbias[:, g, 0:n], ALU.mult, ALU.add).then_inc(steps, 1)
                dve.wait_ge(steps, 3 * o + 2)
                dve.tensor_reduce(att_out[:, g, HD:HD + 1], sc[:, 0:n], AX.X, ALU.max).then_inc(steps, 1)
                dve.wait_ge(steps, 3 * o + 3)
                dve.tensor_scalar(nmax[:, :], att_out[:, g, HD:HD + 1], -1.0, None, ALU.mult).then_inc(negated, 1)

            def weigh(o):
                g, n, pr = products(o)
                dve.wait_ge(v_in, seen[g])
                dve.wait_ge(exped, o + 1)
                dve.tensor_tensor(pr, values[:, 0:n, :], ex[:, 0:n, None].broadcast_to([P, n, HD]), ALU.mult).then_inc(v_read, 1)
                next_lo()
                dve.wait_ge(v_read, o + 1)
                dve.tensor_reduce(att_out[:, g, 0:HD], pr.rearrange("p k d -> p d k"), AX.X, ALU.add).then_inc(attended, 1)
                next_lo()
                dve.wait_ge(attended, o + 1)

            dve.wait_ge(sbias_sem, 16)
            dve.wait_ge(q_in, 16 * HG * NG)
            n_own = 0

            def own_step(ins):
                nonlocal n_own
                n_own += 1
                ins.then_inc(own, 1)

            dve.wait_ge(consts_in, 64)
            dve.wait_ge(cleared, 1)
            dve.wait_ge(copied, TILES + 1)

            def means(g):
                if g:
                    dve.wait_ge(own, n_own)
                src, esrc = uT[:, g, :], ext[:, g, :, :]
                for level in range(g + 1):
                    d = 1 << level
                    dst, edst = sums[:, level % 2, :], esums[:, level % 2, :, :]
                    lo = 2 * d - 1
                    own_step(dve.tensor_tensor(dst[:, lo:W], src[:, lo:W], src[:, lo - d:W - d], ALU.add))
                    own_step(dve.tensor_tensor(edst[:, :, lo:EXT], esrc[:, :, lo:EXT], esrc[:, :, lo - d:EXT - d], ALU.add))
                    dve.wait_ge(own, n_own)
                    src, esrc = dst, edst
                w = 2 << g
                own_step(dve.tensor_tensor(head[:, g, :], src[:, PAD:2 * PAD], inv[:, g, :], ALU.mult))
                own_step(dve.scalar_tensor_tensor(zT[:, g, 0:SEQ], src[:, PAD:W], 1.0 / w, uT[:, g, PAD:W], ALU.mult, ALU.subtract))
                own_step(dve.scalar_tensor_tensor(zT[:, g, SEQ:SEQ + NS].rearrange("p (b s) -> p b s", b=DEC_B), esrc[:, :, PSTATE:EXT], 1.0 / w,
                                                  ext[:, g, :, PSTATE:EXT], ALU.mult, ALU.subtract))
                dve.wait_ge(own, n_own)
                dve.tensor_tensor(zT[:, g, 0:PAD], head[:, g, :], uT[:, g, PAD:2 * PAD], ALU.subtract).then_inc(mixed, 1)

            for g in range(PG - 1):
                means(g)
            scores(0)
            means(PG - 1)
            next_lo()
            weigh(0)
            for o in (1, 2):
                scores(o)
                next_lo()
                weigh(o)


def merge_and_route(nc, x, z, att, poolT, w_pa, w_pb, w_o, ln2, w_rg, b_rg, w_re, b_re, ident_in, h_out, xn_out, logits_out):
    NL = EG + NE
    with ExitStack() as ctx:
        m = Memory(nc, ctx, "merge")
        KA, KP = GW // P, PW // P
        RAW = 4
        KW = KA + KP + KC
        w_raw = m.sb("w_raw", [P, RAW, D])
        w_hi = m.sb("w_hi", [P, KW, D], F32R)
        w_lo = m.sb("w_lo", [P, KW, D], F32R)
        w_r = m.sb("w_r", [P, KC, NL])
        bias_r = m.sb("bias_r", [P, NL])
        lnrow = m.sb("lnrow", [P, D])
        ident = m.sb("ident", [P, P])
        eps = m.sb("eps", [P, 1])
        a_in = m.sb("a_in", [P, 2, NG, HG, HD + 2])
        p_in = m.sb("p_in", [P, 2, 2, PG, P], F32R)
        gates = m.sb("gates", [P, 2, D])
        xh = m.sb("xh", [P, 2, D])
        mx = m.sb("mx", [P, HG])
        wt = m.sb("wt", [P, NG, HG])
        den = m.sb("den", [P, HG])
        a_mix = m.sb("a_mix", [P, GW])
        aT = m.sb("aT", [P, 2, KA, P], F32R)
        mix = m.sb("mix", [P, D])
        mT = m.sb("mT", [P, 2, KC, P], F32R)
        xn = m.sb("xn", [P, D])
        junk = m.sb("junk", [P, D])
        xnT = m.sb("xnT", [P, KC, P])
        ss = m.sb("ss", [P, 1])
        rms = m.sb("rms", [P, 1])
        rstd = m.sb("rstd", [P, 1])
        logits = m.sb("logits", [P, 2, NL])
        ps_turn = m.ps("turn", [P, 2, 512])
        ps_a = m.ps("a_ps", [P, 2, 512])
        ps_p = m.ps("p_ps", [P, 2, 512])
        ps_o = m.ps("o_ps", [P, 2, 512])
        consts_in = m.sem("consts_in")
        eps_set = m.sem("eps_set")
        w_in_sem = [m.sem(f"w_in{i}") for i in range(RAW)]
        w_hi_done = m.sem("w_hi_done")
        w_lo_done = m.sem("w_lo_done")
        a_loaded = [m.sem(f"a_loaded{s}") for s in range(2)]
        g_loaded = m.sem("g_loaded")
        x_loaded = [m.sem(f"x_loaded{s}") for s in range(2)]
        p_loaded = [m.sem(f"p_loaded{s}") for s in range(2)]
        mx_done = m.sem("mx_done")
        lowered = m.sem("lowered")
        weights = m.sem("weights")
        own = m.sem("own")
        a_mixed = m.sem("a_mixed")
        a_turned = m.sem("a_turned")
        a_hi = m.sem("a_hi")
        a_split = m.sem("a_split")
        a_product = m.sem("a_product")
        p_product = m.sem("p_product")
        gated = m.sem("gated")
        mixed = m.sem("mixed")
        m_turned = m.sem("m_turned")
        m_hi = m.sem("m_hi")
        m_split = m.sem("m_split")
        o_product = m.sem("o_product")
        h_done = m.sem("h_done")
        squared = m.sem("squared")
        rooted = m.sem("rooted")
        inverted = m.sem("inverted")
        normed = m.sem("normed")
        n_turned = m.sem("n_turned")
        n_copied = m.sem("n_copied")
        l_product = m.sem("l_product")
        l_done = m.sem("l_done")
        h_stored = [m.pool_sem(f"h_stored{s}") for s in range(2)]
        n_stored = m.pool_sem("n_stored")
        l_stored = m.pool_sem("l_stored")
        block = m.block()

        def there(t):
            return not isinstance(t, int) or 0 <= t < TILES

        w_rows = [(w_pa, c) for c in range(KA)] + [(w_pb, c) for c in range(KP)] + [(w_o, c) for c in range(KC)]

        @block.sync
        def _(sp):
            for dst, src in ((ident[:, :], ident_in), (lnrow[:, :], ln2[None, :].partition_broadcast(P)),
                             (bias_r[:, 0:EG], b_rg[None, :].partition_broadcast(P)),
                             (bias_r[:, EG:NL], b_re[None, :].partition_broadcast(P)),
                             (w_r[:, :, 0:EG], w_rg.rearrange("(c p) n -> p c n", p=P)),
                             (w_r[:, :, EG:NL], w_re.rearrange("(c p) n -> p c n", p=P))):
                sp.dma_start(dst, src).then_inc(consts_in, 16)
            for i, (w, c) in enumerate(w_rows):
                wait(sp, w_lo_done, i + 1 - RAW)
                sp.dma_start(w_raw[:, i % RAW, :], w[c * P:(c + 1) * P, :]).then_inc(w_in_sem[i % RAW], 16)

            def load(t, s, k):
                wait_apart(sp, a_mixed, t - 1, (consts_in, 96))
                sp.dma_start(a_in[:, s].rearrange("p g h e -> p g (h e)"), att[:, rows(t), :].rearrange("g p e -> p g e")).then_inc(a_loaded[s], 16)
                wait_apart(sp, p_product, t - 1, (consts_in, 96))
                sp.dma_start(p_in[:, s].bitcast(F32), poolT[t]).then_inc(p_loaded[s], 16)
                wait_apart(sp, mixed, t, (consts_in, 96))
                sp.dma_start(gates[:, 0, :], z["ga"][rows(t), :]).then_inc(g_loaded, 16)
                sp.dma_start(gates[:, 1, :], z["gb"][rows(t), :]).then_inc(g_loaded, 16)
                wait_apart(sp, normed, t - 1, (consts_in, 96))
                if not (isinstance(t, int) and t < 2):
                    wait_apart(sp, h_stored[s], 16 * k, (consts_in, 96))
                sp.dma_start(xh[:, s, :], x[rows(t), :]).then_inc(x_loaded[s], 16)
            by_twos(sp, TILES, load)

        @block.gpsimd
        def _(pool):
            pool.memset(eps[:, :], EPS).then_inc(eps_set, 1)

            def store(t, s, k):
                wait_apart(pool, h_done, t + 1, (eps_set, 1))
                pool.dma_start(h_out[rows(t), :], xh[:, s, :]).then_inc(h_stored[s], 16)
                wait_apart(pool, normed, t + 1, (eps_set, 1))
                pool.dma_start(xn_out[rows(t), :], xn[:, :]).then_inc(n_stored, 16)
                wait_apart(pool, l_done, t + 1, (eps_set, 1))
                pool.dma_start(logits_out[rows(t), :], logits[:, s, :]).then_inc(l_stored, 16)
            by_twos(pool, TILES, store)
            pool.wait_ge(n_stored, 16 * TILES)
            pool.wait_ge(l_stored, 16 * TILES)
            for s in range(2):
                pool.wait_ge(h_stored[s], 16 * ((TILES + 1 - s) // 2))

        @block.tensor
        def _(pe):
            def product(ps, lhs, c0, chunks, n):
                for c in chunks:
                    for i, (part, w) in enumerate(((0, w_hi), (0, w_lo), (1, w_hi))):
                        for b in range(2):
                            last = pe.matmul(ps[:, b, :], lhs(part, c), w[:, c0 + c, b * 512:(b + 1) * 512],
                                             start=(c == 0 and i == 0), stop=(c == n - 1 and i == 2))
                return last

            def turn(src, n, done):
                for c in range(n):
                    last = pe.transpose(ps_turn[:, c // 4, (c % 4) * P:(c % 4 + 1) * P], src[:, c * P:(c + 1) * P], ident[:, :])
                last.then_inc(done, 1)

            def o_part(chunks):
                return product(ps_o, lambda i, c: mT[:, i, c, :], KA + KP, chunks, KC)

            pe.wait_ge(consts_in, 96)
            pe.wait_ge(w_lo_done, KW)

            def step(t, s, k):
                if there(t - 1):
                    pe.wait_ge(mixed, t)
                    wait(pe, l_done, t - 2)
                    turn(mix, KC, m_turned)
                if there(t):
                    pe.wait_ge(p_loaded[s], 16 * k + 16)
                    wait(pe, gated, 2 * t - 1)
                    product(ps_p, lambda i, c: p_in[:, s, i, c, :], KA, range(KP), KP).then_inc(p_product, 1)
                    pe.wait_ge(a_mixed, t + 1)
                    wait(pe, m_split, t)
                    turn(a_mix, KA, a_turned)
                if there(t - 1):
                    pe.wait_ge(m_split, t)
                    wait(pe, h_done, t - 1)
                    o_part(range(KC // 2))
                if there(t):
                    pe.wait_ge(a_split, t + 1)
                    wait(pe, gated, 2 * t)
                    product(ps_a, lambda i, c: aT[:, i, c, :], 0, range(KA), KA).then_inc(a_product, 1)
                if there(t - 2):
                    pe.wait_ge(normed, t - 1)
                    turn(xn, KC, n_turned)
                if there(t - 1):
                    o_part(range(KC // 2, KC)).then_inc(o_product, 1)
                if there(t - 2):
                    pe.wait_ge(n_copied, t - 1)
                    for c in range(KC):
                        last = pe.matmul(ps_turn[:, 0, 0:NL], xnT[:, c, :], w_r[:, c, :], start=(c == 0), stop=(c == KC - 1))
                    last.then_inc(l_product, 1)
            by_twos(pe, TILES, step, peeled=2)
            step(TILES, 1, 0)
            step(TILES + 1, 0, 0)

        @block.scalar
        def _(act):
            act.wait_ge(eps_set, 1)
            for i in range(KW):
                act.wait_ge(w_in_sem[i % RAW], 16 * (i // RAW + 1))
                act.activation(w_hi[:, i, :], w_raw[:, i % RAW, :], ACT.Copy).then_inc(w_hi_done, 1)

            def norm(t, s):
                act.wait_ge(h_done, t + 1)
                act.activation(junk[:, :], xh[:, s, :], ACT.Square, accum_out=ss[:, :]).then_inc(squared, 1)
                act.wait_ge(squared, t + 1)
                wait(act, inverted, t)
                act.activation(rms[:, :], ss[:, :], ACT.Sqrt, bias=eps[:, 0:1], scale=1.0 / D).then_inc(rooted, 1)

            def weigh(t):
                act.wait_ge(lowered, t + 1)
                act.activation(wt[:, :, :], wt[:, :, :], ACT.Exp).then_inc(weights, 1)

            weigh(0)

            def step(t, s, k):
                if there(t - 1):
                    act.wait_ge(m_turned, t)
                    wait(act, o_product, t - 1)
                    act.activation(mT[:, 0, :, :].rearrange("p (b c) n -> p b (c n)", b=2), ps_turn[:, :, :], ACT.Copy).then_inc(m_hi, 1)
                if there(t):
                    act.wait_ge(a_turned, t + 1)
                    wait(act, a_product, t)
                    act.activation(aT[:, 0, :, :].rearrange("p c n -> p (c n)"), ps_turn[:, 0, 0:GW], ACT.Copy).then_inc(a_hi, 1)
                if there(t) and there(t + 1):
                    weigh(t + 1)
                if there(t - 2):
                    act.wait_ge(n_turned, t - 1)
                    wait(act, l_product, t - 2)
                    act.activation(xnT[:, :, :].rearrange("p (b c) n -> p b (c n)", b=2), ps_turn[:, :, :], ACT.Copy).then_inc(n_copied, 1)
                if there(t - 1):
                    norm(t - 1, 1 - s)
            by_twos(act, TILES, step, peeled=2)
            step(TILES, 1, 0)
            step(TILES + 1, 0, 0)

        @block.vector
        def _(dve):
            dve.wait_ge(consts_in, 96)
            for i in range(KW):
                dve.wait_ge(w_hi_done, i + 1)
                dve.tensor_tensor(w_lo[:, i, :], w_raw[:, i % RAW, :], w_hi[:, i, :].bitcast(F32), ALU.subtract).then_inc(w_lo_done, 1)

            def combine(t, s, k):
                a = a_in[:, s]
                dve.wait_ge(a_loaded[s], 16 * k + 16)
                dve.tensor_reduce(mx[:, :], a[:, :, :, HD].rearrange("p g h -> p h g"), AX.X, ALU.max).then_inc(mx_done, 1)
                dve.wait_ge(mx_done, t + 1)
                wait(dve, own, 5 * t)
                dve.tensor_tensor(wt[:, :, :], a[:, :, :, HD], mx[:, None, :].broadcast_to([P, NG, HG]), ALU.subtract).then_inc(lowered, 1)
                dve.wait_ge(weights, t + 1)
                dve.tensor_tensor(a[:, :, :, HD + 1], a[:, :, :, HD + 1], wt[:, :, :], ALU.mult).then_inc(own, 1)
                dve.wait_ge(own, 5 * t + 1)
                dve.tensor_reduce(den[:, :], a[:, :, :, HD + 1].rearrange("p g h -> p h g"), AX.X, ALU.add).then_inc(own, 1)
                dve.wait_ge(own, 5 * t + 2)
                dve.reciprocal(den[:, :], den[:, :]).then_inc(own, 1)
                dve.wait_ge(own, 5 * t + 3)
                dve.tensor_tensor(wt[:, :, :], wt[:, :, :], den[:, None, :].broadcast_to([P, NG, HG]), ALU.mult).then_inc(own, 1)
                dve.wait_ge(own, 5 * t + 4)
                for g in range(NG):
                    last = dve.tensor_tensor(a[:, g, :, 0:HD], a[:, g, :, 0:HD], wt[:, g, :, None].broadcast_to([P, HG, HD]), ALU.mult)
                last.then_inc(own, 1)
                dve.wait_ge(own, 5 * t + 5)
                wait(dve, a_turned, t)
                dve.tensor_reduce(a_mix[:, :].rearrange("p (h d) -> p h d", d=HD), a[:, :, :, 0:HD].rearrange("p g h d -> p h d g"),
                                  AX.X, ALU.add).then_inc(a_mixed, 1)

            def split_a(t):
                dve.wait_ge(a_hi, t + 1)
                dve.tensor_tensor(aT[:, 1, :, :].rearrange("p c n -> p (c n)"), ps_turn[:, 0, 0:GW],
                                  aT[:, 0, :, :].bitcast(F32).rearrange("p c n -> p (c n)"), ALU.subtract).then_inc(a_split, 1)

            def halves(ap):
                return ap.rearrange("p (b n) -> p b n", b=2)

            combine(0, 0, 0)

            def step(t, s, k):
                if there(t - 1):
                    dve.wait_ge(m_hi, t)
                    dve.tensor_tensor(mT[:, 1, :, :].rearrange("p (b c) n -> p b (c n)", b=2), ps_turn[:, :, :],
                                      mT[:, 0, :, :].bitcast(F32).rearrange("p (b c) n -> p b (c n)", b=2), ALU.subtract).then_inc(m_split, 1)
                if there(t):
                    dve.wait_ge(g_loaded, 32 * (t + 1))
                    dve.wait_ge(p_product, t + 1)
                    dve.tensor_tensor(halves(gates[:, 1, :]), halves(gates[:, 1, :]), ps_p[:, :, :], ALU.mult).then_inc(gated, 1)
                    split_a(t)
                if there(t) and there(t + 1):
                    combine(t + 1, 1 - s, k + s)
                if there(t):
                    dve.wait_ge(a_product, t + 1)
                    dve.tensor_tensor(halves(gates[:, 0, :]), halves(gates[:, 0, :]), ps_a[:, :, :], ALU.mult).then_inc(gated, 1)
                    dve.wait_ge(gated, 2 * (t + 1))
                    wait(dve, m_turned, t)
                    dve.tensor_tensor(mix[:, :], gates[:, 0, :], gates[:, 1, :], ALU.add).then_inc(mixed, 1)
                if there(t - 1):
                    dve.wait_ge(o_product, t)
                    dve.wait_ge(x_loaded[1 - s], 16 * (k + s))
                    dve.tensor_tensor(halves(xh[:, 1 - s, :]), halves(xh[:, 1 - s, :]), ps_o[:, :, :], ALU.add).then_inc(h_done, 1)
                if there(t - 2):
                    dve.wait_ge(l_product, t - 1)
                    wait(dve, l_stored, 16 * (t - 3))
                    dve.tensor_tensor(logits[:, s, :], ps_turn[:, 0, 0:NL], bias_r[:, :], ALU.add).then_inc(l_done, 1)
                if there(t - 1):
                    dve.wait_ge(rooted, t)
                    dve.reciprocal(rstd[:, :], rms[:, :]).then_inc(inverted, 1)
                    dve.wait_ge(inverted, t)
                    wait(dve, n_turned, t - 1)
                    wait(dve, n_stored, 16 * (t - 1))
                    dve.scalar_tensor_tensor(xn[:, :], xh[:, 1 - s, :], rstd[:, 0:1], lnrow[:, :], ALU.mult, ALU.mult).then_inc(normed, 1)
            by_twos(dve, TILES, step, peeled=2)
            step(TILES, 1, TILES // 2)
            step(TILES + 1, 0, TILES // 2 + 1)


class RawWeights:

    def __init__(self, nc, ctx, w_gate, w_up, w_down):
        self.m = Memory(nc, ctx, "raw")
        self.gu = self.m.sb("gu", [P, KC, 2, FE])
        self.d = self.m.sb("d", [P, FC, D])
        self.loaded = [self.m.sem(f"loaded{i}") for i in range(4)]
        self.weights = w_gate, w_up, w_down

    def load(self, sp, e, wait_for_part):
        w_gate, w_up, w_down = self.weights
        for i in range(2):
            wait_for_part(i)
            for b, w in enumerate((w_gate, w_up)):
                src = w[bass.ds(e, 1), i * 512:(i + 1) * 512, :].rearrange("o (c p) n -> p (o c) n", p=P)
                sp.dma_start(self.gu[:, 4 * i:4 * i + 4, b, :], src).then_inc(self.loaded[i], 16)
        for i in range(2):
            wait_for_part(2 + i)
            src = w_down[bass.ds(e, 1), i * 256:(i + 1) * 256, :].rearrange("o (c p) n -> p (o c) n", p=P)
            sp.dma_start(self.d[:, 2 * i:2 * i + 2, :], src).then_inc(self.loaded[2 + i], 16)


def routing(nc, logits_in, a, slots, weight_out, counts_out, over_out, pairs, raw):
    PADT, PADE = 16, 16
    with ExitStack() as ctx:
        m = Memory(nc, ctx, "route")
        lg = m.sb("lg", [P, TILES, EG + NE])
        ones = m.sb("ones", [P, P])
        before = m.sb("before", [P, P])
        real = m.sb("real", [P, TILES])
        first_g = m.sb("first_g", [P, EG])
        first_e = m.sb("first_e", [P, NE])
        block_no = m.sb("block_no", [P, OVER, NE])
        entry = m.sb("entry", [P, 2, TILES, SLOT], I32)
        zero = m.sb("zero", [P, BLOCKS * SLOT], I32)
        g4 = [m.sb(f"g4_{i}", [P, TILES, EG]) for i in range(3)]
        t1 = [m.sb(f"t1_{i}", [P, TILES]) for i in range(8)]
        el = m.sb("el", [P, TILES, NE])
        e1 = m.sb("e1", [P, TILES, NE])
        e2 = m.sb("e2", [P, TILES, NE])
        tmp = m.sb("tmp", [P, TILES, NE])
        counts = m.sb("counts", [P, 2, PADT + TILES, NE])
        tile_count = m.sb("tile_count", [P, TILES, NE])
        ends = m.sb("ends", [P, 2, PADE + NE])
        nblk = m.sb("nblk", [P, NE])
        nblk_i = m.sb("nblk_i", [P, NE], I32)
        start = m.sb("start", [P, NE])
        where = m.sb("where", [P, TILES, NE])
        dest_f = m.sb("dest_f", [P, TILES, 2])
        dest = m.sb("dest", [P, 2, TILES], I32)
        weight = m.sb("weight", [P, TILES, 2])
        owner = m.sb("owner", [P, OVER + 1])
        owner_i = m.sb("owner_i", [P, OVER + 1], I32)
        total_i = m.sb("total_i", [P, 2, NE], I32)
        second = m.sb("second", [P, 2, PADE + NE])
        beyond = m.sb("beyond", [P, TILES, NE])
        base = m.sb("base", [P, NE])
        NT = TILES * NE
        HALF = (TILES + 1) // 2
        ps_sum = m.ps("sum_ps", [P, 2, 512])
        ps_rank = m.ps("rank_ps", [P, 2, 512])
        loaded = m.sem("loaded")
        cleared = m.sem("cleared")
        own = m.sem("own")
        copied = m.sem("copied")
        lowered = m.sem("lowered")
        exped = m.sem("exped")
        chosen = m.sem("chosen")
        counted = m.sem("counted")
        placed = m.sem("placed")
        zeroed = m.pool_sem("zeroed")
        scattered = m.pool_sem("scattered")
        stored = m.sem("stored")
        m.sems += raw.m.sems
        block = m.block()

        @block.sync
        def _(sp):
            for dst, src in ((lg[:, :, :], logits_in.rearrange("(t p) n -> p t n", p=P)), (ones[:, :], a["ones"]),
                             (before[:, :], a["before"]), (real[:, :], a["real"]), (first_g[:, :], a["first_group"]),
                             (first_e[:, :], a["first_expert"]), (block_no[:, :, :], a["block_no"]), (base[:, :], a["base"]), (entry[:, :, :, :], a["entry"])):
                sp.dma_start(dst, src).then_inc(loaded, 16)
            raw.load(sp, 0, lambda part: None)
            sp.wait_ge(placed, 1)
            sp.dma_start(weight_out.rearrange("(t p) k -> p t k", p=P), weight[:, :, :], allow_slow_non_contiguous=True).then_inc(stored, 16)
            sp.dma_start(over_out, owner_i[0:1, :]).then_inc(stored, 16)
            sp.dma_start(counts_out, total_i[0:1, :, :].rearrange("p a e -> p (a e)")).then_inc(stored, 16)
            sp.wait_ge(stored, 48)

        @block.gpsimd
        def _(pool):
            pool.memset(zero[:, :], 0).then_inc(cleared, 1)
            pool.memset(counts[:, :, 0:PADT, :], 0.0)
            pool.memset(second[:, :, 0:PADE], 0.0)
            pool.memset(ends[:, :, 0:PADE], 0.0).then_inc(cleared, 1)
            pool.wait_ge(cleared, 2)
            pool.dma_start(slots.rearrange("(p b) e -> p (b e)", p=P), zero[:, :]).then_inc(zeroed, 16)
            pool.wait_ge(zeroed, 16)
            pool.wait_ge(placed, 1)
            pool.wait_ge(loaded, 144)
            for t in range(TILES):
                n = P if t < TILES - 1 else NS
                for k in range(2):
                    pool.indirect_dma_start(out=slots, out_offset=bass.IndirectOffsetOnAxis(ap=dest[0:n, k, t:t + 1], axis=0),
                                            in_=entry[0:n, k, t, :], in_offset=None).then_inc(scattered, 16)
            pool.wait_ge(scattered, 16 * 2 * TILES)

        @block.scalar
        def _(act):
            for dst, src in pairs:
                act.dma_start(dst, src).then_inc(copied, 16)
            act.wait_ge(lowered, 1)
            act.activation(g4[1][:, :, :], g4[1][:, :, :], ACT.Exp).then_inc(exped, 1)
            act.wait_ge(lowered, 2)
            act.activation(t1[5][:, :], t1[5][:, :], ACT.Exp).then_inc(exped, 1)
            act.wait_ge(copied, 16 * len(pairs))

        @block.tensor
        def _(pe):
            pe.wait_ge(loaded, 144)
            pe.wait_ge(chosen, 1)
            for i, (a0, b0) in enumerate(((0, HALF), (HALF, TILES))):
                flat = tmp[:, a0:b0, :].rearrange("p t e -> p (t e)")
                w = (b0 - a0) * NE
                pe.matmul(ps_sum[:, i, 0:w], ones[:, :], flat, start=True, stop=True)
                last = pe.matmul(ps_rank[:, i, 0:w], before[:, :], flat, start=True, stop=True)
            last.then_inc(counted, 1)

        @block.vector
        def _(dve):
            n_own = 0

            def then(ins):
                nonlocal n_own
                n_own += 1
                ins.then_inc(own, 1)
                dve.wait_ge(own, n_own)

            def over(ap, n):
                return ap[:, :, None].broadcast_to([P, TILES, n])

            def table(ap, n):
                return ap[:, None, :].broadcast_to([P, TILES, n])

            def pick_first(out, values, best, order, n, scratch):
                then(dve.tensor_tensor(out, values, over(best, n), ALU.is_equal))
                then(dve.tensor_tensor(out, out, table(order, n), ALU.mult))
                then(dve.tensor_reduce(scratch, out, AX.X, ALU.max))
                then(dve.tensor_tensor(out, out, over(scratch, n), ALU.is_equal))

            dve.wait_ge(loaded, 144)
            dve.wait_ge(cleared, 2)
            gl = lg[:, :, 0:EG]
            then(dve.tensor_reduce(t1[0][:, :], gl, AX.X, ALU.max))
            dve.tensor_tensor(g4[1][:, :, :], gl, over(t1[0][:, :], EG), ALU.subtract).then_inc(lowered, 1)
            pick_first(g4[0][:, :, :], gl, t1[0][:, :], first_g[:, :], EG, t1[1][:, :])
            then(dve.tensor_scalar(g4[2][:, :, :], g4[0][:, :, :], 1.0, 1e30, ALU.subtract, ALU.mult))
            for g in range(EG):
                here = slice(g * EPG, (g + 1) * EPG)
                then(dve.tensor_tensor(el[:, :, here], lg[:, :, EG + g * EPG:EG + (g + 1) * EPG], over(g4[0][:, :, g], EPG), ALU.mult))
                then(dve.tensor_tensor(el[:, :, here], el[:, :, here], over(g4[2][:, :, g], EPG), ALU.add))
            then(dve.tensor_reduce(t1[2][:, :], el[:, :, :], AX.X, ALU.max))
            pick_first(e1[:, :, :], el[:, :, :], t1[2][:, :], first_e[:, :], NE, t1[1][:, :])
            then(dve.scalar_tensor_tensor(tmp[:, :, :], e1[:, :, :], -3e38, el[:, :, :], ALU.mult, ALU.add))
            then(dve.tensor_reduce(t1[3][:, :], tmp[:, :, :], AX.X, ALU.max))
            pick_first(e2[:, :, :], tmp[:, :, :], t1[3][:, :], first_e[:, :], NE, t1[1][:, :])
            dve.tensor_tensor(t1[5][:, :], t1[3][:, :], t1[2][:, :], ALU.subtract).then_inc(lowered, 1)
            then(dve.tensor_tensor(e1[:, :, :], e1[:, :, :], over(real[:, :], NE), ALU.mult))
            then(dve.tensor_tensor(e2[:, :, :], e2[:, :, :], over(real[:, :], NE), ALU.mult))
            dve.tensor_tensor(tmp[:, :, :], e1[:, :, :], e2[:, :, :], ALU.add).then_inc(chosen, 1)
            dve.wait_ge(exped, 2)
            then(dve.tensor_reduce(t1[4][:, :], g4[1][:, :, :], AX.X, ALU.add))
            then(dve.scalar_tensor_tensor(t1[6][:, :], t1[5][:, :], 1.0, t1[4][:, :], ALU.add, ALU.mult))
            then(dve.reciprocal(weight[:, :, 0], t1[6][:, :]))
            then(dve.tensor_tensor(weight[:, :, 1], weight[:, :, 0], t1[5][:, :], ALU.mult))
            dve.wait_ge(counted, 1)
            for i, (a0, b0) in enumerate(((0, HALF), (HALF, TILES))):
                w = (b0 - a0) * NE
                then(dve.tensor_copy(tile_count[:, a0:b0, :], ps_sum[:, i, 0:w].rearrange("p (t e) -> p t e", e=NE)))
            then(dve.tensor_copy(counts[:, 0, PADT:, :], tile_count[:, :, :]))
            cur = 0
            for d in (1, 2, 4, 8, 16):
                then(dve.tensor_tensor(counts[:, 1 - cur, PADT:, :], counts[:, cur, PADT:, :], counts[:, cur, PADT - d:PADT + TILES - d, :], ALU.add))
                cur = 1 - cur
            total = counts[:, cur, PADT + TILES - 1, :]
            then(dve.tensor_copy(total_i[:, 0, :], total))
            then(dve.tensor_scalar(second[:, 0, PADE:], total, float(P), None, ALU.is_gt))
            sc = 0
            for d in (1, 2, 4, 8, 16):
                then(dve.tensor_tensor(second[:, 1 - sc, PADE:], second[:, sc, PADE:], second[:, sc, PADE - d:PADE + NE - d], ALU.add))
                sc = 1 - sc
            then(dve.tensor_copy(total_i[:, 1, :], second[:, sc, PADE:]))
            then(dve.tensor_scalar(nblk[:, :], total, float(P - 1), None, ALU.add))
            then(dve.tensor_copy(nblk_i[:, :], nblk[:, :]))
            then(dve.tensor_scalar(nblk_i[:, :], nblk_i[:, :], 7, None, ALU.logical_shift_right))
            then(dve.tensor_copy(nblk[:, :], nblk_i[:, :]))
            then(dve.tensor_scalar(nblk[:, :], nblk[:, :], 2.0, 0.0, ALU.subtract, ALU.max))
            then(dve.tensor_copy(ends[:, 0, PADE:], nblk[:, :]))
            ec = 0
            for d in (1, 2, 4, 8, 16):
                then(dve.tensor_tensor(ends[:, 1 - ec, PADE:], ends[:, ec, PADE:], ends[:, ec, PADE - d:PADE + NE - d], ALU.add))
                ec = 1 - ec
            then(dve.tensor_tensor(start[:, :], ends[:, ec, PADE:], nblk[:, :], ALU.subtract))
            then(dve.tensor_tensor(where[:, :, :], counts[:, cur, PADT:, :], tile_count[:, :, :], ALU.subtract))
            for i, (a0, b0) in enumerate(((0, HALF), (HALF, TILES))):
                w = (b0 - a0) * NE
                then(dve.tensor_tensor(where[:, a0:b0, :], where[:, a0:b0, :], ps_rank[:, i, 0:w].rearrange("p (t e) -> p t e", e=NE), ALU.add))
            then(dve.tensor_scalar(beyond[:, :, :], where[:, :, :], float(2 * P), None, ALU.is_ge))
            then(dve.tensor_tensor(where[:, :, :], where[:, :, :], table(base[:, :], NE), ALU.add))
            then(dve.tensor_scalar(start[:, :], start[:, :], float(P), float((NE - 1) * 2 * P), ALU.mult, ALU.add))
            then(dve.tensor_tensor(start[:, :], start[:, :], base[:, :], ALU.subtract))
            then(dve.tensor_tensor(beyond[:, :, :], beyond[:, :, :], table(start[:, :], NE), ALU.mult))
            then(dve.tensor_tensor(where[:, :, :], where[:, :, :], beyond[:, :, :], ALU.add))
            for k, e in enumerate((e1, e2)):
                then(dve.tensor_tensor(tmp[:, :, :], where[:, :, :], e[:, :, :], ALU.mult))
                then(dve.tensor_reduce(dest_f[:, :, k], tmp[:, :, :], AX.X, ALU.add))
                then(dve.tensor_copy(dest[:, k, :], dest_f[:, :, k]))
            last_e = ends[:, ec, PADE:][:, None, :].broadcast_to([P, OVER, NE])
            then(dve.tensor_tensor(block_no[:, :, :], last_e, block_no[:, :, :], ALU.is_le))
            then(dve.tensor_reduce(owner[:, 1:], block_no[:, :, :], AX.X, ALU.add))
            then(dve.tensor_scalar(owner[:, 1:], owner[:, 1:], float(NE - 1), None, ALU.min))
            then(dve.tensor_copy(owner[:, 0:1], ends[:, ec, PADE + NE - 1:PADE + NE]))
            dve.tensor_copy(owner_i[:, :], owner[:, :]).then_inc(placed, 1)


def experts(nc, xn, slots, counts_in, raw, ident_in, y_tok):
    U = 12
    with ExitStack() as ctx:
        m = Memory(nc, ctx, "moe")
        ident = m.sb("ident", [P, P])
        counts = m.sb("counts", [1, 2 * NE], I32)
        raw_gu, raw_d, raw_in = raw.gu, raw.d, raw.loaded
        gu_hi = m.sb("gu_hi", [P, KC, 2, 2, FE // 2], F32R)
        gu_lo = m.sb("gu_lo", [P, KC, 2, 2, FE // 2], F32R)
        d_hi = m.sb("d_hi", [P, FC, D], F32R)
        d_lo = m.sb("d_lo", [P, FC, D], F32R)
        lists = m.sb("lists", [P, 2 * NE, SLOT], I32)
        rows_in = m.sb("rows_in", [P, 2, 2], I32)
        rows_out = m.sb("rows_out", [P, 2, 2], I32)
        ps_turn = m.ps("turn", [P, 2, 512])
        ps_gu = m.ps("gu", [P, 2, 2, FE // 2])
        ps_y = m.ps("y_ps", [P, 2, 512])
        ps_h = m.ps("h_ps", [P, 2, 512])
        consts_in = m.sem("consts_in")
        w_hi = m.sem("w_hi")
        w_lo = m.sem("w_lo")
        passed = m.sem("passed")
        lists_in = m.sem("lists_in")
        picked = m.sem("picked")

        class Kind:

            def __init__(self, f, number):
                self.number = number
                self.xg = m.sb(f"xg_{f}", [P, D])
                self.xT = m.sb(f"xT_{f}", [P, 2, KC, P], F32R)
                self.sig = m.sb(f"sig_{f}", [P, 2, FE // 2])
                self.hid = m.sb(f"hid_{f}", [P, 2, FE // 2])
                self.hT = m.sb(f"hT_{f}", [P, 2, FC, P], F32R)
                self.y = m.sb(f"y_{f}", [P, D])
                self.x_in = m.pool_sem(f"x_in_{f}")
                self.x_turned = m.sem(f"x_turned_{f}")
                self.x_hi = m.sem(f"x_hi_{f}")
                self.x_lo = m.sem(f"x_lo_{f}")
                self.used = m.sem(f"used_{f}")
                self.sigged = m.sem(f"sigged_{f}")
                self.gated = m.sem(f"gated_{f}")
                self.hidden = m.sem(f"hidden_{f}")
                self.h_turned = m.sem(f"h_turned_{f}")
                self.h_hi = m.sem(f"h_hi_{f}")
                self.h_lo = m.sem(f"h_lo_{f}")
                self.y_copied = m.sem(f"y_copied_{f}")
                self.stored = m.pool_sem(f"stored_{f}")

        X, M = Kind("x", 1), Kind("m", 0)
        X.y_free = m.sem("y_free_x")
        block = m.block()

        def loop(eng, body):
            body(0, 0, 0)
            body(1, 1, 0)
            with eng.Fori(1, NE // 2 - 1) as j:
                body(j * 2, 0, j)
                body(j * 2 + 1, 1, j)
            body(NE - 2, 0, NE // 2 - 1)
            body(NE - 1, 1, NE // 2 - 1)

        def x_blocks(eng, e):
            return eng.value_load(counts[0:1, bass.ds(e + NE, 1)], min_val=1, max_val=NE)

        def is_last(e):
            return isinstance(e, int) and e == NE - 1

        def if_x(eng, e, do, otherwise):
            count = eng.value_load(counts[0:1, bass.ds(e, 1)], min_val=0, max_val=SEQ + NS)
            with eng.If(count > P):
                do()
            with eng.Else():
                otherwise()

        def x_then_m(eng, run_x, skip_x, run_m):
            def one(e, s, k):
                if_x(eng, e, lambda: run_x(e), lambda: skip_x(e))
                run_m(e)
            loop(eng, one)

        @block.sync
        def _(sp):
            sp.dma_start(ident[:, :], ident_in).then_inc(consts_in, 16)
            sp.dma_start(counts[:, :], counts_in).then_inc(consts_in, 16)
            sp.dma_start(lists[:, :, :], slots[0:2 * NE * P, :].rearrange("(b p) w -> p b w", p=P)).then_inc(lists_in, 16)

            def load(e, s, k):
                if not (isinstance(e, int) and e == 0):
                    raw.load(sp, e, lambda part: sp.wait_ge(w_lo, U * e - U + 6 + 2 * part))
            loop(sp, load)

        @block.gpsimd
        def _(pool):
            def has_x(e):
                return pool.value_load(counts[0:1, bass.ds(e, 1)], min_val=0, max_val=SEQ + NS) > P

            def pick(to, e, s, word, n):
                first = e * 2
                pool.tensor_copy(to[:, s, :], lists[:, bass.ds(first, 2), word]).then_inc(picked, 1)
                pool.wait_ge(picked, n)

            def gather(B, s):
                pool.sem_inc(passed, 1)
                pool.indirect_dma_start(out=B.xg[:, :], out_offset=None, in_=xn,
                                        in_offset=bass.IndirectOffsetOnAxis(ap=rows_in[:, s, B.number:B.number + 1], axis=0)).then_inc(B.x_in, 16)

            def scatter(B, e, s):
                pool.wait_ge(B.y_copied, e + 1)
                pool.sem_inc(passed, 1)
                pool.indirect_dma_start(out=y_tok, out_offset=bass.IndirectOffsetOnAxis(ap=rows_out[:, s, B.number:B.number + 1], axis=0),
                                        in_=B.y[:, :], in_offset=None).then_inc(B.stored, 16)

            def step(e, s, k):
                this_has_x = has_x(e)
                if not is_last(e):
                    next_has_x = has_x(e + 1)
                    pool.wait_ge(M.x_turned, e + 1)
                    wait(pool, X.x_turned, e)
                    pick(rows_in, e + 1, 1 - s, 0, e * 2 + 2)
                    gather(M, 1 - s)
                    pool.wait_ge(X.x_turned, e + 1)
                    pool.sem_inc(passed, 1)
                    with pool.If(next_has_x):
                        gather(X, 1 - s)
                wait(pool, M.stored, 16 * e)
                pick(rows_out, e, s, 1, e * 2 + 3 - is_last(e))
                pool.sem_inc(passed, 1)
                with pool.If(this_has_x):
                    scatter(X, e, s)
                    pool.wait_ge(X.stored, 16 * x_blocks(pool, e))
                pool.sem_inc(X.y_free, 1)
                scatter(M, e, s)

            pool.wait_ge(consts_in, 32)
            pool.wait_ge(lists_in, 16)
            pick(rows_in, 0, 0, 0, 1)
            gather(M, 0)
            with pool.If(has_x(0)):
                gather(X, 0)
            loop(pool, step)
            pool.wait_ge(M.stored, 16 * NE)

        def unit(i):
            if i < 8:
                half, c = i // 4, 2 * (i % 4)
                cs, cols = slice(c, c + 2), slice(half * FE // 2, (half + 1) * FE // 2)
                return gu_hi[:, cs, half, :, :], gu_lo[:, cs, half, :, :], raw_gu[:, cs, :, cols], (c // 4, 32)
            c = i - 8
            return d_hi[:, c, :], d_lo[:, c, :], raw_d[:, c, :], (2 + c // 2, 16)

        @block.tensor
        def _(pe):
            def turn_x(B, e, other, others):
                pe.wait_ge(B.x_in, 16 * (x_blocks(pe, e) if B is X else e + 1))
                wait(pe, other.x_lo, others)
                for c in range(KC):
                    last = pe.transpose(ps_turn[:, c // 4, (c % 4) * P:(c % 4 + 1) * P], B.xg[:, c * P:(c + 1) * P], ident[:, :])
                last.then_inc(B.x_turned, 1)

            def gate_up(B, e, i):
                half = i // 4
                wait(pe, w_lo, U * e + i + 1)
                for c in (2 * (i % 4), 2 * (i % 4) + 1):
                    for n, (part, w) in enumerate(((0, gu_hi), (0, gu_lo), (1, gu_hi))):
                        last = pe.matmul(ps_gu[:, half, :, :].rearrange("p a n -> p (a n)"), B.xT[:, part, c, :],
                                         w[:, c, half, :, :].rearrange("p a n -> p (a n)"),
                                         start=(c == 0 and n == 0), stop=(c == KC - 1 and n == 2))
                last.then_inc(B.used, 1)

            def turn_h(B, e, half, other, others):
                pe.wait_ge(B.hidden, 2 * e + half + 1)
                wait(pe, other.h_lo, 2 * others - 1 + half)
                for c in range(2):
                    last = pe.transpose(ps_h[:, half, c * P:(c + 1) * P], B.hid[:, half, c * P:(c + 1) * P], ident[:, :])
                last.then_inc(B.h_turned, 1)

            def down(B, e, i, other, others):
                c = i - 8
                wait(pe, w_lo, U * e + i + 1)
                if c == 0:
                    wait(pe, other.y_copied, others)
                if c % 2 == 0:
                    pe.wait_ge(B.h_lo, 2 * e + c // 2 + 1)
                for n, (part, w) in enumerate(((0, d_hi), (0, d_lo), (1, d_hi))):
                    for b in range(2):
                        last = pe.matmul(ps_y[:, b, :], B.hT[:, part, c, :], w[:, c, b * 512:(b + 1) * 512],
                                         start=(c == 0 and n == 0), stop=(c == FC - 1 and n == 2))
                last.then_inc(B.used, 1)

            def run(B, e, other, others, turn_next):
                pe.wait_ge(B.x_lo, e + 1)
                wait(pe, other.hidden, 2 * others - 1)
                for i in range(4):
                    gate_up(B, e, i)
                wait(pe, other.hidden, 2 * others)
                gate_up(B, e, 4)
                gate_up(B, e, 5)
                turn_h(B, e, 0, other, others)
                gate_up(B, e, 6)
                gate_up(B, e, 7)
                if turn_next:
                    turn_x(M, e + 1, X, e + 1)
                down(B, e, 8, other, others)
                turn_h(B, e, 1, other, others)
                down(B, e, 9, other, others)
                if turn_next:
                    if_x(pe, e + 1, lambda: turn_x(X, e + 1, M, e + 2), lambda: pe.sem_inc(X.x_turned, 1))
                down(B, e, 10, other, others)
                down(B, e, 11, other, others)

            def run_x(e):
                run(X, e, M, e, False)

            def skip_x(e):
                pe.sem_inc(X.used, U)
                pe.sem_inc(X.h_turned, 2)

            def run_m(e):
                run(M, e, X, e + 1, not is_last(e))

            pe.wait_ge(consts_in, 32)
            turn_x(M, 0, X, 0)
            if_x(pe, 0, lambda: turn_x(X, 0, M, 1), lambda: pe.sem_inc(X.x_turned, 1))
            x_then_m(pe, run_x, skip_x, run_m)

        @block.scalar
        def _(act):
            def split_hi(e, i):
                hi, _, raw, (part, n) = unit(i)
                act.wait_ge(raw_in[part], n * (e + 1))
                wait(act, M.used, U * (e - 1) + i + 1)
                act.activation(hi, raw, ACT.Copy).then_inc(w_hi, 1)

            def x_hi(B, e):
                act.wait_ge(B.x_turned, e + 1)
                wait(act, B.used, U * (e - 1) + 8)
                act.activation(B.xT[:, 0].rearrange("p (b c) n -> p b (c n)", b=2), ps_turn[:, :, :], ACT.Copy).then_inc(B.x_hi, 1)

            def sigmoid(B, e, half):
                act.wait_ge(B.used, U * e + 4 * half + 4)
                wait(act, B.hidden, 2 * e - 1 + half)
                act.activation(B.sig[:, half, :], ps_gu[:, half, 0, :], ACT.Sigmoid).then_inc(B.sigged, 1)

            def h_hi(B, e, half):
                act.wait_ge(B.h_turned, 2 * e + half + 1)
                wait(act, B.used, U * e)
                act.activation(B.hT[:, 0, 2 * half:2 * half + 2, :].rearrange("p c n -> p (c n)"), ps_h[:, half, 0:2 * P],
                               ACT.Copy).then_inc(B.h_hi, 1)

            def store_y(B, e):
                act.wait_ge(B.used, U * e + U)
                if B is X:
                    wait(act, X.y_free, e)
                else:
                    wait(act, M.stored, 16 * e)
                act.activation(B.y[:, :].rearrange("p (b n) -> p b n", b=2), ps_y[:, :, :], ACT.Copy).then_inc(B.y_copied, 1)

            def last_units(e):
                split_hi(e, 10)
                split_hi(e, 11)

            def run_x(e):
                last_units(e)
                sigmoid(X, e, 0)
                h_hi(X, e, 0)
                sigmoid(X, e, 1)
                h_hi(X, e, 1)
                store_y(X, e)

            def skip_x(e):
                act.sem_inc(X.sigged, 2)
                act.sem_inc(X.h_hi, 2)
                act.sem_inc(X.y_copied, 1)
                last_units(e)

            def run_m(e):
                def split(*units):
                    if not is_last(e):
                        for i in units:
                            split_hi(e + 1, i)
                split(0, 1, 2)
                sigmoid(M, e, 0)
                split(3, 4)
                h_hi(M, e, 0)
                split(5)
                sigmoid(M, e, 1)
                if not is_last(e):
                    x_hi(M, e + 1)
                h_hi(M, e, 1)
                split(6, 7)
                if not is_last(e):
                    if_x(act, e + 1, lambda: x_hi(X, e + 1), lambda: act.sem_inc(X.x_hi, 1))
                split(8, 9)
                store_y(M, e)

            act.wait_ge(consts_in, 32)
            for i in range(10):
                split_hi(0, i)
                if i == 4:
                    x_hi(M, 0)
                    if_x(act, 0, lambda: x_hi(X, 0), lambda: act.sem_inc(X.x_hi, 1))
            x_then_m(act, run_x, skip_x, run_m)

        @block.vector
        def _(dve):
            def split_lo(e, i):
                hi, lo, raw, _ = unit(i)
                dve.wait_ge(w_hi, U * e + i + 1)
                dve.tensor_tensor(lo, raw, hi.bitcast(F32), ALU.subtract).then_inc(w_lo, 1)

            def x_lo(B, e):
                dve.wait_ge(B.x_hi, e + 1)
                dve.tensor_tensor(B.xT[:, 1].rearrange("p (b c) n -> p b (c n)", b=2), ps_turn[:, :, :],
                                  B.xT[:, 0].bitcast(F32).rearrange("p (b c) n -> p b (c n)", b=2), ALU.subtract).then_inc(B.x_lo, 1)

            def hidden(B, e, half):
                dve.wait_ge(B.sigged, 2 * e + half + 1)
                wait(dve, B.h_turned, 2 * e - 1 + half)
                dve.tensor_tensor(B.hid[:, half, :], B.sig[:, half, :], ps_gu[:, half, 0, :], ALU.mult).then_inc(B.gated, 1)
                dve.wait_ge(B.gated, 2 * e + half + 1)
                dve.tensor_tensor(B.hid[:, half, :], B.hid[:, half, :], ps_gu[:, half, 1, :], ALU.mult).then_inc(B.hidden, 1)

            def h_lo(B, e, half):
                dve.wait_ge(B.h_hi, 2 * e + half + 1)
                part = slice(2 * half, 2 * half + 2)
                dve.tensor_tensor(B.hT[:, 1, part, :].rearrange("p c n -> p (c n)"), ps_h[:, half, 0:2 * P],
                                  B.hT[:, 0, part, :].bitcast(F32).rearrange("p c n -> p (c n)"), ALU.subtract).then_inc(B.h_lo, 1)

            def last_units(e):
                split_lo(e, 10)
                split_lo(e, 11)

            def run_x(e):
                last_units(e)
                hidden(X, e, 0)
                h_lo(X, e, 0)
                hidden(X, e, 1)
                h_lo(X, e, 1)

            def skip_x(e):
                dve.sem_inc(X.gated, 2)
                dve.sem_inc(X.hidden, 2)
                dve.sem_inc(X.h_lo, 2)
                last_units(e)

            def run_m(e):
                def split(*units):
                    if not is_last(e):
                        for i in units:
                            split_lo(e + 1, i)
                split(0, 1, 2)
                hidden(M, e, 0)
                split(3, 4)
                h_lo(M, e, 0)
                split(5)
                hidden(M, e, 1)
                if not is_last(e):
                    x_lo(M, e + 1)
                h_lo(M, e, 1)
                split(6, 7)
                if not is_last(e):
                    if_x(dve, e + 1, lambda: x_lo(X, e + 1), lambda: dve.sem_inc(X.x_lo, 1))
                split(8, 9)

            dve.wait_ge(consts_in, 32)
            for i in range(10):
                split_lo(0, i)
                if i == 4:
                    x_lo(M, 0)
                    if_x(dve, 0, lambda: x_lo(X, 0), lambda: dve.sem_inc(X.x_lo, 1))
            x_then_m(dve, run_x, skip_x, run_m)


def expert_overflow(nc, xn, slots, over_in, w_gate, w_up, w_down, ident_in, y_tok):
    with ExitStack() as ctx:
        m = Memory(nc, ctx, "over")
        ident = m.sb("ident", [P, P])
        over = m.sb("over", [1, OVER + 1], I32)
        wg = m.sb("wg", [P, KC, FE])
        wu = m.sb("wu", [P, KC, FE])
        wd = m.sb("wd", [P, FC, D])
        idx = m.sb("idx", [P, 2, SLOT], I32)
        xg = m.sb("xg", [P, D])
        xgT = m.sb("xgT", [P, KC, P])
        hid = m.sb("hid", [P, 2, FE])
        hidT = m.sb("hidT", [P, FC, P])
        y = m.sb("y", [P, D])
        ps_turn = m.ps("turn", [P, 2, 512])
        ps_gu = m.ps("gu", [P, 2, 512])
        ps_y = m.ps("y_ps", [P, 2, 512])
        consts_in = m.sem("consts_in")
        fresh = m.sem("fresh")
        w_in_sem = m.sem("w_in")
        idx_in = [m.pool_sem(f"idx_in{i}") for i in range(2)]
        x_in = m.pool_sem("x_in")
        passed = m.sem("passed")
        x_turned = m.sem("x_turned")
        x_copied = m.sem("x_copied")
        gu_done = m.sem("gu_done")
        sigged = m.sem("sigged")
        gated = m.sem("gated")
        hidden = m.sem("hidden")
        h_turned = m.sem("h_turned")
        h_copied = m.sem("h_copied")
        y_done = m.sem("y_done")
        y_copied = m.sem("y_copied")
        stored = m.pool_sem("stored")
        block = m.block()

        def each(eng, body):
            eng.wait_ge(consts_in, 32)
            n = eng.value_load(over[0:1, 0:1], min_val=0, max_val=OVER)
            with eng.If(n > 0):
                with eng.Fori(0, OVER) as j:
                    body(j)
            with eng.Else():
                eng.wait_ge(consts_in, 32)

        @block.sync
        def _(sp):
            sp.dma_start(ident[:, :], ident_in).then_inc(consts_in, 16)
            sp.dma_start(over[:, :], over_in).then_inc(consts_in, 16)

            def load(j):
                e = sp.value_load(over[0:1, bass.ds(j + 1, 1)], min_val=0, max_val=NE - 1)
                wait_apart(sp, fresh, j + 1, (consts_in, 32))
                for dst, w in ((wg, w_gate), (wu, w_up), (wd, w_down)):
                    sp.dma_start(dst[:, :, :], w[bass.ds(e, 1)].rearrange("o (c p) n -> p (o c) n", p=P)).then_inc(w_in_sem, 16)
            each(sp, load)

        @block.gpsimd
        def _(pool):
            first = NE * 2 * P
            pool.dma_start(idx[:, 0, :], slots[first:first + P, :]).then_inc(idx_in[0], 16)
            pool.wait_ge(consts_in, 32)
            n = pool.value_load(over[0:1, 0:1], min_val=0, max_val=OVER)
            with pool.If(n > 0):
                with pool.Fori(0, OVER // 2) as k:
                    for half in range(2):
                        j = k * 2 + half
                        wait_apart(pool, idx_in[half], 16 * k + 16, (consts_in, 32))
                        pool.dma_start(idx[:, 1 - half, :], slots[bass.ds(j * P + (first + P), P), :]).then_inc(idx_in[1 - half], 16)
                        pool.indirect_dma_start(out=xg[:, :], out_offset=None, in_=xn,
                                                in_offset=bass.IndirectOffsetOnAxis(ap=idx[:, half, 0:1], axis=0)).then_inc(x_in, 16)
                        pool.wait_ge(y_copied, j + 1)
                        pool.sem_inc(passed, 1)
                        pool.indirect_dma_start(out=y_tok, out_offset=bass.IndirectOffsetOnAxis(ap=idx[:, half, 1:2], axis=0),
                                                in_=y[:, :], in_offset=None).then_inc(stored, 16)
                        pool.wait_ge(stored, 16 * j + 16)
                pool.wait_ge(idx_in[0], 16 * (OVER // 2) + 16)
            with pool.Else():
                pool.wait_ge(idx_in[0], 16)

        @block.tensor
        def _(pe):
            def step(j):
                pe.wait_ge(x_in, 16 * j + 16)
                for c in range(KC):
                    last = pe.transpose(ps_turn[:, c // 4, (c % 4) * P:(c % 4 + 1) * P], xg[:, c * P:(c + 1) * P], ident[:, :])
                last.then_inc(x_turned, 1)
                pe.wait_ge(x_copied, j + 1)
                pe.wait_ge(w_in_sem, 48 * j + 48)
                for c in range(KC):
                    for b, w in enumerate((wg, wu)):
                        last = pe.matmul(ps_gu[:, b, :], xgT[:, c, :], w[:, c, :], start=(c == 0), stop=(c == KC - 1))
                last.then_inc(gu_done, 1)
                pe.wait_ge(hidden, j + 1)
                for c in range(FC):
                    last = pe.transpose(ps_turn[:, 0, c * P:(c + 1) * P], hid[:, 1, c * P:(c + 1) * P], ident[:, :])
                last.then_inc(h_turned, 1)
                pe.wait_ge(h_copied, j + 1)
                for c in range(FC):
                    for b in range(2):
                        last = pe.matmul(ps_y[:, b, :], hidT[:, c, :], wd[:, c, b * 512:(b + 1) * 512], start=(c == 0), stop=(c == FC - 1))
                last.then_inc(y_done, 1)
            each(pe, step)

        @block.scalar
        def _(act):
            act.sem_inc(fresh, 1)

            def step(j):
                act.wait_ge(x_turned, j + 1)
                act.activation(xgT[:, :, :].rearrange("p (b c) n -> p b (c n)", b=2), ps_turn[:, :, :], ACT.Copy).then_inc(x_copied, 1)
                act.wait_ge(gu_done, j + 1)
                act.activation(hid[:, 0, :], ps_gu[:, 0, :], ACT.Sigmoid).then_inc(sigged, 1)
                act.wait_ge(h_turned, j + 1)
                act.activation(hidT[:, :, :].rearrange("p c n -> p (c n)"), ps_turn[:, 0, :], ACT.Copy).then_inc(h_copied, 1)
                act.wait_ge(y_done, j + 1)
                act.activation(y[:, :].rearrange("p (b n) -> p b n", b=2), ps_y[:, :, :], ACT.Copy).then_inc(y_copied, 1)
                act.wait_ge(stored, 16 * j + 16)
                act.sem_inc(fresh, 1)
            each(act, step)

        @block.vector
        def _(dve):
            def step(j):
                dve.wait_ge(sigged, j + 1)
                dve.tensor_tensor(hid[:, 1, :], hid[:, 0, :], ps_gu[:, 0, :], ALU.mult).then_inc(gated, 1)
                dve.wait_ge(gated, j + 1)
                dve.tensor_tensor(hid[:, 1, :], hid[:, 1, :], ps_gu[:, 1, :], ALU.mult).then_inc(hidden, 1)
            each(dve, step)


def add_results(nc, h, y_tok, weight_in, y_prompt, y_sample):
    with ExitStack() as ctx:
        m = Memory(nc, ctx, "final")
        SLOTS = 3
        weight = m.sb("weight", [P, TILES, 2])
        ht = m.sb("ht", [P, SLOTS, D])
        ys = m.sb("ys", [P, SLOTS, 2, D])
        out = m.sb("out", [P, SLOTS, D])
        loaded = m.sem("loaded")
        tile_in = [m.sem(f"tile_in{s}") for s in range(SLOTS)]
        one = m.sem("one")
        two = m.sem("two")
        stored = [m.sem(f"stored{s}") for s in range(SLOTS)]
        block = m.block()

        def n_rows(t):
            return NS if t == TILES - 1 else P

        @block.sync
        def _(sp):
            sp.dma_start(weight[:, :, :], weight_in.rearrange("(t p) k -> p t k", p=P), allow_slow_non_contiguous=True).then_inc(loaded, 16)
            for t in range(TILES):
                s, n = t % SLOTS, n_rows(t)
                wait(sp, two, t + 1 - SLOTS)
                sp.dma_start(ht[0:n, s, :], h[t * P:t * P + n, :]).then_inc(tile_in[s], 16)
                for k in range(2):
                    first = 1 + k * ROWS + t * P
                    sp.dma_start(ys[0:n, s, k, :], y_tok[first:first + n, :]).then_inc(tile_in[s], 16)

        @block.vector
        def _(dve):
            dve.wait_ge(loaded, 16)
            for t in range(TILES):
                s, n = t % SLOTS, n_rows(t)
                dve.wait_ge(tile_in[s], 48 * (t // SLOTS + 1))
                wait(dve, stored[s], 16 * (t // SLOTS))
                dve.scalar_tensor_tensor(out[0:n, s, :], ys[0:n, s, 0, :], weight[0:n, t, 0:1], ht[0:n, s, :], ALU.mult, ALU.add).then_inc(one, 1)
                dve.wait_ge(one, t + 1)
                dve.scalar_tensor_tensor(out[0:n, s, :], ys[0:n, s, 1, :], weight[0:n, t, 1:2], out[0:n, s, :], ALU.mult, ALU.add).then_inc(two, 1)

        @block.scalar
        def _(act):
            for t in range(TILES):
                s = t % SLOTS
                act.wait_ge(two, t + 1)
                if t < TILES - 1:
                    act.dma_start(y_prompt[t * P:(t + 1) * P, :], out[:, s, :]).then_inc(stored[s], 16)
                else:
                    act.dma_start(y_sample, out[0:NS, s, :]).then_inc(stored[s], 16)
            for s in range(SLOTS):
                act.wait_ge(stored[s], 16 * ((TILES + SLOTS - 1 - s) // SLOTS))


def kept_rows(a, outs):
    out = []
    for g, w in enumerate(WIN):
        for i, n in enumerate("kv"):
            keep = min(w, PAST + DEC_S)
            dst = outs[9 + 2 * g + i].rearrange("b t h d -> b t (h d)")[:, 0:keep - DEC_S, :]
            src = a[f"cache_{n}_w{w}"].rearrange("b t h d -> b t (h d)")[:, LB[g] + DEC_S - keep:LB[g], :]
            out.append(tuple(x.rearrange("b (o t) c -> b o t c", o=2) for x in (dst, src)))
    return out


def new_rows(a, z, outs):
    pairs = []
    for g, w in enumerate(WIN):
        for i, n in enumerate("kv"):
            new = z[n][:, g * GW:(g + 1) * GW]
            pairs.append((outs[2 + 2 * g + i][0].rearrange("t h d -> t (h d)"), new[SEQ - w:SEQ, :]))
            keep = min(w, PAST + DEC_S)
            out = outs[9 + 2 * g + i].rearrange("b t h d -> b t (h d)")
            pairs.append((out[:, keep - DEC_S:keep, :], new[SEQ:SEQ + NS, :].rearrange("(b s) c -> b s c", b=DEC_B)))
    pairs.append((outs[8][0], z["u"][SEQ - PSTATE:SEQ, :]))
    pairs.append((outs[15][:, 0:PSTATE - DEC_S, :], a["state_pool"][:, DEC_S:PSTATE, :]))
    pairs.append((outs[15][:, PSTATE - DEC_S:PSTATE, :], z["u"][SEQ:SEQ + NS, :].rearrange("(b s) c -> b s c", b=DEC_B)))
    return pairs


def build(nc, a, outs):
    def dram(name, shape, dt=F32):
        return nc.dram_tensor(name, shape, dt).ap()

    xT = dram("xT", [TILES, P, 2, KC, P])
    z = {n: dram("z_" + n, [ROWS, w]) for n, w in (("q", AW), ("k", AW), ("v", AW), ("u", PW), ("ga", D), ("gb", D))}
    att = dram("att", [NG, ROWS, ATTW])
    joined = [dram(f"joined_{n}", [DEC_B, P + DEC_S, GW]) for n in "kv"]
    poolT = dram("poolT", [TILES, P, 2, PG, P])
    h = dram("h", [ROWS, D])
    xn = dram("xn", [ROWS, D])
    logits = dram("logits", [ROWS, EG + NE])
    slots = dram("slots", [BLOCKS * P, SLOT], I32)
    weight = dram("weight", [ROWS, 2])
    counts = dram("counts", [1, 2 * NE], I32)
    over = dram("over", [1, OVER + 1], I32)
    y_tok = dram("y_tok", [1 + 2 * ROWS, D])
    caches_kv = [[a[f"cache_{n}_w{w}"].rearrange("b t h d -> b t (h d)") for n in "kv"] for w in WIN]

    norm_and_turn(nc, a["x"], a["ln1"], a["ident"], xT)
    project(nc, xT, a["w_in"], a["q_gain"], a["k_gain"], z, kept_rows(a, outs))
    prompt_attention(nc, z, att, a["ident"], a["bias"])
    sample_and_pooling(nc, z, att, caches_kv, joined, a["sbias"], a["state_pool"], a["pool_lin"], a["pool_scale"], a["ident"],
                       a["inv_count"], poolT)
    merge_and_route(nc, a["x"], z, att, poolT, a["w_pa"], a["w_pb"], a["w_o"], a["ln2"], a["w_rg"], a["b_rg"],
                    a["w_re"], a["b_re"], a["ident"], h, xn, logits)
    with ExitStack() as ctx:
        raw = RawWeights(nc, ctx, a["w_gate"], a["w_up"], a["w_down"])
        routing(nc, logits, a, slots, weight, counts, over, new_rows(a, z, outs), raw)
        experts(nc, xn, slots, counts, raw, a["ident"], y_tok)
    expert_overflow(nc, xn, slots, over, a["w_gate"], a["w_up"], a["w_down"], a["ident"], y_tok)
    add_results(nc, h, y_tok, weight, outs[0][0], outs[1].rearrange("b t d -> (b t) d"))


def constants(np):
    slope = np.exp2(-8.0 * np.arange(1, NG * HG + 1, dtype=np.float32) / (NG * HG)).astype(np.float32)
    qi, kb = np.arange(P)[:, None], np.arange(2 * P)[None, :]
    rel = qi + P - kb
    valid = (rel >= 0) & (rel <= P)
    bias = np.full((NG + 2, P, HG, 2 * P), -1e30, np.float32)
    for g in range(NG):
        for h in range(HG):
            b = -slope[g * HG + h] * (DIL[g] * rel).astype(np.float32)
            bias[g, :, SEAT[h]] = np.where(valid, b, np.float32(-1e30))
            if g < 2:
                bias[NG + g, :, SEAT[h]] = np.where(valid & (kb >= P), b, np.float32(-1e30))
    sbias = np.zeros((P, NG, P + 1), np.float32)
    for g in range(NG):
        n = LB[g] // DIL[g]
        dist = (DIL[g] * (n - np.arange(n + 1))).astype(np.float32)
        sbias[:, g, :n + 1] = -slope[g * HG + np.arange(P) % HG][:, None] * dist[None, :]
    pos = np.arange(16)
    inv_count = np.stack([1.0 / np.minimum(pos + 1, 2 << g) for g in range(PG)]).astype(np.float32)
    e = np.arange(NE)
    tile_rows = np.arange(TILES)[None, :] * P + np.arange(P)[:, None]
    entry = np.zeros((P, 2, TILES, SLOT), np.int32)
    entry[:, :, :, 0] = tile_rows[:, None, :]
    entry[:, :, :, 1] = 1 + ROWS * np.arange(2)[None, :, None] + tile_rows[:, None, :]
    return {
        "ident": np.eye(P, dtype=np.float32),
        "ones": np.ones((P, P), np.float32),
        "before": (np.arange(P)[:, None] < np.arange(P)[None, :]).astype(np.float32),
        "bias": bias,
        "sbias": sbias,
        "inv_count": np.broadcast_to(inv_count, (P, PG, 16)).copy(),
        "first_group": np.broadcast_to((EG - np.arange(EG)).astype(np.float32), (P, EG)).copy(),
        "first_expert": np.broadcast_to((NE - e).astype(np.float32), (P, NE)).copy(),
        "block_no": np.broadcast_to(np.arange(OVER, dtype=np.float32)[None, :, None], (P, OVER, NE)).copy(),
        "base": np.broadcast_to((2 * P * e).astype(np.float32), (P, NE)).copy(),
        "real": (tile_rows < SEQ + NS).astype(np.float32),
        "entry": entry,
    }
def kernel(**inputs):
    import numpy as np
    import concourse.bacc as bacc
    from concourse.bass_utils import run_bass_kernel_spmd

    nc = bacc.Bacc("TRN2", target_bir_lowering=False, num_devices=1)
    arrays = {}
    ins = {}

    def give(name, a):
        a = np.ascontiguousarray(a)
        arrays[name] = a
        ins[name] = nc.dram_tensor(name, a.shape, mybir.dt.from_np(a.dtype), kind="ExternalInput").ap()

    x = np.zeros((ROWS, D), np.float32)
    x[:SEQ] = np.asarray(inputs["x_prompt"]).reshape(SEQ, D)
    x[SEQ:SEQ + NS] = np.asarray(inputs["x_sample"]).reshape(NS, D)
    give("x", x)
    for name, a in inputs.items():
        if not name.startswith("x_"):
            give(name, np.asarray(a))
    for name, a in constants(np).items():
        give(name, a)
    shapes = ([(1, SEQ, D), (DEC_B, DEC_S, D)]
              + [(1, w, HG, HD) for w in WIN for _ in range(2)] + [(1, PSTATE, PW)]
              + [(DEC_B, min(w, PAST + DEC_S), HG, HD) for w in WIN for _ in range(2)] + [(DEC_B, PSTATE, PW)])
    outs = [nc.dram_tensor(f"out_{i}", s, F32, kind="ExternalOutput").ap() for i, s in enumerate(shapes)]
    build(nc, ins, outs)
    r = run_bass_kernel_spmd(nc, [arrays], core_ids=[0])
    return tuple(r.results[0][f"out_{i}"] for i in range(len(shapes)))
```
